# Optimizing a Trainium2 kernel written in Bass

```python
import math
import jax, jax.numpy as jnp
from jax import lax
import numpy as np

D_MODEL = 1024
BATCH = 1
SEQ = 256
DEPTH = 2

EPS = 1e-6
Q_BLOCK = 128
RET_HEADS = 4
RET_DK = 128
RET_DV = 256
RET_CHUNK = 128
DIFF_HEADS = 8
DIFF_DH = 64
MLA_HEADS = 16
MLA_Q_LORA = 256
MLA_KV_LORA = 128
MLA_NOPE = 64
MLA_ROPE = 32
MLA_V = 64
ROPE_THETA = 10000.0
REL_BUCKETS = 32
REL_MAX_DIST = 128
D_FF = 4 * D_MODEL
N_BRANCH = 3

RET_QK_W = RET_HEADS * RET_DK
RET_V_W = RET_HEADS * RET_DV
DIFF_QK_W = 2 * DIFF_HEADS * DIFF_DH
DIFF_V_W = DIFF_HEADS * 2 * DIFF_DH
MLA_QH = MLA_NOPE + MLA_ROPE
MLA_KVH = MLA_NOPE + MLA_V
MLA_V_W = MLA_HEADS * MLA_V
IN_SPLITS = (RET_QK_W, RET_QK_W, RET_V_W, RET_V_W,
             DIFF_QK_W, DIFF_QK_W, DIFF_V_W,
             MLA_Q_LORA, MLA_KV_LORA, MLA_ROPE,
             N_BRANCH * D_MODEL)
D_IN = sum(IN_SPLITS)

kernel_name = 'hybrid_gated_retention_diffattn_mla_block'

def rms_norm(x, g=None):
    xf = x.astype(jnp.float32)
    y = xf * lax.rsqrt(jnp.mean(xf * xf, axis=-1, keepdims=True) + EPS)
    if g is not None:
        y = y * g.astype(jnp.float32)
    return y.astype(x.dtype)

def rope_tables(inv_freq):
    pos = jnp.arange(SEQ, dtype=jnp.float32)
    ang = pos[:, None] * inv_freq[None, :]
    return jnp.cos(ang), jnp.sin(ang)

def apply_rope(x, cos, sin):
    d2 = x.shape[-1] // 2
    x1, x2 = x[..., :d2], x[..., d2:]
    c = cos[:, None, :].astype(x.dtype)
    s = sin[:, None, :].astype(x.dtype)
    return jnp.concatenate([x1 * c - x2 * s, x2 * c + x1 * s], axis=-1)

def t5_bucket(n):
    max_exact = REL_BUCKETS // 2
    nf = jnp.maximum(n, 1).astype(jnp.float32)
    large = max_exact + (jnp.log(nf / max_exact) / math.log(REL_MAX_DIST / max_exact)
                         * (REL_BUCKETS - max_exact)).astype(jnp.int32)
    large = jnp.minimum(large, REL_BUCKETS - 1)
    return jnp.where(n < max_exact, n, large)

def retention(q, k, v):
    b = q.shape[0]
    n_chunks = SEQ // RET_CHUNK

    def chunks(t):
        return t.reshape(b, n_chunks, RET_CHUNK, RET_HEADS, t.shape[-1]).transpose(1, 0, 3, 2, 4)

    log_g = jnp.log1p(-jnp.exp2(-5.0 - jnp.arange(RET_HEADS, dtype=jnp.float32)))
    idx = jnp.arange(RET_CHUNK, dtype=jnp.float32)
    rel = idx[:, None] - idx[None, :]
    dmask = jnp.where(rel >= 0, jnp.exp(jnp.maximum(rel, 0.0)[None] * log_g[:, None, None]), 0.0)
    xi = jnp.exp((idx + 1.0)[None, :] * log_g[:, None])[:, :, None]
    zeta = jnp.exp((RET_CHUNK - 1.0 - idx)[None, :] * log_g[:, None])[:, :, None]
    g_chunk = jnp.exp(RET_CHUNK * log_g)[:, None, None]

    def step(state, qkv):
        qc, kc, vc = qkv
        inner = jnp.einsum('bhid,bhjd->bhij', qc, kc) * dmask
        out = (jnp.einsum('bhij,bhje->bhie', inner, vc)
               + jnp.einsum('bhid,bhde->bhie', qc * xi, state))
        state = g_chunk * state + jnp.einsum('bhjd,bhje->bhde', kc * zeta, vc)
        return state, out

    state0 = jnp.zeros((b, RET_HEADS, RET_DK, RET_DV), jnp.float32)
    _, o = lax.scan(step, state0, (chunks(q), chunks(k), chunks(v)))
    return o.transpose(1, 0, 3, 2, 4).reshape(b, SEQ, RET_HEADS, RET_DV)

def diff_attention(q, k, v, lam, rel_bias):
    scale = DIFF_DH ** -0.5
    kpos = jnp.arange(SEQ)

    def block(i):
        q0 = i * Q_BLOCK
        qb = lax.dynamic_slice_in_dim(q, q0, Q_BLOCK, axis=1)
        dist = (q0 + jnp.arange(Q_BLOCK))[:, None] - kpos[None, :]
        bias = rel_bias[t5_bucket(jnp.maximum(dist, 0))].astype(jnp.float32)
        logits = (jnp.einsum('bqhcd,bkhcd->bhcqk', qb, k).astype(jnp.float32) * scale
                  + jnp.transpose(bias, (2, 0, 1))[None, :, None])
        logits = jnp.where(dist >= 0, logits, -jnp.inf)
        p = jax.nn.softmax(logits, axis=-1)
        a = p[:, :, 0] - lam * p[:, :, 1]
        return jnp.einsum('bhqk,bkhe->bqhe', a.astype(v.dtype), v)

    out = lax.map(block, jnp.arange(SEQ // Q_BLOCK))
    return jnp.swapaxes(out, 0, 1).reshape(v.shape)

def mla_attention(q_nope, q_pe, k_nope, k_pe, v):
    scale = MLA_QH ** -0.5
    kpos = jnp.arange(SEQ)

    def block(i):
        q0 = i * Q_BLOCK
        qn = lax.dynamic_slice_in_dim(q_nope, q0, Q_BLOCK, axis=1)
        qp = lax.dynamic_slice_in_dim(q_pe, q0, Q_BLOCK, axis=1)
        dist = (q0 + jnp.arange(Q_BLOCK))[:, None] - kpos[None, :]
        logits = (jnp.einsum('bqhd,bkhd->bhqk', qn, k_nope)
                  + jnp.einsum('bqhd,bkd->bhqk', qp, k_pe)).astype(jnp.float32) * scale
        logits = jnp.where(dist >= 0, logits, -jnp.inf)
        p = jax.nn.softmax(logits, axis=-1)
        return jnp.einsum('bhqk,bkhe->bqhe', p.astype(v.dtype), v)

    out = lax.map(block, jnp.arange(SEQ // Q_BLOCK))
    return jnp.swapaxes(out, 0, 1).reshape(v.shape)

def setup_inputs(seed: int = 0) -> dict:
    key = jax.random.key(seed)
    ks = jax.random.split(key, 32)
    f32 = jnp.float32

    def w(k, shape, fan_in):
        return jax.random.normal(k, shape, f32) * fan_in ** -0.5

    def gain(k, shape):
        return 1.0 + 0.05 * jax.random.normal(k, shape, f32)

    L = DEPTH
    return {
        'x': jax.random.normal(ks[0], (BATCH, SEQ, D_MODEL), f32),
        'rel_bias': 0.5 * jax.random.normal(ks[1], (REL_BUCKETS, DIFF_HEADS), f32),
        'pre_mix_g': gain(ks[2], (L, D_MODEL)),
        'w_in': w(ks[3], (L, D_MODEL, D_IN), D_MODEL),
        'w_ret_o': w(ks[4], (L, RET_V_W, D_MODEL), RET_V_W),
        'lambda_q1': 0.1 * jax.random.normal(ks[5], (L, DIFF_DH), f32),
        'lambda_k1': 0.1 * jax.random.normal(ks[6], (L, DIFF_DH), f32),
        'lambda_q2': 0.1 * jax.random.normal(ks[7], (L, DIFF_DH), f32),
        'lambda_k2': 0.1 * jax.random.normal(ks[8], (L, DIFF_DH), f32),
        'diff_subln_g': gain(ks[9], (L, 2 * DIFF_DH)),
        'w_diff_o': w(ks[10], (L, DIFF_V_W, D_MODEL), DIFF_V_W),
        'mla_q_norm_g': gain(ks[11], (L, MLA_Q_LORA)),
        'w_mla_uq': w(ks[12], (L, MLA_Q_LORA, MLA_HEADS * MLA_QH), MLA_Q_LORA),
        'mla_kv_norm_g': gain(ks[13], (L, MLA_KV_LORA)),
        'w_mla_ukv': w(ks[14], (L, MLA_KV_LORA, MLA_HEADS * MLA_KVH), MLA_KV_LORA),
        'w_mla_o': w(ks[15], (L, MLA_V_W, D_MODEL), MLA_V_W),
        'w_out': w(ks[16], (L, D_MODEL, D_MODEL), D_MODEL),
        'post_mix_g': gain(ks[17], (L, D_MODEL)),
        'pre_mlp_g': gain(ks[18], (L, D_MODEL)),
        'w_up': w(ks[19], (L, D_MODEL, D_FF), D_MODEL),
        'w_down': w(ks[20], (L, D_FF, D_MODEL), D_FF),
        'post_mlp_g': gain(ks[21], (L, D_MODEL)),
    }

def reference(x, rel_bias, pre_mix_g, w_in, w_ret_o, lambda_q1, lambda_k1, lambda_q2, lambda_k2,
              diff_subln_g, w_diff_o, mla_q_norm_g, w_mla_uq, mla_kv_norm_g, w_mla_ukv, w_mla_o,
              w_out, post_mix_g, pre_mlp_g, w_up, w_down, post_mlp_g):
    b = x.shape[0]
    offs = np.cumsum(np.array(IN_SPLITS))[:-1].tolist()
    ret_cos, ret_sin = rope_tables(1.0 / (10000.0 ** jnp.linspace(0.0, 1.0, RET_DK // 2)))
    mla_cos, mla_sin = rope_tables(1.0 / (ROPE_THETA ** (jnp.arange(0, MLA_ROPE, 2, dtype=jnp.float32) / MLA_ROPE)))

    for l in range(DEPTH):
        h = rms_norm(x, pre_mix_g[l])
        (rq, rk, rv, rg, dq, dk, dv, cq, ckv, kpe, gates) = jnp.split(h @ w_in[l], offs, axis=-1)

        rq = apply_rope(rq.reshape(b, SEQ, RET_HEADS, RET_DK), ret_cos, ret_sin)
        rk = apply_rope(rk.reshape(b, SEQ, RET_HEADS, RET_DK), ret_cos, ret_sin) * (RET_DK ** -0.5)
        ret = retention(rq, rk, rv.reshape(b, SEQ, RET_HEADS, RET_DV))
        ret = rms_norm(ret).reshape(b, SEQ, RET_V_W).astype(h.dtype)
        branch_a = (jax.nn.silu(rg) * ret) @ w_ret_o[l]

        lambda_init = 0.8 - 0.6 * math.exp(-0.3 * l)
        lam = (jnp.exp(jnp.sum(lambda_q1[l] * lambda_k1[l]).astype(jnp.float32))
               - jnp.exp(jnp.sum(lambda_q2[l] * lambda_k2[l]).astype(jnp.float32)) + lambda_init)
        da = diff_attention(dq.reshape(b, SEQ, DIFF_HEADS, 2, DIFF_DH),
                            dk.reshape(b, SEQ, DIFF_HEADS, 2, DIFF_DH),
                            dv.reshape(b, SEQ, DIFF_HEADS, 2 * DIFF_DH), lam, rel_bias)
        da = rms_norm(da, diff_subln_g[l]) * (1.0 - lambda_init)
        branch_b = da.reshape(b, SEQ, DIFF_V_W).astype(h.dtype) @ w_diff_o[l]

        qh = (rms_norm(cq, mla_q_norm_g[l]) @ w_mla_uq[l]).reshape(b, SEQ, MLA_HEADS, MLA_QH)
        q_nope, q_pe = qh[..., :MLA_NOPE], apply_rope(qh[..., MLA_NOPE:], mla_cos, mla_sin)
        kvh = (rms_norm(ckv, mla_kv_norm_g[l]) @ w_mla_ukv[l]).reshape(b, SEQ, MLA_HEADS, MLA_KVH)
        k_nope, v_mla = kvh[..., :MLA_NOPE], kvh[..., MLA_NOPE:]
        k_pe = apply_rope(kpe[:, :, None, :], mla_cos, mla_sin)[:, :, 0, :]
        mo = mla_attention(q_nope, q_pe, k_nope, k_pe, v_mla)
        branch_c = mo.reshape(b, SEQ, MLA_V_W) @ w_mla_o[l]

        g = jax.nn.sigmoid(gates).reshape(b, SEQ, N_BRANCH, D_MODEL)
        merged = g[:, :, 0] * branch_a + g[:, :, 1] * branch_b + g[:, :, 2] * branch_c
        x = x + rms_norm(merged @ w_out[l], post_mix_g[l])

        h = rms_norm(x, pre_mlp_g[l])
        m = jnp.square(jax.nn.relu(h @ w_up[l])) @ w_down[l]
        x = x + rms_norm(m, post_mlp_g[l])
    return x


_drawn_inputs = setup_inputs


def setup_inputs(seed=0):
    import zlib

    import numpy as np

    out = dict(_drawn_inputs(seed))
    spreads = {}
    factors = {'mla_q_norm_g': 5.84, 'mla_kv_norm_g': 3.135}
    for name, (base, spread) in spreads.items():
        noise = np.random.default_rng([zlib.crc32(name.encode()), seed]).standard_normal(out[name].shape)
        drawn = base * np.exp(spread * noise) if base else spread * noise
        out[name] = __import__('jax').numpy.asarray(drawn.astype(out[name].dtype))
    for name, factor in factors.items():
        out[name] = (out[name] * factor).astype(out[name].dtype)
    return out
```

```python
from contextlib import ExitStack

import numpy as np

import concourse.bass as bass
from concourse import mybir

F32 = mybir.dt.float32
F32R = mybir.dt.float32r
ALU = mybir.AluOpType
ACT = mybir.ActivationFunctionType
ENG = mybir.EngineType

P = 128
L, S, DM, FF = 2, 256, 1024, 4096
TT = S // P
KD = DM // P
EPS = 1e-6
RH, RDK, RDV = 4, 128, 256
DH, DD = 8, 64
MH, MN, MR, MV = 16, 64, 32, 64
MQ = MN + MR
QL, KVL = 256, 128
LAT = QL + KVL + MR
NEG = -1e30
BIG = 3e38
BUCKETS, MAX_DIST = 32, 128
LINE = 384

C_RQ, C_RK, C_RV, C_RG = 0, 512, 1024, 2048
C_DQ, C_DK, C_DV, C_LAT = 3072, 4096, 5120, 6144
C_G0, C_G1, C_G2 = 6560, 7584, 8608

K_ID = 0
K_MASK = K_ID + P
K_DEC = K_MASK + S
K_RC = K_DEC + RH * 384
K_RS = K_RC + TT * RDK
K_MC = K_RS + TT * RDK
K_MS = K_MC + TT * MR
K_LI = K_MS + TT * MR
K_END = K_LI + 2 * L

G_MIX, G_MLP, G_Q, G_KV, G_SUB, G_LAM, G_N = 0, 8, 16, 18, 19, 20, 21


def weight_units():
    units = []

    def rows(name, col, n):
        units.extend((name, 2 * P * i, col, 2, n) for i in range(4))

    rows("w_in", C_LAT, LAT)
    rows("w_in", C_RQ, 512)
    rows("w_in", C_RK, 512)
    units.extend(("w_mla_ukv", 0, 512 * m, 1, 512) for m in range(4))
    units.extend(("w_mla_uq", 0, 4 * MQ * m, 2, 4 * MQ) for m in range(4))
    for name, col in (("w_in", C_DQ), ("w_in", C_DK), ("w_in", C_DV), ("w_in", C_G2), ("w_in", C_RV),
                      ("w_mla_o", 0), ("w_in", C_RG), ("w_in", C_G1), ("w_in", C_G0), ("w_diff_o", 0),
                      ("w_ret_o", 0), ("w_out", 0)):
        rows(name, col, 512)
        rows(name, col + 512, 512)

    def up(j):
        rows("w_up", 512 * j, 512)

    def down(j):
        units.extend(("w_down", 512 * j + 2 * P * (i % 2), 512 * (i // 2), 2, 512) for i in range(4))

    up(0)
    for j in range(1, 8):
        up(j)
        down(j - 1)
    down(7)
    return units


UNITS = weight_units()
NU = len(UNITS)
SLOTS = 4
U_LAT, U_RQ, U_RK, U_UKV, U_UQ = 0, 4, 8, 12, 16
U_DQ, U_DK, U_DV, U_G2, U_RV, U_MLAO, U_RG, U_G1, U_G0, U_DIFFO, U_RETO, U_WOUT = range(20, 116, 8)
U_UP = [116] + [120 + 8 * (j - 1) for j in range(1, 8)]
U_DN = [124 + 8 * j for j in range(7)] + [176]
assert NU == 180

GROUPS = {}


def _groups():
    n = 0
    for first, units in [(U_LAT, 4), (U_RQ, 4), (U_RK, 4)] + [(u, 1) for u in range(U_UKV, U_DQ)] + \
            [(u, 4) for u in range(U_DQ, U_UP[0], 4)] + [(u, 4) for u in U_UP]:
        GROUPS[first] = (units, n)
        n += 1
    return n


N_GROUPS = _groups()


def group(first):
    return GROUPS[first][1]


J_PRE = (0, 17)
J_LAT = 2
J_HEAD = 3
J_POST = (15, 19)
N_JOBS = 21

N_HEADS = MH + 2 * DH + RH


def mix_index(H):
    if H < 0 or H >= N_HEADS:
        return None
    if H < MH:
        return H
    if H < MH + 2 * DH:
        return MH + (H - MH) // 2 if H % 2 else None
    return MH + DH + H - MH - 2 * DH


def head_index(H):
    j = mix_index(H)
    return None if j is None or j < MH else j - MH


def build(nc, io):
    with ExitStack() as ctx:
        def sb(name, shape, dt=F32):
            return ctx.enter_context(nc.sbuf_tensor(name, shape, dt))

        def sem(name):
            return ctx.enter_context(nc.semaphore(name))

        raw = sb("raw", [P, SLOTS, 1024])
        w_hi = sb("w_hi", [P, SLOTS, 1024], F32R)
        w_lo = sb("w_lo", [P, SLOTS, 1024], F32R)
        x = sb("x", [P, TT, DM])
        const = sb("const", [P, K_END])
        bias = sb("bias", [P, DH, S])
        hT_hi = sb("hT_hi", [P, KD, S], F32R)
        hT_lo = sb("hT_lo", [P, KD, S], F32R)
        bT_hi = sb("bT_hi", [P, KD, S], F32R)
        bT_lo = sb("bT_lo", [P, KD, S], F32R)
        dT_hi = sb("dT_hi", [P, KD, S], F32R)
        dT_lo = sb("dT_lo", [P, KD, S], F32R)
        area_d = sb("area_d", [P, 8192])
        area_e = sb("area_e", [P, 6144])
        area_g = sb("area_g", [P, 2048])
        area_r = sb("area_r", [P, 2, 1024])
        qkT = sb("qkT", [MQ, 2 * S])
        logits = sb("logits", [P, 2, 384])
        probs = sb("probs", [P, 2, 384])
        probsT = sb("probsT", [P, 384])
        orow = sb("orow", [P, 512])
        junk = sb("junk", [P, 512], mybir.dt.bfloat16)
        gains = sb("gains", [P, L, G_N])
        gl = sb("gl", [P, G_N])
        negmax = sb("negmax", [P, 2, 2])
        rowsum = sb("rowsum", [P, 2, 2])
        rrow_sum = sb("rrow_sum", [P, 2, 2, 2])
        negr = sb("negr", [P, 2])
        ss = sb("ss", [P, N_JOBS, 4])
        rstd = sb("rstd", [P, N_JOBS, 4])
        neghalf = sb("neghalf", [P, 4])
        lam = sb("lam", [P, 8])

        def view(area, first, shape):
            n = int(np.prod(shape))
            flat = area[:, first:first + n]
            names = "abcd"[:len(shape)]
            return flat.rearrange(f"p ({' '.join(names)}) -> p {' '.join(names)}", **dict(zip(names, shape)))

        q_rows = view(area_d, 0, (TT, MH, MQ))
        k_rows = view(area_d, 3072, (TT, MH, MQ))
        v_rows = view(area_d, 6144, (TT, MH, MV))
        rv_rows = view(area_d, 0, (TT, DM))
        rg_rows = view(area_d, 2048, (TT, DM))
        merged = view(area_d, 4096, (TT, DM))
        tanh_g1 = view(area_d, 6144, (TT, DM))
        dqT = view(area_e, 0, (DH, S))
        dkT = view(area_e, 2048, (DH, S))
        dv_rows = view(area_e, 4096, (TT, DM))
        lat = view(area_e, 0, (TT, LAT))
        r_rows = view(area_e, 1024, (TT, RH, RDK))
        r_tmp = view(area_e, 2048, (TT, RH, RDK))
        kpe_tmp = view(area_e, 3072, (TT, 2 * MR))
        gain_rows = view(area_e, 2048, (2, DM))
        tanh_g = view(area_g, 0, (TT, DM))
        xn = view(area_g, 0, (TT, DM))
        rqT = area_r[:, 0, :].rearrange("p (h s) -> p h s", h=RH)
        rkT = area_r[:, 1, :].rearrange("p (h s) -> p h s", h=RH)
        relu_h = area_r[:, 0, :]
        square_h = area_r[:, 1, :]
        norm_junk = area_r[:, :, :]
        lat_junk = view(area_g, 0, (TT, QL + KVL))
        hid_hi = dT_hi[:, :, :].rearrange("p (b k) s -> p b k s", b=2)
        hid_lo = dT_lo[:, :, :].rearrange("p (b k) s -> p b k s", b=2)

        ident = const[:, K_ID:K_ID + P]
        mask = const[:, K_MASK:K_MASK + S]
        decay = const[:, K_DEC:K_DEC + RH * 384].rearrange("p (h n) -> p h n", h=RH)
        r_cos = const[:, K_RC:K_RC + TT * RDK].rearrange("p (t n) -> p t n", t=TT)
        r_sin = const[:, K_RS:K_RS + TT * RDK].rearrange("p (t n) -> p t n", t=TT)
        m_cos = const[:, K_MC:K_MC + TT * MR].rearrange("p (t n) -> p t n", t=TT)
        m_sin = const[:, K_MS:K_MS + TT * MR].rearrange("p (t n) -> p t n", t=TT)
        lam_init = const[:, K_LI:K_LI + L]
        one_less = const[:, K_LI + L:K_LI + 2 * L]

        G = ctx.enter_context(nc.psum_tensor("G", [P, 2, TT, 512], F32))
        A = ctx.enter_context(nc.psum_tensor("A", [P, 4, 512], F32))

        def f32(ap):
            return ap.bitcast(F32)

        consts_in = sem("consts_in")
        small_in = sem("small_in")
        rows_in = sem("rows_in")
        x_in = sem("x_in")
        pool_set = sem("pool_set")
        lines_made = sem("lines_made")
        gains_turned = sem("gains_turned")
        line_ready = sem("line_ready")
        line_out = sem("line_out")
        bias_in = sem("bias_in")
        lam_step = sem("lam_step")
        bias_flipped = sem("bias_flipped")
        lam_dots = sem("lam_dots")
        lam_exp = sem("lam_exp")

        lam_vec = view(area_d, 0, (L, 4, DD))
        lam_prod = view(area_d, 2048, (L, 2, DD))
        gain_in = area_d[0:40, 4096:4096 + P]
        rel_in = area_d[0:BUCKETS + 1, 5000:5000 + DH]
        onehot = area_d[0:BUCKETS + 1, 5120:5120 + LINE]
        line_sb = area_d[0:DH, 6000:6000 + LINE]
        upside_down = view(area_e, 0, (DH, S))
        flip = area_e[:, 2048:2048 + P]

        with nc.Block() as block:
            @block.sync
            def _(sp):
                sp.dma_start(const[:, :], io["consts"]).then_inc(consts_in, 16)
                sp.dma_start(x[:, :, :], io["x"][0].rearrange("(t p) d -> p t d", p=P)).then_inc(x_in, 16)
                sp.dma_start(onehot, io["onehot"]).then_inc(rows_in, 16)
                sp.dma_start(flip, io["flip"]).then_inc(rows_in, 16)
                sp.wait_ge(line_ready, 1)
                sp.dma_start(io["line"], line_sb).then_inc(line_out, 16)
                sp.wait_ge(line_out, 16)
                shifted = bass.AP(io["line"].tensor, 0, [[1, P], [LINE, DH], [1, S]])
                sp.dma_start(upside_down, shifted).then_inc(bias_in, 16)
                sp.wait_ge(x_in, 16)

            @block.gpsimd
            def _(pool):
                nc.gpsimd.memset(neghalf[:, :], -0.5).then_inc(pool_set, 1)
                pool.wait_ge(pool_set, 1)
                nc.gpsimd.memset(area_d[BUCKETS:BUCKETS + 1, 5000:5000 + DH], NEG).then_inc(pool_set, 1)

            @block.scalar
            def _(act):
                act.dma_start(area_d[0:BUCKETS, 5000:5000 + DH], io["rel_bias"]).then_inc(rows_in, 16)
                for l in range(L):
                    for row, name, n in ((G_MIX, "pre_mix_g", KD), (G_MLP, "pre_mlp_g", KD), (G_Q, "mla_q_norm_g", 2),
                                         (G_KV, "mla_kv_norm_g", 1), (G_SUB, "diff_subln_g", 1)):
                        first = 20 * l + row
                        act.dma_start(gain_in[first:first + n, :],
                                      io[name][l].rearrange("(k p) -> k p", p=P)).then_inc(small_in, 16)
                    for i, name in enumerate(("lambda_q1", "lambda_k1", "lambda_q2", "lambda_k2")):
                        act.dma_start(lam_vec[:, l, i, :],
                                      io[name][l:l + 1, :].broadcast_to([P, DD])).then_inc(small_in, 16)
                act.wait_ge(lines_made, 1)
                nc.scalar.activation(line_sb, A[0:DH, 0, 0:LINE], ACT.Copy, scale=8.0).then_inc(line_ready, 1)
                act.wait_ge(lam_dots, 1)
                nc.scalar.activation(lam[:, 4:8], lam[:, 0:4], ACT.Exp).then_inc(lam_exp, 1)

            @block.tensor
            def _(pe):
                pe.wait_ge(rows_in, 48)
                pe.wait_ge(pool_set, 2)
                nc.tensor.matmul(A[0:DH, 0, 0:LINE], rel_in, onehot, start=True, stop=True).then_inc(lines_made, 1)
                pe.wait_ge(consts_in, 16)
                pe.wait_ge(small_in, 16 * 18)
                nc.tensor.transpose(A[:, 1, 0:40], gain_in, ident[0:40, 0:40]).then_inc(gains_turned, 1)
                pe.wait_ge(bias_in, 16)
                pe.wait_ge(line_ready, 1)
                pe.wait_ge(lam_step, L + 1)
                for i in range(4):
                    last = nc.tensor.matmul(A[:, i, :], flip, upside_down[:, 2 * i:2 * i + 2, :], start=True, stop=True)
                last.then_inc(bias_flipped, 1)

            @block.vector
            def _(dve):
                dve.wait_ge(small_in, 16 * 18)
                dve.wait_ge(consts_in, 16)
                for l in range(L):
                    nc.vector.tensor_tensor(lam_prod[:, l, :, :], lam_vec[:, l, 0:4:2, :], lam_vec[:, l, 1:4:2, :],
                                            ALU.mult).then_inc(lam_step, 1)
                dve.wait_ge(lam_step, L)
                nc.vector.tensor_reduce(lam[:, 0:4].rearrange("p (l i) -> p l i", l=L), lam_prod[:, :, :, :],
                                        mybir.AxisListType.X, ALU.add).then_inc(lam_dots, 1)
                dve.wait_ge(gains_turned, 1)
                nc.vector.tensor_copy(gains[:, :, 0:20],
                                      A[:, 1, 0:40].rearrange("p (l k) -> p l k", l=L)).then_inc(lam_step, 1)
                dve.wait_ge(lam_step, L + 1)
                dve.wait_ge(bias_flipped, 1)
                nc.vector.tensor_copy(bias[:, :, :].rearrange("p h s -> p (h s)"),
                                      A[:, :, :].rearrange("p a b -> p (a b)")).then_inc(lam_step, 1)
                dve.wait_ge(lam_exp, 1)
                for l in range(L):
                    nc.vector.scalar_tensor_tensor(gains[:, l, G_LAM:G_LAM + 1], lam[:, 5 + 2 * l:6 + 2 * l],
                                                   lam[:, 4 + 2 * l:5 + 2 * l], lam_init[:, l:l + 1],
                                                   ALU.subtract, ALU.subtract).then_inc(lam_step, 1)
                    nc.vector.tensor_tensor(gains[:, l, G_SUB:G_SUB + 1], gains[:, l, G_SUB:G_SUB + 1],
                                            one_less[:, l:l + 1], ALU.mult).then_inc(lam_step, 1)

        first_sem = raw_in = [sem(f"raw_in{i}") for i in range(SLOTS)]
        hi_made = sem("hi_made")
        lo_made = sem("lo_made")
        unit_used = sem("unit_used")
        gains_set = sem("gains_set")
        stats_made = sem("stats_made")
        rstd_made = sem("rstd_made")
        pool_step = sem("pool_step")
        dve_step = sem("dve_step")
        xn_made = sem("xn_made")
        xn_turned = sem("xn_turned")
        h_hi_made = sem("h_hi_made")
        h_lo_made = sem("h_lo_made")
        x_made = sem("x_made")
        lat_copied = sem("lat_copied")
        silu_made = sem("silu_made")
        gated = sem("gated")
        lat_rows_made = sem("lat_rows_made")
        lat_turned = sem("lat_turned")
        lat_hi_made = sem("lat_hi_made")
        lat_lo_made = sem("lat_lo_made")
        kpe_made = sem("kpe_made")
        kpe_spread = sem("kpe_spread")
        r_rows_made = sem("r_rows_made")
        r_turned = sem("r_turned")
        r_cols_made = sem("r_cols_made")
        kv_rows_made = sem("kv_rows_made")
        q_copied = sem("q_copied")
        q_rows_made = sem("q_rows_made")
        qk_turned = sem("qk_turned")
        qk_cols_made = sem("qk_cols_made")
        scores_made = sem("scores_made")
        logits_made = sem("logits_made")
        exp_made = sem("exp_made")
        probs_made = sem("probs_made")
        probs_turned = sem("probs_turned")
        probsT_made = sem("probsT_made")
        mix_made = sem("mix_made")
        pair_hi_made = sem("pair_hi_made")
        pair_lo_made = sem("pair_lo_made")
        head_stats = sem("head_stats")
        head_rows = sem("head_rows")
        head_turned = sem("head_turned")
        head_hi = sem("head_hi")
        head_lo = sem("head_lo")
        tanh_made = sem("tanh_made")
        evacuated = sem("evacuated")
        merged_made = sem("merged_made")
        merged_turned = sem("merged_turned")
        merged_hi = sem("merged_hi")
        merged_lo = sem("merged_lo")
        gain_rows_in = sem("gain_rows_in")
        relu_made = sem("relu_made")
        square_made = sem("square_made")
        hid_hi_made = sem("hid_hi_made")
        hid_lo_made = last_sem = sem("hid_lo_made")

        def tanh_index(first):
            order = [U_G2, U_G2 + 4, U_RG, U_RG + 4, U_G1, U_G1 + 4, U_G0, U_G0 + 4]
            return order.index(first)

        def left_banks(n):
            first = next(f for f, (_, g) in GROUPS.items() if g == n)
            half = first % 8 // 4 ^ (U_DQ % 8 // 4)
            if first == U_LAT:
                return lat_copied, 1
            if first in (U_RQ, U_RK):
                return r_rows_made, 1 + (first == U_RK)
            if U_UKV <= first < U_UQ:
                return kv_rows_made, first - U_UKV + 1
            if U_UQ <= first < U_DQ:
                return q_copied, first - U_UQ + 1
            for i, base in enumerate((U_DQ, U_DK, U_DV, U_RV)):
                if base <= first < base + 8:
                    return evacuated, 2 * i + half + 1
            if U_RG <= first < U_RG + 8:
                return silu_made, half + 1
            for base in (U_G2, U_G1, U_G0):
                if base <= first < base + 8:
                    return tanh_made, tanh_index(first) + 1
            for i, base in enumerate((U_MLAO, U_DIFFO, U_RETO)):
                if base <= first < base + 8:
                    return gated, 2 * i + half + 1
            if U_WOUT <= first < U_WOUT + 8:
                return x_made, TT
            return square_made, U_UP.index(first) + 1

        def layer(l):
            with nc.Block() as block:
                @block.sync
                def _(sp):
                    for u, (name, row, col, kt, n) in enumerate(UNITS):
                        if u >= SLOTS:
                            sp.wait_ge(lo_made, u - SLOTS + 1)
                        sp.dma_start(raw[:, u % SLOTS, 0:kt * n].rearrange("p (k n) -> p k n", k=kt),
                                     io[name][l, row:row + kt * P, col:col + n].rearrange("(k p) n -> p k n", p=P)
                                     ).then_inc(raw_in[u % SLOTS], 16)

                @block.gpsimd
                def _(pool):
                    steps = [0]

                    def settle(ins):
                        steps[0] += 1
                        ins.then_inc(pool_step, 1)
                        pool.wait_ge(pool_step, steps[0])

                    def inverse_rms(j, cols, parts):
                        pool.wait_ge(stats_made, j + 1)
                        for at, n, count in parts:
                            settle(nc.gpsimd.tensor_scalar(rstd[:, j, at:at + n], ss[:, j, at:at + n], 1.0 / count, EPS,
                                                           ALU.mult, ALU.add))
                        nc.gpsimd.tensor_tensor(rstd[:, j, 0:cols], rstd[:, j, 0:cols], neghalf[:, 0:cols],
                                                ALU.pow).then_inc(rstd_made, 1)

                    def post(j):
                        pool.wait_ge(stats_made, j + 1)
                        settle(nc.gpsimd.tensor_tensor(ss[:, j, 2:3], ss[:, j, 0:1], ss[:, j, 1:2], ALU.add))
                        settle(nc.gpsimd.tensor_scalar(rstd[:, j, 0:1], ss[:, j, 2:3], 1.0 / DM, EPS, ALU.mult, ALU.add))
                        nc.gpsimd.tensor_tensor(rstd[:, j, 0:1], rstd[:, j, 0:1], neghalf[:, 0:1],
                                                ALU.pow).then_inc(rstd_made, 1)

                    for t in range(TT):
                        inverse_rms(J_PRE[0] + t, 1, [(0, 1, DM)])
                    inverse_rms(J_LAT, 4, [(0, 2, QL), (2, 2, KVL)])
                    pool.wait_ge(kpe_made, 1)
                    for t in range(TT):
                        nc.gpsimd.tensor_copy(k_rows[:, t, :, MN:MQ],
                                              kpe_tmp[:, t:t + 1, 0:MR].broadcast_to([P, MH, MR])).then_inc(kpe_spread, 1)
                    for k in range(DH):
                        inverse_rms(J_HEAD + k, 2, [(0, 2, 2 * DD)])
                    for k in range(RH):
                        inverse_rms(J_HEAD + DH + k, 2, [(0, 2, RDV)])
                    for t in range(TT):
                        post(J_POST[0] + t)
                    for t in range(TT):
                        inverse_rms(J_PRE[1] + t, 1, [(0, 1, DM)])
                    for t in range(TT):
                        post(J_POST[1] + t)

                @block.scalar
                def _(act):
                    def split(u):
                        _, _, _, kt, n = UNITS[u]
                        act.wait_ge(raw_in[u % SLOTS], 16 * (u // SLOTS + 1))
                        if u >= SLOTS:
                            act.wait_ge(unit_used, u - SLOTS + 1)
                        nc.scalar.activation(w_hi[:, u % SLOTS, 0:kt * n], raw[:, u % SLOTS, 0:kt * n],
                                             ACT.Copy).then_inc(hi_made, 1)

                    def wait_group(first):
                        act.wait_ge(unit_used, first + GROUPS[first][0])

                    def pre_norm_stats(which, t):
                        if which == 1:
                            act.wait_ge(x_made, t + 1)
                        nc.scalar.activation(norm_junk[:, t, :], x[:, t, :], ACT.Square,
                                             accum_out=ss[:, J_PRE[which] + t, 0:1]).then_inc(stats_made, 1)

                    def pre_norm_hi(which):
                        act.wait_ge(xn_turned, which + 1)
                        if which == 0:
                            act.wait_ge(gains_set, 1)
                        g0 = (G_MIX, G_MLP)[which]
                        for k in range(KD):
                            nc.scalar.activation(hT_hi[:, k, :], A[:, k // 2, (k % 2) * S:(k % 2 + 1) * S], ACT.Copy,
                                                 scale=gl[:, g0 + k:g0 + k + 1]).then_inc(h_hi_made, 1)

                    def before_mla(u):
                        if u == U_LAT + 4:
                            wait_group(U_LAT)
                            rows = G[:, group(U_LAT) % 2, :, 0:LAT]
                            for t in range(TT):
                                nc.scalar.activation(lat_junk[:, t, 0:QL], rows[:, t, 0:QL], ACT.Square,
                                                     accum_out=ss[:, J_LAT, t:t + 1])
                            for t in range(TT):
                                ins = nc.scalar.activation(lat_junk[:, t, QL:], rows[:, t, QL:QL + KVL], ACT.Square,
                                                           accum_out=ss[:, J_LAT, 2 + t:3 + t])
                            ins.then_inc(stats_made, 1)
                            nc.scalar.activation(lat[:, :, :], rows, ACT.Copy).then_inc(lat_copied, 1)
                        if u == U_LAT + 8:
                            act.wait_ge(lat_turned, 1)
                            for k in range(3):
                                g = G_Q + k if k < 2 else G_KV
                                src = A[:, k // 2, (k % 2) * S:(k % 2 + 1) * S]
                                nc.scalar.activation(bT_hi[:, k, :], src, ACT.Copy,
                                                     scale=gl[:, g:g + 1]).then_inc(lat_hi_made, 1)
                        for i, at in enumerate((U_RQ + 6, U_RK + 6)):
                            if u == at:
                                act.wait_ge(r_turned, i + 1)
                                nc.scalar.activation(area_r[:, i, :], A[:, 2:4, :].rearrange("p a b -> p (a b)"),
                                                     ACT.Copy).then_inc(r_cols_made, 1)
                        m = u - (U_UKV + 1)
                        if 0 <= m < 4:
                            wait_group(U_UKV + m)
                            kv = G[:, group(U_UKV + m) % 2, :, :].rearrange("p t (h n) -> p t h n", h=4)
                            nc.scalar.activation(k_rows[:, :, 4 * m:4 * m + 4, 0:MN], kv[:, :, :, 0:MN], ACT.Copy)
                            nc.scalar.activation(v_rows[:, :, 4 * m:4 * m + 4, :], kv[:, :, :, MN:],
                                                 ACT.Copy).then_inc(kv_rows_made, 1)
                        m = u - (U_UQ + 1)
                        if 0 <= m < 4:
                            wait_group(U_UQ + m)
                            q = G[:, group(U_UQ + m) % 2, :, 0:4 * MQ].rearrange("p t (h n) -> p t h n", h=4)
                            nc.scalar.activation(q_rows[:, :, 4 * m:4 * m + 4, :], q, ACT.Copy).then_inc(q_copied, 1)

                    def exps(H):
                        if not 0 <= H < MH + 2 * DH:
                            return
                        act.wait_ge(logits_made, H + 1)
                        if H >= MH:
                            act.wait_ge(probs_turned, MH + (H - MH) // 2)
                        elif H >= 2:
                            act.wait_ge(probs_turned, H - 1)
                        b = H % 2
                        nc.scalar.activation(probs[:, b, 0:P], logits[:, b, 0:P], ACT.Exp, bias=negmax[:, b, 0:1],
                                             scale=-1.0, accum_out=rowsum[:, b, 0:1])
                        nc.scalar.activation(probs[:, b, P:384], logits[:, b, P:384], ACT.Exp, bias=negmax[:, b, 1:2],
                                             scale=-1.0, accum_out=rowsum[:, b, 1:2]).then_inc(exp_made, 1)

                    def probs_cols(H):
                        J = mix_index(H)
                        if J is None or J >= MH + DH:
                            return
                        act.wait_ge(probs_turned, J + 1)
                        if J >= 1:
                            act.wait_ge(mix_made, J)
                        nc.scalar.activation(probsT[:, :], A[:, 2, 0:384], ACT.Copy).then_inc(probsT_made, 1)

                    def mixed(H):
                        J, K = mix_index(H), head_index(H)
                        if J is None:
                            return
                        if J < MH and J % 2:
                            act.wait_ge(mix_made, J + 1)
                            nc.scalar.activation(bT_hi[:, J // 2, :], A[:, 3, 0:S], ACT.Copy).then_inc(pair_hi_made, 1)
                        if K is not None and K < DH:
                            act.wait_ge(mix_made, J + 1)
                            if K >= 1:
                                act.wait_ge(head_turned, K)
                            for t in range(TT):
                                ins = nc.scalar.activation(junk[:, t * P:(t + 1) * P], A[:, 3, t * P:(t + 1) * P], ACT.Square,
                                                           scale=rrow_sum[:, K % 2, 0, t:t + 1],
                                                           accum_out=ss[:, J_HEAD + K, t:t + 1])
                            ins.then_inc(stats_made, 1)
                            for t in range(TT):
                                ins = nc.scalar.activation(orow[:, t * P:(t + 1) * P], A[:, 3, t * P:(t + 1) * P],
                                                           ACT.Copy, scale=rrow_sum[:, K % 2, 0, t:t + 1])
                            ins.then_inc(head_stats, 1)
                        if K is not None and K >= DH:
                            act.wait_ge(mix_made, J + 1)
                            for t in range(TT):
                                ins = nc.scalar.activation(junk[:, t * RDV:(t + 1) * RDV], A[:, 3, t * RDV:(t + 1) * RDV], ACT.Square,
                                                           accum_out=ss[:, J_HEAD + K, t:t + 1])
                            ins.then_inc(stats_made, 1)

                    def head_cols(H):
                        K = head_index(H)
                        if K is None:
                            return
                        act.wait_ge(head_turned, K + 1)
                        if K < DH:
                            nc.scalar.activation(dT_hi[:, K, :], A[:, 0, 0:S], ACT.Copy,
                                                 scale=gl[:, G_SUB:G_SUB + 1]).then_inc(head_hi, 1)
                        else:
                            r = K - DH
                            act.wait_ge(unit_used, U_MLAO + 8)
                            nc.scalar.activation(bT_hi[:, 2 * r:2 * r + 2, :].rearrange("p k s -> p (k s)"), A[:, 0, :],
                                                 ACT.Copy, scale=0.5).then_inc(head_hi, 1)

                    def attention(u):
                        s = u - U_DQ
                        if s < 0:
                            return
                        m = s // 2
                        if s % 2 == 0:
                            exps(m - 1)
                            probs_cols(m - 2)
                        else:
                            if m < MH:
                                act.wait_ge(qk_turned, m + 1)
                                if m >= 1:
                                    act.wait_ge(scores_made, m)
                                nc.scalar.activation(qkT[:, :], A[0:MQ, 0, :], ACT.Copy).then_inc(qk_cols_made, 1)
                            mixed(m - 2)
                            head_cols(m - 3)

                    def gates(u):
                        for first, out in ((U_G2, tanh_g), (U_RG, rg_rows), (U_G1, tanh_g1), (U_G0, tanh_g)):
                            for half in range(2):
                                if u == first + 4 * half + 4:
                                    wait_group(first + 4 * half)
                                    if first == U_G0:
                                        act.wait_ge(gated, 2)
                                    if first == U_RG:
                                        act.wait_ge(mix_made, MH)
                                    nc.scalar.activation(
                                        out[:, :, 512 * half:512 * half + 512],
                                        G[:, group(first + 4 * half) % 2, :, :], ACT.Tanh, scale=0.5
                                    ).then_inc(tanh_made, 1)

                    def merged_cols(half):
                        act.wait_ge(merged_turned, half + 1)
                        nc.scalar.activation(hT_hi[:, 4 * half:4 * half + 4, :].rearrange("p k s -> p (k s)"),
                                             A[:, 2 * half:2 * half + 2, :].rearrange("p a b -> p (a b)"),
                                             ACT.Copy, scale=0.5).then_inc(merged_hi, 1)

                    def post_stats(j, t, half, src):
                        ins = nc.scalar.activation(norm_junk[:, t, 512 * half:512 * half + 512], src, ACT.Square,
                                                   accum_out=ss[:, j + t, half:half + 1])
                        if half == 1:
                            ins.then_inc(stats_made, 1)

                    def hidden(u):
                        for j in range(8):
                            if u == U_UP[j] + 4:
                                wait_group(U_UP[j])
                                if j >= 1:
                                    act.wait_ge(square_made, j)
                                nc.scalar.activation(relu_h, G[:, group(U_UP[j]) % 2, :, :].rearrange("p a b -> p (a b)"),
                                                     ACT.Relu).then_inc(relu_made, 1)
                            if u == U_UP[j] + 5:
                                act.wait_ge(square_made, j + 1)
                                if j >= 2:
                                    act.wait_ge(unit_used, U_DN[j - 2] + 4)
                                nc.scalar.activation(hid_hi[:, j % 2, :, :].rearrange("p k s -> p (k s)"), square_h,
                                                     ACT.Copy).then_inc(hid_hi_made, 1)

                    for t in range(TT):
                        pre_norm_stats(0, t)
                    for u in range(SLOTS):
                        split(u)
                    pre_norm_hi(0)
                    for u in range(1, U_UP[0]):
                        if SLOTS <= u + 3:
                            split(u + 3)
                        before_mla(u)
                        attention(u)
                        gates(u)
                        if u == U_RETO:
                            for i, name in enumerate(("post_mix_g", "post_mlp_g")):
                                act.dma_start(gain_rows[:, i, :], io[name][l].rearrange("(a n) -> a n", a=1).broadcast_to([P, DM])).then_inc(
                                    gain_rows_in, 16)
                        if u == U_RETO + 6:
                            merged_cols(0)
                        if u == U_WOUT + 2:
                            merged_cols(1)
                        if u == U_WOUT + 4:
                            wait_group(U_WOUT)
                            for t in range(TT):
                                post_stats(J_POST[0], t, 0, G[:, group(U_WOUT) % 2, t, :])
                    wait_group(U_WOUT + 4)
                    for t in range(TT):
                        post_stats(J_POST[0], t, 1, G[:, group(U_WOUT + 4) % 2, t, :])
                    for t in range(TT):
                        pre_norm_stats(1, t)
                    pre_norm_hi(1)
                    for u in range(U_UP[0], NU):
                        if u + 3 < NU:
                            split(u + 3)
                        hidden(u)
                    act.wait_ge(unit_used, NU)
                    for t in range(TT):
                        for half in range(2):
                            post_stats(J_POST[1], t, half, A[:, 2 * t + half, :])

                @block.vector
                def _(dve):
                    steps = [0]

                    def settle(ins):
                        steps[0] += 1
                        ins.then_inc(dve_step, 1)
                        dve.wait_ge(dve_step, steps[0])

                    def split(u):
                        _, _, _, kt, n = UNITS[u]
                        dve.wait_ge(hi_made, u + 1)
                        nc.vector.tensor_tensor(w_lo[:, u % SLOTS, 0:kt * n], raw[:, u % SLOTS, 0:kt * n],
                                                f32(w_hi[:, u % SLOTS, 0:kt * n]), ALU.subtract).then_inc(lo_made, 1)

                    def wait_group(first):
                        dve.wait_ge(unit_used, first + GROUPS[first][0])

                    def pre_norm_rows(which, t):
                        dve.wait_ge(rstd_made, J_PRE[which] + t + 1)
                        nc.vector.tensor_scalar(xn[:, t, :], x[:, t, :], rstd[:, J_PRE[which] + t, 0:1], None,
                                                ALU.mult).then_inc(xn_made, 1)

                    def pre_norm_lo(which):
                        g0 = (G_MIX, G_MLP)[which]
                        for k in range(KD):
                            dve.wait_ge(h_hi_made, KD * which + k - k % 2 + 2)
                            nc.vector.scalar_tensor_tensor(
                                hT_lo[:, k, :], A[:, k // 2, (k % 2) * S:(k % 2 + 1) * S], gl[:, g0 + k:g0 + k + 1],
                                f32(hT_hi[:, k, :]), ALU.mult, ALU.subtract).then_inc(h_lo_made, 1)

                    def post_norm(which, t, sources):
                        j = J_POST[which] + t
                        dve.wait_ge(rstd_made, j + 1)
                        dve.wait_ge(gain_rows_in, 32)
                        for half, src in enumerate(sources):
                            ins = nc.vector.scalar_tensor_tensor(
                                xn[:, t, 512 * half:512 * half + 512], src, rstd[:, j, 0:1],
                                gain_rows[:, which, 512 * half:512 * half + 512], ALU.mult, ALU.mult)
                            settle(ins)
                        nc.vector.tensor_tensor(x[:, t, :], x[:, t, :], xn[:, t, :], ALU.add).then_inc(x_made, 1)
                        dve.wait_ge(x_made, TT * which + t + 1)

                    def rope(out, src, cos, sin, half, tmp):
                        nc.vector.tensor_tensor(out, src, cos, ALU.mult)
                        nc.vector.tensor_tensor(tmp[..., 0:half], src[..., half:], sin[..., 0:half], ALU.mult)
                        return nc.vector.tensor_tensor(tmp[..., half:], src[..., 0:half], sin[..., half:], ALU.mult)

                    def before_mla(u):
                        if u == U_LAT + 6:
                            dve.wait_ge(rstd_made, J_LAT + 1)
                            dve.wait_ge(lat_copied, 1)
                            kp = lat[:, :, QL + KVL:LAT]
                            settle(rope(kpe_tmp[:, :, 0:MR], kp, m_cos, m_sin, MR // 2, kpe_tmp[:, :, MR:2 * MR]))
                            nc.vector.tensor_tensor(kpe_tmp[:, :, 0:MR], kpe_tmp[:, :, 0:MR], kpe_tmp[:, :, MR:2 * MR],
                                                    ALU.add).then_inc(kpe_made, 1)
                            for t in range(TT):
                                nc.vector.tensor_scalar(lat[:, t, 0:QL], lat[:, t, 0:QL], rstd[:, J_LAT, t:t + 1], None,
                                                        ALU.mult)
                                ins = nc.vector.tensor_scalar(lat[:, t, QL:QL + KVL], lat[:, t, QL:QL + KVL],
                                                              rstd[:, J_LAT, 2 + t:3 + t], None, ALU.mult)
                            ins.then_inc(lat_rows_made, 1)
                        if u == U_LAT + 8:
                            for k in range(3):
                                g = G_Q + k if k < 2 else G_KV
                                dve.wait_ge(lat_hi_made, 2 if k < 2 else 3)
                                nc.vector.scalar_tensor_tensor(
                                    bT_lo[:, k, :], A[:, k // 2, (k % 2) * S:(k % 2 + 1) * S], gl[:, g:g + 1],
                                    f32(bT_hi[:, k, :]), ALU.mult, ALU.subtract).then_inc(lat_lo_made, 1)
                        for i, first in enumerate((U_RQ, U_RK)):
                            if u == first + 4:
                                wait_group(first)
                                if i:
                                    dve.wait_ge(r_turned, 1)
                                cos = r_cos.rearrange("p t (h n) -> p t h n", h=1).broadcast_to([P, TT, RH, RDK])
                                sin = r_sin.rearrange("p t (h n) -> p t h n", h=1).broadcast_to([P, TT, RH, RDK])
                                src = G[:, group(first) % 2, :, :].rearrange("p t (h n) -> p t h n", h=RH)
                                settle(rope(r_rows, src, cos, sin, RDK // 2, r_tmp))
                                nc.vector.tensor_tensor(r_rows, r_rows, r_tmp, ALU.add).then_inc(r_rows_made, 1)
                        m = u - (U_UQ + 1)
                        if 0 <= m < 4:
                            dve.wait_ge(q_copied, m + 1)
                            q = q_rows[:, :, 4 * m:4 * m + 4, MN:MQ]
                            cos = m_cos.rearrange("p t (h n) -> p t h n", h=1).broadcast_to([P, TT, 4, MR])
                            sin = m_sin.rearrange("p t (h n) -> p t h n", h=1).broadcast_to([P, TT, 4, MR])
                            a, b = r_rows[:, :, :, 0:MR], r_rows[:, :, :, MR:2 * MR]
                            if m == 0:
                                dve.wait_ge(r_turned, 2)
                            settle(rope(a, q, cos, sin, MR // 2, b))
                            ins = nc.vector.tensor_tensor(q, a, b, ALU.add)
                            ins.then_inc(q_rows_made, 1)
                            dve.wait_ge(q_rows_made, m + 1)

                    def logits_of(H):
                        if not 0 <= H < N_HEADS:
                            return
                        dve.wait_ge(scores_made, H + 1)
                        b = H % 2
                        if H >= MH + 2 * DH:
                            r = H - MH - 2 * DH
                            if r == 0:
                                dve.wait_ge(exp_made, H)
                            if r >= 2:
                                dve.wait_ge(mix_made, MH + DH + r - 1)
                            nc.vector.tensor_tensor(logits[:, b, :], A[:, 1, 0:384], decay[:, r, :],
                                                    ALU.mult).then_inc(logits_made, 1)
                            return
                        if H >= 2:
                            dve.wait_ge(exp_made, H - 1)
                        if H < MH:
                            add, scale = mask, float(MQ) ** -0.5
                        else:
                            add, scale = bias[:, (H - MH) // 2, :], float(DD) ** -0.5
                        nc.vector.tensor_tensor_reduce(logits[:, b, 0:P], A[:, 1, 0:P], add[:, P:S], -scale, BIG,
                                                       ALU.add, ALU.min, negmax[:, b, 0:1])
                        nc.vector.tensor_tensor_reduce(logits[:, b, P:384], A[:, 1, P:384], add, -scale, BIG,
                                                       ALU.add, ALU.min, negmax[:, b, 1:2]).then_inc(logits_made, 1)

                    def probs_of(H):
                        J = mix_index(H)
                        if J is None or J >= MH + DH:
                            return
                        dve.wait_ge(exp_made, H + 1)
                        if H < MH:
                            b = H % 2
                            settle(nc.vector.reciprocal(rrow_sum[:, b, 0, :], rowsum[:, b, :]))
                            nc.vector.tensor_scalar(probs[:, b, 0:P], probs[:, b, 0:P], rrow_sum[:, b, 0, 0:1], None,
                                                    ALU.mult)
                            nc.vector.tensor_scalar(probs[:, b, P:384], probs[:, b, P:384], rrow_sum[:, b, 0, 1:2], None,
                                                    ALU.mult).then_inc(probs_made, 1)
                        else:
                            k = J - MH
                            if k >= 2:
                                dve.wait_ge(head_stats, k - 1)
                            settle(nc.vector.reciprocal(rrow_sum[:, k % 2, :, :], rowsum[:, :, :]))
                            settle(nc.vector.scalar_tensor_tensor(negr[:, :], rrow_sum[:, k % 2, 1, :],
                                                                  gl[:, G_LAM:G_LAM + 1], rowsum[:, 0, :],
                                                                  ALU.mult, ALU.mult))
                            nc.vector.scalar_tensor_tensor(probs[:, 0, 0:P], probs[:, 1, 0:P], negr[:, 0:1],
                                                           probs[:, 0, 0:P], ALU.mult, ALU.add)
                            nc.vector.scalar_tensor_tensor(probs[:, 0, P:384], probs[:, 1, P:384], negr[:, 1:2],
                                                           probs[:, 0, P:384], ALU.mult, ALU.add).then_inc(probs_made, 1)

                    def pair_lo(H):
                        J = mix_index(H)
                        if J is not None and J < MH and J % 2:
                            dve.wait_ge(pair_hi_made, J // 2 + 1)
                            nc.vector.tensor_tensor(bT_lo[:, J // 2, :], A[:, 3, 0:S], f32(bT_hi[:, J // 2, :]),
                                                    ALU.subtract).then_inc(pair_lo_made, 1)

                    def head_rows_of(H):
                        K = head_index(H)
                        if K is None:
                            return
                        dve.wait_ge(rstd_made, J_HEAD + K + 1)
                        if K >= 1:
                            dve.wait_ge(head_turned, K)
                        for t in range(TT):
                            inv = rstd[:, J_HEAD + K, t:t + 1]
                            if K < DH:
                                if t == 0:
                                    dve.wait_ge(head_stats, K + 1)
                                ins = nc.vector.tensor_scalar(orow[:, t * P:(t + 1) * P], orow[:, t * P:(t + 1) * P], inv,
                                                              None, ALU.mult)
                            else:
                                r = K - DH
                                ins = nc.vector.scalar_tensor_tensor(
                                    orow[:, t * RDV:(t + 1) * RDV], A[:, 3, t * RDV:(t + 1) * RDV], inv,
                                    rg_rows[:, t, r * RDV:(r + 1) * RDV], ALU.mult, ALU.mult)
                        ins.then_inc(head_rows, 1)

                    def head_cols(H):
                        K = head_index(H)
                        if K is None:
                            return
                        dve.wait_ge(head_hi, K + 1)
                        if K < DH:
                            nc.vector.scalar_tensor_tensor(dT_lo[:, K, :], A[:, 0, 0:S], gl[:, G_SUB:G_SUB + 1],
                                                           f32(dT_hi[:, K, :]), ALU.mult, ALU.subtract).then_inc(head_lo, 1)
                        else:
                            r = K - DH
                            nc.vector.scalar_tensor_tensor(
                                bT_lo[:, 2 * r:2 * r + 2, :].rearrange("p k s -> p (k s)"), A[:, 0, :], 0.5,
                                f32(bT_hi[:, 2 * r:2 * r + 2, :]).rearrange("p k s -> p (k s)"),
                                ALU.mult, ALU.subtract).then_inc(head_lo, 1)

                    def attention_first(u):
                        s = u - U_DQ
                        if s >= 0 and s % 2 == 0:
                            logits_of(s // 2 - 1)
                            head_rows_of(s // 2 - 3)

                    def attention_then(u):
                        s = u - U_DQ
                        if s >= 0 and s % 2 == 0:
                            probs_of(s // 2 - 1)
                        if s >= 0 and s % 2 == 1:
                            pair_lo(s // 2 - 2)
                            head_cols(s // 2 - 3)

                    def evacuate(u):
                        for first, out in ((U_DQ, dqT), (U_DK, dkT)):
                            for half in range(2):
                                if u == first + 4 * half + 4:
                                    wait_group(first + 4 * half)
                                    nc.vector.tensor_copy(
                                        out[:, 4 * half:4 * half + 4, :].rearrange("p k s -> p (k s)"),
                                        G[:, group(first + 4 * half) % 2, :, :].rearrange("p a b -> p (a b)")
                                    ).then_inc(evacuated, 1)
                        for first, out in ((U_DV, dv_rows), (U_RV, rv_rows)):
                            for half in range(2):
                                if u == first + 4 * half + 4:
                                    wait_group(first + 4 * half)
                                    if first == U_RV:
                                        dve.wait_ge(mix_made, MH)
                                    nc.vector.tensor_copy(out[:, :, 512 * half:512 * half + 512],
                                                          G[:, group(first + 4 * half) % 2, :, :]).then_inc(evacuated, 1)
                        for half in range(2):
                            cols = slice(512 * half, 512 * half + 512)
                            if u == U_RG + 4 * half + 4:
                                first = U_RG + 4 * half
                                dve.wait_ge(tanh_made, tanh_index(first) + 1)
                                for t in range(TT):
                                    ins = nc.vector.scalar_tensor_tensor(rg_rows[:, t, cols], rg_rows[:, t, cols], 1.0,
                                                                         G[:, group(first) % 2, t, :], ALU.add, ALU.mult)
                                ins.then_inc(silu_made, 1)
                            for i, (first, gate, gate_first) in enumerate((
                                    (U_MLAO, tanh_g, U_G2), (U_DIFFO, tanh_g1, U_G1), (U_RETO, tanh_g, U_G0))):
                                if u == first + 4 * half + 4:
                                    at = first + 4 * half
                                    wait_group(at)
                                    dve.wait_ge(tanh_made, tanh_index(gate_first + 4 * half) + 1)
                                    out = merged if i == 0 else gate
                                    ins = nc.vector.scalar_tensor_tensor(out[:, :, cols], gate[:, :, cols], 1.0,
                                                                         G[:, group(at) % 2, :, :], ALU.add, ALU.mult)
                                    ins.then_inc(gated, 1)
                                    if i:
                                        dve.wait_ge(gated, 2 * i + half + 1)
                                        nc.vector.tensor_tensor(merged[:, :, cols], merged[:, :, cols],
                                                                gate[:, :, cols], ALU.add).then_inc(merged_made, 1)

                    def merged_cols(half):
                        dve.wait_ge(merged_hi, half + 1)
                        nc.vector.scalar_tensor_tensor(
                            hT_lo[:, 4 * half:4 * half + 4, :].rearrange("p k s -> p (k s)"),
                            A[:, 2 * half:2 * half + 2, :].rearrange("p a b -> p (a b)"), 0.5,
                            f32(hT_hi[:, 4 * half:4 * half + 4, :]).rearrange("p k s -> p (k s)"),
                            ALU.mult, ALU.subtract).then_inc(merged_lo, 1)

                    def hidden(u):
                        for j in range(8):
                            if u == U_UP[j] + 4:
                                dve.wait_ge(relu_made, j + 1)
                                if j >= 1:
                                    dve.wait_ge(hid_lo_made, j)
                                ins = nc.vector.tensor_tensor(
                                    square_h, G[:, group(U_UP[j]) % 2, :, :].rearrange("p a b -> p (a b)"), relu_h,
                                    ALU.mult)
                                ins.then_inc(square_made, 1)
                            if u == U_UP[j] + 5:
                                dve.wait_ge(hid_hi_made, j + 1)
                                nc.vector.tensor_tensor(hid_lo[:, j % 2, :, :].rearrange("p k s -> p (k s)"), square_h,
                                                        f32(hid_hi[:, j % 2, :, :]).rearrange("p k s -> p (k s)"),
                                                        ALU.subtract).then_inc(hid_lo_made, 1)

                    nc.vector.tensor_copy(gl[:, :], gains[:, l, :]).then_inc(gains_set, 1)
                    dve.wait_ge(gains_set, 1)
                    for t in range(TT):
                        pre_norm_rows(0, t)
                    for u in range(SLOTS):
                        split(u)
                    pre_norm_lo(0)
                    for u in range(1, U_UP[0]):
                        attention_first(u)
                        if SLOTS <= u + 3:
                            split(u + 3)
                        before_mla(u)
                        attention_then(u)
                        evacuate(u)
                        if u == U_RETO + 6:
                            merged_cols(0)
                        if u == U_WOUT + 2:
                            merged_cols(1)
                    for t in range(TT):
                        post_norm(0, t, [G[:, group(U_WOUT + 4 * half) % 2, t, :] for half in range(2)])
                    for t in range(TT):
                        pre_norm_rows(1, t)
                    pre_norm_lo(1)
                    for u in range(U_UP[0], NU):
                        if u + 3 < NU:
                            split(u + 3)
                        hidden(u)
                    for t in range(TT):
                        post_norm(1, t, [A[:, 2 * t + half, :] for half in range(2)])

                @block.tensor
                def _(pe):
                    def three(out, stationary, moving, start, stop, check=False):
                        for i, (a, b) in enumerate(((0, 0), (0, 1), (1, 0))):
                            ins = nc.tensor.matmul(out, stationary[a], moving[b], start=start and i == 0,
                                                   stop=stop and i == 2, skip_group_check=check)
                        return ins

                    def tokens_stationary(u, n_tiles, first_tile, acts, outs, start, stop):
                        _, _, _, kt, n = UNITS[u]
                        pe.wait_ge(lo_made, u + 1)
                        for kk in range(kt):
                            k = first_tile + kk
                            for t in range(TT):
                                last = three(outs[t],
                                             (acts[0][:, k, t * P:(t + 1) * P], acts[1][:, k, t * P:(t + 1) * P]),
                                             (w_hi[:, u % SLOTS, kk * n:(kk + 1) * n],
                                              w_lo[:, u % SLOTS, kk * n:(kk + 1) * n]),
                                             start and kk == 0, stop and kk == kt - 1)
                        last.then_inc(unit_used, 1)

                    def weights_stationary(u, first_tile, acts, out, start, stop):
                        pe.wait_ge(lo_made, u + 1)
                        for c in range(4):
                            for kk in range(2):
                                k = first_tile + kk
                                at = kk * 512 + c * P
                                last = three(out[:, c, :],
                                             (w_hi[:, u % SLOTS, at:at + P], w_lo[:, u % SLOTS, at:at + P]),
                                             (acts[0][:, k, :], acts[1][:, k, :]),
                                             start and kk == 0 and c % 2 == 0, stop and kk == 1, check=True)
                        last.then_inc(unit_used, 1)

                    def take_pair(first):
                        n = group(first)
                        if n >= 2:
                            pe.wait_ge(*left_banks(n - 2))
                        return G[:, n % 2, :, :]

                    acts_h, acts_b, acts_d = (hT_hi, hT_lo), (bT_hi, bT_lo), (dT_hi, dT_lo)

                    def gemm(u):
                        if u < U_UKV or U_DQ <= u:
                            first, i = u - u % 4, u % 4
                        else:
                            first, i = u, 0
                        pair = take_pair(first) if u == first else G[:, group(first) % 2, :, :]
                        n = UNITS[u][4]
                        start, stop = u == first, u == first + GROUPS[first][0] - 1
                        if U_UKV <= u < U_UQ:
                            tokens_stationary(u, 1, 2, acts_b, [pair[:, t, 0:n] for t in range(TT)], True, True)
                        elif U_UQ <= u < U_DQ:
                            tokens_stationary(u, 2, 0, acts_b, [pair[:, t, 0:n] for t in range(TT)], True, True)
                        elif U_DQ <= u < U_DV or u >= U_UP[0]:
                            weights_stationary(u, 2 * i, acts_h,
                                               pair.rearrange("p t n -> p (t n)").rearrange("p (c s) -> p c s", c=4),
                                               start, stop)
                        else:
                            acts = acts_h
                            if U_MLAO <= u < U_RG or U_RETO <= u < U_WOUT:
                                acts = acts_b
                            if U_DIFFO <= u < U_RETO:
                                acts = acts_d
                            tokens_stationary(u, 2, 2 * i, acts, [pair[:, t, 0:n] for t in range(TT)], start, stop)

                    def norm_turn(which):
                        for t in range(TT):
                            pe.wait_ge(xn_made, TT * which + t + 1)
                            for k in range(KD):
                                last = nc.tensor.transpose(A[:, k // 2, (k % 2) * S + t * P:(k % 2) * S + (t + 1) * P],
                                                           xn[:, t, k * P:(k + 1) * P], ident)
                        last.then_inc(xn_turned, 1)

                    def before_mla(u):
                        if u == U_LAT + 7:
                            pe.wait_ge(lat_rows_made, 1)
                            for k in range(3):
                                for t in range(TT):
                                    last = nc.tensor.transpose(
                                        A[:, k // 2, (k % 2) * S + t * P:(k % 2) * S + (t + 1) * P],
                                        lat[:, t, k * P:(k + 1) * P], ident)
                            last.then_inc(lat_turned, 1)
                        for i, at in enumerate((U_RQ + 5, U_RK + 5)):
                            if u == at:
                                pe.wait_ge(r_rows_made, i + 1)
                                if i:
                                    pe.wait_ge(r_cols_made, 1)
                                for h in range(RH):
                                    for t in range(TT):
                                        last = nc.tensor.transpose(
                                            A[:, 2 + h // 2, (h % 2) * S + t * P:(h % 2) * S + (t + 1) * P],
                                            r_rows[:, t, h, :], ident)
                                last.then_inc(r_turned, 1)

                    def turn_qk(h):
                        if h >= MH:
                            return
                        if h == 0:
                            pe.wait_ge(kpe_spread, TT)
                            pe.wait_ge(kv_rows_made, 4)
                        else:
                            pe.wait_ge(qk_cols_made, h)
                        pe.wait_ge(q_rows_made, h // 4 + 1)
                        for i, rows in enumerate((q_rows, k_rows)):
                            for t in range(TT):
                                last = nc.tensor.transpose(A[0:MQ, 0, i * S + t * P:i * S + (t + 1) * P],
                                                           rows[:, t, h, :], ident)
                        last.then_inc(qk_turned, 1)

                    def scores(H):
                        if not 0 <= H < N_HEADS:
                            return
                        if H >= 1:
                            pe.wait_ge(logits_made, H)
                        out = A[:, 1, :]
                        if H < MH:
                            pe.wait_ge(qk_cols_made, H + 1)
                            nc.tensor.matmul(out[:, 0:P], qkT[:, 0:P], qkT[:, S:S + P], start=True, stop=True)
                            last = nc.tensor.matmul(out[:, P:384], qkT[:, P:S], qkT[:, S:2 * S], start=True, stop=True)
                        elif H < MH + 2 * DH:
                            h, c = (H - MH) // 2, (H - MH) % 2
                            if H == MH:
                                pe.wait_ge(evacuated, 4)
                            q, k = dqT[c * DD:(c + 1) * DD, h, :], dkT[c * DD:(c + 1) * DD, h, :]
                            nc.tensor.matmul(out[:, 0:P], q[:, 0:P], k[:, 0:P], start=True, stop=True)
                            last = nc.tensor.matmul(out[:, P:384], q[:, P:S], k, start=True, stop=True)
                        else:
                            r = H - MH - 2 * DH
                            nc.tensor.matmul(out[:, 0:S], rkT[:, r, 0:P], rqT[:, r, :], start=True, stop=True)
                            last = nc.tensor.matmul(out[:, S:384], rkT[:, r, P:S], rqT[:, r, P:S], start=True, stop=True)
                        last.then_inc(scores_made, 1)

                    def turn_probs(H):
                        J = mix_index(H)
                        if J is None or J >= MH + DH:
                            return
                        pe.wait_ge(probs_made, J + 1)
                        if J >= 1:
                            pe.wait_ge(probsT_made, J)
                        else:
                            pe.wait_ge(r_cols_made, 2)
                        b = J % 2 if J < MH else 0
                        for i in range(3):
                            last = nc.tensor.transpose(A[:, 2, i * P:(i + 1) * P], probs[:, b, i * P:(i + 1) * P], ident)
                        last.then_inc(probs_turned, 1)

                    def mix(H):
                        J = mix_index(H)
                        if J is None:
                            return
                        out = A[:, 3, :]
                        if J < MH + DH:
                            pe.wait_ge(probsT_made, J + 1)
                        if J < MH:
                            if J % 2 == 0 and J >= 2:
                                pe.wait_ge(pair_lo_made, J // 2)
                            row = MV * (J % 2)
                            nc.tensor.matmul(out[row:row + MV, 0:S], v_rows[:, 0, J, :], probsT[:, 0:S], start=True,
                                             stop=False)
                            last = nc.tensor.matmul(out[row:row + MV, P:S], v_rows[:, 1, J, :], probsT[:, S:384],
                                                    start=False, stop=True)
                        elif J < MH + DH:
                            k = J - MH
                            if k == 0:
                                pe.wait_ge(pair_lo_made, MH // 2)
                                pe.wait_ge(evacuated, 6)
                            else:
                                pe.wait_ge(head_stats, k)
                            v0, v1 = dv_rows[:, 0, k * P:(k + 1) * P], dv_rows[:, 1, k * P:(k + 1) * P]
                            nc.tensor.matmul(out[:, 0:P], probsT[:, 0:P], v0, start=True, stop=True)
                            nc.tensor.matmul(out[:, P:S], probsT[:, P:S], v0, start=True, stop=False)
                            last = nc.tensor.matmul(out[:, P:S], probsT[:, S:384], v1, start=False, stop=True)
                        else:
                            r = J - MH - DH
                            pe.wait_ge(logits_made, H + 1)
                            if r == 0:
                                pe.wait_ge(head_stats, DH)
                                pe.wait_ge(evacuated, 8)
                            else:
                                pe.wait_ge(head_rows, DH + r)
                            w = logits[:, H % 2, :]
                            v0, v1 = rv_rows[:, 0, r * RDV:(r + 1) * RDV], rv_rows[:, 1, r * RDV:(r + 1) * RDV]
                            nc.tensor.matmul(out[:, 0:RDV], w[:, 0:P], v0, start=True, stop=True)
                            nc.tensor.matmul(out[:, RDV:2 * RDV], w[:, P:S], v0, start=True, stop=False)
                            last = nc.tensor.matmul(out[:, RDV:2 * RDV], w[:, S:384], v1, start=False, stop=True)
                        last.then_inc(mix_made, 1)

                    def turn_head(H):
                        K = head_index(H)
                        if K is None:
                            return
                        pe.wait_ge(head_rows, K + 1)
                        if K == 0:
                            pe.wait_ge(qk_cols_made, MH)
                        else:
                            pe.wait_ge(head_lo, K)
                        if K < DH:
                            for t in range(TT):
                                last = nc.tensor.transpose(A[:, 0, t * P:(t + 1) * P], orow[:, t * P:(t + 1) * P], ident)
                        else:
                            for f in range(RDV // P):
                                for t in range(TT):
                                    last = nc.tensor.transpose(A[:, 0, f * S + t * P:f * S + (t + 1) * P],
                                                               orow[:, t * RDV + f * P:t * RDV + (f + 1) * P], ident)
                        last.then_inc(head_turned, 1)

                    def attention(u):
                        s = u - U_DQ
                        if s < 0:
                            return
                        m = s // 2
                        if s % 2 == 0:
                            turn_qk(m)
                            mix(m - 2)
                            turn_head(m - 3)
                        else:
                            scores(m)
                            turn_probs(m - 1)

                    def turn_merged(half):
                        pe.wait_ge(merged_made, 2 + half + 1)
                        if half == 0:
                            pe.wait_ge(head_lo, DH + RH)
                        for k in range(4):
                            for t in range(TT):
                                at = (k % 2) * S + t * P
                                last = nc.tensor.transpose(A[:, 2 * half + k // 2, at:at + P],
                                                           merged[:, t, 512 * half + k * P:512 * half + (k + 1) * P],
                                                           ident)
                        last.then_inc(merged_turned, 1)

                    def down(j, u, i):
                        half, pair = i // 2, i % 2
                        tokens_stationary(u, 2, 2 * pair, (hid_hi[:, j % 2, :, :], hid_lo[:, j % 2, :, :]),
                                          [A[:, 2 * t + half, :] for t in range(TT)], j == 0 and pair == 0,
                                          j == 7 and pair == 1)

                    norm_turn(0)
                    for u in range(U_UP[0]):
                        if u < 4:
                            pe.wait_ge(h_lo_made, 2 * u + 2)
                        if u == U_UKV:
                            pe.wait_ge(lat_lo_made, 3)
                        if u == U_MLAO:
                            pe.wait_ge(pair_lo_made, MH // 2)
                        if u == U_DIFFO:
                            pe.wait_ge(head_lo, DH)
                        if u == U_RETO:
                            pe.wait_ge(head_lo, DH + RH)
                        if u == U_WOUT:
                            pe.wait_ge(merged_lo, 1)
                        if u == U_WOUT + 2:
                            pe.wait_ge(merged_lo, 2)
                        gemm(u)
                        before_mla(u)
                        attention(u)
                        if u == U_RETO + 5:
                            turn_merged(0)
                        if u == U_WOUT + 1:
                            turn_merged(1)
                    norm_turn(1)
                    for j in range(9):
                        if j < 8:
                            for i in range(4):
                                if j == 0:
                                    pe.wait_ge(h_lo_made, KD + 2 * i + 2)
                                gemm(U_UP[j] + i)
                        if j >= 1:
                            pe.wait_ge(hid_lo_made, j)
                            for i in range(4):
                                down(j - 1, U_DN[j - 1] + i, i)

        with nc.Fori(0, L) as l:
            layer(l)
            nc.multi_engine_barrier([ENG.PE, ENG.Activation, ENG.DVE, ENG.Pool, ENG.SP],
                                    sems_to_clear=range(first_sem[0].num, last_sem.num + 1))

        out_stored = sem("out_stored")
        with nc.Block() as block:
            @block.sync
            def _(sp):
                sp.dma_start(io["out"][0].rearrange("(t p) d -> p t d", p=P), x[:, :, :]).then_inc(out_stored, 16)
                sp.wait_ge(out_stored, 16)


def shape_constants():
    f = np.float32
    packed = np.zeros((P, K_END), f)
    p, k = np.arange(P)[:, None], np.arange(P)[None, :]
    packed[:, K_ID:K_ID + P] = np.eye(P, dtype=f)
    packed[:, K_MASK + P:K_MASK + S] = np.where(p >= k, 0.0, NEG)
    log_g = np.log1p(-np.exp2(-5.0 - np.arange(RH, dtype=np.float64)))
    for h in range(RH):
        rel = np.arange(S)[None, :] - p
        wide = np.where(rel >= 0, np.exp(np.maximum(rel, 0) * log_g[h]), 0.0) * RDK ** -0.5
        packed[:, K_DEC + 384 * h:K_DEC + 384 * (h + 1)] = np.concatenate([wide, wide[:, 0:P]], axis=1)

    def rotations(at_cos, at_sin, inv_freq, width):
        pos = np.arange(S, dtype=f)
        angle = (pos[:, None] * inv_freq.astype(f)[None, :]).astype(np.float64)
        cos, sin = np.cos(angle), np.sin(angle)
        for t in range(TT):
            rows = slice(t * P, (t + 1) * P)
            packed[:, at_cos + t * width:at_cos + (t + 1) * width] = np.concatenate([cos[rows], cos[rows]], axis=1)
            packed[:, at_sin + t * width:at_sin + (t + 1) * width] = np.concatenate([-sin[rows], sin[rows]], axis=1)

    rotations(K_RC, K_RS, 1.0 / (10000.0 ** np.linspace(0.0, 1.0, RDK // 2)), RDK)
    rotations(K_MC, K_MS, 1.0 / (10000.0 ** (np.arange(0, MR, 2) / MR)), MR)
    init = 0.8 - 0.6 * np.exp(-0.3 * np.arange(L))
    packed[:, K_LI:K_LI + L] = init
    packed[:, K_LI + L:K_LI + 2 * L] = 1.0 - init

    dist = S - 1 - np.arange(LINE)
    exact = BUCKETS // 2
    far = exact + (np.log(np.maximum(dist, 1).astype(f) / f(exact)) / f(np.log(MAX_DIST / exact))
                   * f(BUCKETS - exact)).astype(np.int32)
    bucket = np.where(dist < exact, np.maximum(dist, 0), np.minimum(far, BUCKETS - 1))
    onehot = np.zeros((BUCKETS + 1, LINE), f)
    onehot[bucket, np.arange(LINE)] = dist >= 0
    onehot[BUCKETS] = dist < 0
    return packed, onehot, np.ascontiguousarray(np.eye(P, dtype=f)[::-1])


_INS = ["x", "rel_bias", "pre_mix_g", "w_in", "w_ret_o", "lambda_q1", "lambda_k1", "lambda_q2", "lambda_k2",
        "diff_subln_g", "w_diff_o", "mla_q_norm_g", "w_mla_uq", "mla_kv_norm_g", "w_mla_ukv", "w_mla_o", "w_out",
        "post_mix_g", "pre_mlp_g", "w_up", "w_down", "post_mlp_g"]


def kernel(**inputs):
    import concourse.bacc as bacc
    from concourse.bass_utils import run_bass_kernel_spmd

    nc = bacc.Bacc("TRN2", target_bir_lowering=False, num_devices=1)
    packed, onehot, flip = shape_constants()
    arrays, io = {}, {}
    for name, a in [(n, np.ascontiguousarray(inputs[n])) for n in _INS] + [
            ("consts", packed), ("onehot", onehot), ("flip", flip)]:
        arrays[f"in_{name}"] = a
        io[name] = nc.dram_tensor(f"in_{name}", a.shape, mybir.dt.from_np(a.dtype), kind="ExternalInput").ap()
    io["line"] = nc.dram_tensor("line", (DH, LINE), F32, kind="Internal").ap()
    io["out"] = nc.dram_tensor("out", (1, S, DM), F32, kind="ExternalOutput").ap()
    build(nc, io)
    r = run_bass_kernel_spmd(nc, [arrays], core_ids=[0])
    return r.results[0]["out"]
```

```python
import math
from contextlib import ExitStack

import numpy as np

import concourse.bass as bass
from concourse import mybir

F32 = mybir.dt.float32
F32R = mybir.dt.float32r
ALU = mybir.AluOpType
ACT = mybir.ActivationFunctionType
ENG = mybir.EngineType

P = 128
L, S, DM, FF = 2, 256, 1024, 4096
TT = S // P
KD = DM // P
EPS = 1e-6
RH, RDK, RDV = 4, 128, 256
DH, DD = 8, 64
MH, MN, MR, MV = 16, 64, 32, 64
MQ = MN + MR
QL, KVL = 256, 128
LAT = QL + KVL + MR
NEG = -1e30
BIG = 3e38
BUCKETS, MAX_DIST = 32, 128
LINE = 384
COPIES = 32

C_RQ, C_RK, C_RV, C_RG = 0, 512, 1024, 2048
C_DQ, C_DK, C_DV, C_LAT = 3072, 4096, 5120, 6144
C_G0, C_G1, C_G2 = 6560, 7584, 8608

K_ID = 0
K_MASK = K_ID + P
K_RC = K_MASK + S
K_RS = K_RC + TT * RDK
K_MC = K_RS + TT * RDK
K_MS = K_MC + TT * MR
K_LI = K_MS + TT * MR
K_END = K_LI

G_Q, G_KV, G_SUB, G_LAM, G_INIT, G_LESS, G_N = 0, 2, 3, 4, 5, 6, 7


def lambda_init(l):
    return 0.8 - 0.6 * math.exp(-0.3 * l)


def weight_units():
    units = []

    def rows(name, col, n):
        units.extend((name, 2 * P * i, col, 2, n) for i in range(4))

    rows("w_in", C_LAT, LAT)
    rows("w_in", C_RQ, 512)
    rows("w_in", C_RK, 512)
    units.extend(("w_mla_ukv", 0, 512 * m, 1, 512) for m in range(4))
    units.extend(("w_mla_uq", 0, 4 * MQ * m, 2, 4 * MQ) for m in range(4))
    for name, col in (("w_in", C_DQ), ("w_in", C_DK), ("w_in", C_DV), ("w_in", C_G2), ("w_in", C_RV),
                      ("w_mla_o", 0), ("w_in", C_RG), ("w_in", C_G1), ("w_in", C_G0), ("w_diff_o", 0),
                      ("w_ret_o", 0)):
        rows(name, col, 512)
        rows(name, col + 512, 512)
    for rows_half in range(2):
        for cols_half in range(2):
            units.extend(("w_out", 2 * P * (2 * rows_half + i), 512 * cols_half, 2, 512) for i in range(2))

    def up(j):
        rows("w_up", 512 * j, 512)

    def down(j):
        units.extend(("w_down", 512 * j + 2 * P * (i % 2), 512 * (i // 2), 2, 512) for i in range(4))

    up(0)
    for j in range(1, 8):
        up(j)
        down(j - 1)
    down(7)
    return units


UNITS = weight_units()
NU = len(UNITS)
SLOTS = 4
POOL_UNITS = (2, 3)
U_LAT, U_RQ, U_RK, U_UKV, U_UQ = 0, 4, 8, 12, 16
U_DQ, U_DK, U_DV, U_G2, U_RV, U_MLAO, U_RG, U_G1, U_G0, U_DIFFO, U_RETO, U_WOUT = range(20, 116, 8)
U_UP = [116] + [120 + 8 * (j - 1) for j in range(1, 8)]
U_DN = [124 + 8 * j for j in range(7)] + [176]
assert NU == 180

GROUPS = {}


def _groups():
    n = 0
    for first, units in [(U_LAT, 4), (U_RQ, 4), (U_RK, 4)] + [(u, 1) for u in range(U_UKV, U_DQ)] + \
            [(u, 4) for u in range(U_DQ, U_UP[0], 4)] + [(u, 4) for u in U_UP]:
        GROUPS[first] = (units, n)
        n += 1
    return n


N_GROUPS = _groups()


def group(first):
    return GROUPS[first][1]


J_LAT = 0
J_HEAD = 1
N_JOBS = 13

PRE_MIX, POST_MIX, PRE_MLP, POST_MLP = range(4)
SUMS = [(PRE_MIX, 0, 0), (PRE_MIX, 0, 1), (PRE_MIX, 1, 0), (PRE_MIX, 1, 1), (POST_MIX, 0, 0), (POST_MIX, 0, 1),
        (PRE_MLP, 0, 0), (PRE_MLP, 0, 1), (POST_MIX, 1, 0), (POST_MIX, 1, 1), (PRE_MLP, 1, 0), (PRE_MLP, 1, 1),
        (POST_MLP, 0, 0), (POST_MLP, 0, 1), (POST_MLP, 1, 0), (POST_MLP, 1, 1)]
ROOT_DM = 32.0
assert ROOT_DM ** 2 == DM
R_POST_MIX, R_POST_MLP, R_PRE_MLP, R_NEXT_PRE_MIX = range(4)



def sums_by(norm, t, half):
    return SUMS.index((norm, t, half)) + 1


def inv_by(norm, t):
    return [s[:2] for s in SUMS if s[2]].index((norm, t)) + 1


def normed_by(norm, t, b):
    return 4 * (norm == PRE_MLP) + 2 * t + b + 1


def x_halves_by(norm, t, half):
    return 4 * (norm == POST_MLP) + 2 * t + half + 1

N_HEADS = MH + 2 * DH + RH


def mix_index(H):
    if H < 0 or H >= N_HEADS:
        return None
    if H < MH:
        return H
    if H < MH + 2 * DH:
        return MH + (H - MH) // 2 if H % 2 else None
    return MH + DH + H - MH - 2 * DH


def head_index(H):
    j = mix_index(H)
    return None if j is None or j < MH else j - MH


def build(nc, io):
    with ExitStack() as ctx:
        def sb(name, shape, dt=F32):
            return ctx.enter_context(nc.sbuf_tensor(name, shape, dt))

        def sem(name):
            return ctx.enter_context(nc.semaphore(name))

        raw = sb("raw", [P, SLOTS, 1024])
        w_hi = sb("w_hi", [P, SLOTS, 1024], F32R)
        w_lo = sb("w_lo", [P, SLOTS, 1024], F32R)
        x = sb("x", [P, TT, DM])
        const = sb("const", [P, K_END])
        bias = sb("bias", [P, DH, S])
        decay = sb("decay", [P, RH, 384])
        hT_hi = sb("hT_hi", [P, KD, S], F32R)
        hT_lo = sb("hT_lo", [P, KD, S], F32R)
        bT_hi = sb("bT_hi", [P, KD, S], F32R)
        bT_lo = sb("bT_lo", [P, KD, S], F32R)
        dT_hi = sb("dT_hi", [P, KD, S], F32R)
        dT_lo = sb("dT_lo", [P, KD, S], F32R)
        area_d = sb("area_d", [P, 8192])
        area_e = sb("area_e", [P, 6144])
        area_g = sb("area_g", [P, 2048])
        area_r = sb("area_r", [P, 2, 1024])
        qkT = sb("qkT", [MQ, 2 * S])
        logits = sb("logits", [P, 2, 384])
        probs = sb("probs", [P, 2, 384])
        probsT = sb("probsT", [P, 384])
        orow = sb("orow", [P, 512])
        junk = sb("junk", [P, 512], mybir.dt.bfloat16)
        gains = sb("gains", [P, L, G_N])
        gl = sb("gl", [P, G_N])
        negmax = sb("negmax", [P, 2, 2])
        rowsum = sb("rowsum", [P, 2, 2])
        rrow_sum = sb("rrow_sum", [P, 2, 2, 2])
        negr = sb("negr", [P, 2])
        ss = sb("ss", [P, N_JOBS, 4])
        rstd = sb("rstd", [P, N_JOBS, 4])
        sums = sb("sums", [P, 4, TT, 4])
        inv = sb("inv", [P, 4, TT])
        neghalf = sb("neghalf", [P, 4])
        lam = sb("lam", [P, 8])

        def view(area, first, shape):
            n = int(np.prod(shape))
            flat = area[:, first:first + n]
            names = "abcd"[:len(shape)]
            return flat.rearrange(f"p ({' '.join(names)}) -> p {' '.join(names)}", **dict(zip(names, shape)))

        q_rows = view(area_d, 0, (TT, MH, MQ))
        k_rows = view(area_d, 3072, (TT, MH, MQ))
        v_rows = view(area_d, 6144, (TT, MH, MV))
        rv_rows = view(area_d, 0, (TT, DM))
        rg_rows = view(area_d, 2048, (TT, DM))
        merged = view(area_d, 4096, (TT, DM))
        tanh_g1 = view(area_d, 6144, (TT, DM))
        dqT = view(area_e, 0, (DH, S))
        dkT = view(area_e, 2048, (DH, S))
        dv_rows = view(area_e, 4096, (TT, DM))
        lat = view(area_e, 0, (TT, LAT))
        r_rows = view(area_e, 1024, (TT, RH, RDK))
        r_tmp = view(area_e, 2048, (TT, RH, RDK))
        kpe_tmp = view(area_e, 3072, (TT, 2 * MR))
        r_src = view(area_e, 4096, (TT, RH, RDK))
        gain_rows = view(area_e, 2048, (4, DM))
        tanh_g = view(area_g, 0, (TT, DM))
        xn = view(area_g, 0, (TT, DM))
        rqT = area_r[:, 0, :].rearrange("p (h s) -> p h s", h=RH)
        rkT = area_r[:, 1, :].rearrange("p (h s) -> p h s", h=RH)
        relu_h = area_r[:, 0, :]
        square_h = area_r[:, 1, :]
        norm_junk = area_r[:, :, :]
        lat_junk = view(area_g, 0, (TT, QL + KVL))
        hid_hi = dT_hi[:, :, :].rearrange("p (b k) s -> p b k s", b=2)
        hid_lo = dT_lo[:, :, :].rearrange("p (b k) s -> p b k s", b=2)

        ident = const[:, K_ID:K_ID + P]
        mask = const[:, K_MASK:K_MASK + S]

        r_cos = const[:, K_RC:K_RC + TT * RDK].rearrange("p (t n) -> p t n", t=TT)
        r_sin = const[:, K_RS:K_RS + TT * RDK].rearrange("p (t n) -> p t n", t=TT)
        m_cos = const[:, K_MC:K_MC + TT * MR].rearrange("p (t n) -> p t n", t=TT)
        m_sin = const[:, K_MS:K_MS + TT * MR].rearrange("p (t n) -> p t n", t=TT)


        G = ctx.enter_context(nc.psum_tensor("G", [P, 2, TT, 512], F32))
        A = ctx.enter_context(nc.psum_tensor("A", [P, 4, 512], F32))

        def f32(ap):
            return ap.bitcast(F32)

        rows_in = sem("rows_in")
        x_in = [sem(f"x_in{t}") for t in range(TT)]
        consts_in = sem("consts_in")
        small_in = sem("small_in")
        pool_set = sem("pool_set")
        lines_made = sem("lines_made")
        line_ready = sem("line_ready")
        line_out = sem("line_out")
        lam_step = sem("lam_step")
        lambdas_in = sem("lambdas_in")
        first_gain_in = sem("first_gain_in")
        lam_dots = sem("lam_dots")
        lam_exp = sem("lam_exp")

        lam_vec = area_d[0:DD, 0:4 * L].rearrange("p (l i) -> p l i", l=L)
        lam_prod = area_d[0:DD, 64:64 + 2 * L]
        ones = area_d[0:DD, 128:128 + P]
        rel_in = area_d[0:BUCKETS + 1, 5000:5000 + DH]
        onehot = area_d[0:BUCKETS + 1, 5120:5120 + LINE]
        line_sb = area_d[0:DH, 6000:6000 + LINE]

        with nc.Block() as block:
            @block.sync
            def _(sp):
                sp.dma_start(onehot, io["onehot"]).then_inc(rows_in, 16)
                for t in range(TT):
                    sp.dma_start(x[:, t, :], io["x"][0, t * P:(t + 1) * P, :]).then_inc(x_in[t], 16)

                sp.dma_start(gain_rows[:, R_NEXT_PRE_MIX, :],
                             io["gain_rows"][L - 1:L, R_NEXT_PRE_MIX * DM:].broadcast_to([P, DM])
                             ).then_inc(first_gain_in, 16)
                sp.dma_start(const[:, :], io["consts"]).then_inc(consts_in, 16)
                sp.wait_ge(line_ready, 1)
                sp.dma_start(io["line"].rearrange("r h n -> h r n"),
                             line_sb.rearrange("h (r n) -> h r n", r=1).broadcast_to([DH, COPIES, LINE])
                             ).then_inc(line_out, 16)


            @block.gpsimd
            def _(pool):
                nc.gpsimd.memset(neghalf[:, :], -0.5).then_inc(pool_set, 1)
                pool.wait_ge(pool_set, 1)
                nc.gpsimd.memset(area_d[BUCKETS:BUCKETS + 1, 5000:5000 + DH], NEG).then_inc(pool_set, 1)
                pool.wait_ge(pool_set, 2)
                nc.gpsimd.memset(ones, 1.0).then_inc(pool_set, 1)

            @block.scalar
            def _(act):
                act.dma_start(area_d[0:BUCKETS, 5000:5000 + DH], io["rel_bias"]).then_inc(rows_in, 16)
                act.dma_start(area_d[0:DD, 0:4 * L], io["lambdas"]).then_inc(lambdas_in, 16)
                act.dma_start(gains[:, :, :], io["gains"]).then_inc(small_in, 16)
                act.wait_ge(lines_made, 1)
                nc.scalar.activation(line_sb, A[0:DH, 0, 0:LINE], ACT.Copy, scale=8.0).then_inc(line_ready, 1)
                act.wait_ge(lam_dots, 1)
                nc.scalar.activation(lam[:, 0:2 * L], A[:, 1, 0:2 * L], ACT.Exp).then_inc(lam_exp, 1)

            @block.tensor
            def _(pe):
                pe.wait_ge(rows_in, 32)
                pe.wait_ge(pool_set, 2)
                nc.tensor.matmul(A[0:DH, 0, 0:LINE], rel_in, onehot, start=True, stop=True).then_inc(lines_made, 1)
                pe.wait_ge(lam_step, L)
                pe.wait_ge(pool_set, 3)
                nc.tensor.matmul(A[:, 1, 0:2 * L], ones, lam_prod, start=True, stop=True).then_inc(lam_dots, 1)

            @block.vector
            def _(dve):
                dve.wait_ge(lambdas_in, 16)
                for l in range(L):
                    nc.vector.tensor_tensor(lam_prod[:, 2 * l:2 * l + 2], lam_vec[:, l, 0:4:2], lam_vec[:, l, 1:4:2],
                                            ALU.mult).then_inc(lam_step, 1)
                dve.wait_ge(small_in, 16)
                dve.wait_ge(lam_exp, 1)
                for l in range(L):
                    nc.vector.scalar_tensor_tensor(gains[:, l, G_LAM:G_LAM + 1], lam[:, 2 * l + 1:2 * l + 2],
                                                   lam[:, 2 * l:2 * l + 1], gains[:, l, G_INIT:G_INIT + 1],
                                                   ALU.subtract, ALU.subtract).then_inc(lam_step, 1)
                    nc.vector.tensor_tensor(gains[:, l, G_SUB:G_SUB + 1], gains[:, l, G_SUB:G_SUB + 1],
                                            gains[:, l, G_LESS:G_LESS + 1], ALU.mult).then_inc(lam_step, 1)

        first_sem = raw_in = [sem(f"raw_in{i}") for i in range(SLOTS)]
        hi_made = sem("hi_made")
        lo_made = sem("lo_made")
        pool_lo_made = sem("pool_lo_made")
        unit_used = sem("unit_used")
        gains_set = sem("gains_set")
        sums_made = sem("sums_made")
        inv_made = sem("inv_made")
        tables_in = sem("tables_in")
        y_tile0 = sem("y_tile0")
        y_read = sem("y_read")
        stats_made = sem("stats_made")
        rstd_made = sem("rstd_made")
        pool_step = sem("pool_step")
        dve_step = sem("dve_step")
        xn_made = sem("xn_made")
        xn_turned = sem("xn_turned")
        h_hi_made = sem("h_hi_made")
        h_lo_made = sem("h_lo_made")
        x_made = sem("x_made")
        lat_copied = sem("lat_copied")
        silu_made = sem("silu_made")
        gated = sem("gated")
        lat_rows_made = sem("lat_rows_made")
        lat_turned = sem("lat_turned")
        lat_hi_made = sem("lat_hi_made")
        lat_lo_made = sem("lat_lo_made")
        kpe_made = sem("kpe_made")
        kpe_spread = sem("kpe_spread")
        r_rows_made = sem("r_rows_made")
        r_copied = sem("r_copied")
        r_turned = sem("r_turned")
        r_cols_made = sem("r_cols_made")
        kv_rows_made = sem("kv_rows_made")
        q_copied = sem("q_copied")
        q_rows_made = sem("q_rows_made")
        qk_turned = sem("qk_turned")
        qk_cols_made = sem("qk_cols_made")
        scores_made = sem("scores_made")
        logits_made = sem("logits_made")
        exp_made = sem("exp_made")
        probs_made = sem("probs_made")
        probs_turned = sem("probs_turned")
        probsT_made = sem("probsT_made")
        mix_made = sem("mix_made")
        pair_hi_made = sem("pair_hi_made")
        pair_lo_made = sem("pair_lo_made")
        head_stats = sem("head_stats")
        head_rows = sem("head_rows")
        head_turned = sem("head_turned")
        head_hi = sem("head_hi")
        head_lo = sem("head_lo")
        tanh_made = sem("tanh_made")
        evacuated = sem("evacuated")
        merged_made = sem("merged_made")
        merged_turned = sem("merged_turned")
        merged_hi = sem("merged_hi")
        merged_lo = sem("merged_lo")
        gain_rows_in = sem("gain_rows_in")
        relu_made = sem("relu_made")
        square_made = sem("square_made")
        hid_hi_made = sem("hid_hi_made")
        hid_lo_made = last_sem = sem("hid_lo_made")

        def tanh_index(first):
            order = [U_G2, U_G2 + 4, U_RG, U_RG + 4, U_G1, U_G1 + 4, U_G0, U_G0 + 4]
            return order.index(first)

        def left_banks(n):
            first = next(f for f, (_, g) in GROUPS.items() if g == n)
            half = first % 8 // 4 ^ (U_DQ % 8 // 4)
            if first == U_LAT:
                return lat_copied, 1
            if first in (U_RQ, U_RK):
                return r_copied, 1 + (first == U_RK)
            if U_UKV <= first < U_UQ:
                return kv_rows_made, first - U_UKV + 1
            if U_UQ <= first < U_DQ:
                return q_copied, first - U_UQ + 1
            for i, base in enumerate((U_DQ, U_DK, U_DV, U_RV)):
                if base <= first < base + 8:
                    return evacuated, 2 * i + half + 1
            if U_RG <= first < U_RG + 8:
                return silu_made, half + 1
            for base in (U_G2, U_G1, U_G0):
                if base <= first < base + 8:
                    return tanh_made, tanh_index(first) + 1
            for i, base in enumerate((U_MLAO, U_DIFFO, U_RETO)):
                if base <= first < base + 8:
                    return gated, 2 * i + half + 1
            if U_WOUT <= first < U_WOUT + 8:
                return y_read, 2 * (TT - 1) + half + 1
            return square_made, U_UP.index(first) + 1

        def lo_ready(u):
            if u in POOL_UNITS:
                return pool_lo_made, u - POOL_UNITS[0] + 1
            return lo_made, u + 1 - (len(POOL_UNITS) if u > POOL_UNITS[0] else 0)

        def layer(l):
            with nc.Block() as block:
                @block.sync
                def _(sp):
                    for u, (name, row, col, kt, n) in enumerate(UNITS):
                        if u >= SLOTS:
                            sp.wait_ge(*lo_ready(u - SLOTS))
                        for first in range(0, P, COPIES):
                            if u == U_DQ + 2 + first // COPIES * 4:
                                sp.wait_ge(line_out, 16)
                                shifted = bass.AP(io["line"].tensor, P - 1 - first,
                                                  [[DH * LINE - 1, COPIES], [LINE, DH], [1, S]])
                                sp.dma_start(bias[first:first + COPIES, :, :], shifted).then_inc(tables_in, 16)
                        if u == U_G2:
                            sp.dma_start(decay[:, :, :], io["decay"]).then_inc(tables_in, 16)
                        sp.dma_start(raw[:, u % SLOTS, 0:kt * n].rearrange("p (k n) -> p k n", k=kt),
                                     io[name][l, row:row + kt * P, col:col + n].rearrange("(k p) n -> p k n", p=P)
                                     ).then_inc(raw_in[u % SLOTS], 16)

                @block.gpsimd
                def _(pool):
                    steps = [0]

                    def settle(ins):
                        steps[0] += 1
                        ins.then_inc(pool_step, 1)
                        pool.wait_ge(pool_step, steps[0])

                    def inverse_rms(j, cols, parts):
                        pool.wait_ge(stats_made, j + 1)
                        for at, n, count in parts:
                            settle(nc.gpsimd.tensor_scalar(rstd[:, j, at:at + n], ss[:, j, at:at + n], 1.0 / count, EPS,
                                                           ALU.mult, ALU.add))
                        nc.gpsimd.tensor_tensor(rstd[:, j, 0:cols], rstd[:, j, 0:cols], neghalf[:, 0:cols],
                                                ALU.pow).then_inc(rstd_made, 1)




                    def inverse_roots(which):
                        for norm, t, half in SUMS:
                            if norm not in which:
                                continue
                            pool.wait_ge(sums_made, sums_by(norm, t, half))
                            if half == 0:
                                settle(nc.gpsimd.tensor_scalar(sums[:, norm, t, 2:3], sums[:, norm, t, 0:1], EPS,
                                                               None, ALU.add))
                            else:
                                settle(nc.gpsimd.tensor_tensor(sums[:, norm, t, 3:4], sums[:, norm, t, 1:2],
                                                               sums[:, norm, t, 2:3], ALU.add))
                                nc.gpsimd.tensor_tensor(inv[:, norm, t:t + 1], sums[:, norm, t, 3:4],
                                                        neghalf[:, 0:1], ALU.pow).then_inc(inv_made, 1)

                    inverse_roots((PRE_MIX,))
                    for i, u in enumerate(POOL_UNITS):
                        _, _, _, kt, n = UNITS[u]
                        pool.wait_ge(hi_made, u + 1)
                        nc.gpsimd.tensor_tensor(w_lo[:, u % SLOTS, 0:kt * n], raw[:, u % SLOTS, 0:kt * n],
                                                f32(w_hi[:, u % SLOTS, 0:kt * n]), ALU.subtract).then_inc(pool_lo_made, 1)
                        pool.wait_ge(pool_lo_made, i + 1)
                    inverse_rms(J_LAT, 4, [(0, 2, QL), (2, 2, KVL)])
                    pool.wait_ge(kpe_made, 1)
                    for t in range(TT):
                        nc.gpsimd.tensor_copy(k_rows[:, t, :, MN:MQ],
                                              kpe_tmp[:, t:t + 1, 0:MR].broadcast_to([P, MH, MR])).then_inc(kpe_spread, 1)
                    for k in range(DH):
                        inverse_rms(J_HEAD + k, 2, [(0, 2, 2 * DD)])
                    for k in range(RH):
                        inverse_rms(J_HEAD + DH + k, 2, [(0, 2, RDV)])
                    inverse_roots((POST_MIX, PRE_MLP, POST_MLP))


                @block.scalar
                def _(act):
                    def split(u):
                        _, _, _, kt, n = UNITS[u]
                        act.wait_ge(raw_in[u % SLOTS], 16 * (u // SLOTS + 1))
                        if u >= SLOTS:
                            act.wait_ge(unit_used, u - SLOTS + 1)
                        nc.scalar.activation(w_hi[:, u % SLOTS, 0:kt * n], raw[:, u % SLOTS, 0:kt * n],
                                             ACT.Copy).then_inc(hi_made, 1)

                    def wait_group(first):
                        act.wait_ge(unit_used, first + GROUPS[first][0])

                    def add_squares(norm, t, half, src):
                        nc.scalar.activation(norm_junk[:, t, 512 * half:512 * half + 512], src, ACT.Square,
                                             scale=1.0 / ROOT_DM, accum_out=sums[:, norm, t, half:half + 1]).then_inc(sums_made, 1)

                    def y_squares(norm, t, half, bank):
                        if t == 0:
                            act.wait_ge(y_tile0, 2 * (norm == POST_MLP) + half + 1)
                        else:
                            first = U_DN[7] if norm == POST_MLP else U_WOUT + 4
                            act.wait_ge(unit_used, first + 2 * half + 2)
                        add_squares(norm, t, half, bank)

                    def pre_mlp_squares(t):
                        for half in range(2):
                            act.wait_ge(x_made, x_halves_by(POST_MIX, t, half))
                            add_squares(PRE_MLP, t, half, x[:, t, 512 * half:512 * half + 512])

                    def normed_hi(norm, t, b):
                        act.wait_ge(xn_turned, normed_by(norm, t, b))
                        nc.scalar.activation(hT_hi[:, 4 * b:4 * b + 4, t * P:(t + 1) * P],
                                             A[:, 2 * t + b, :].rearrange("p (k s) -> p k s", k=4),
                                             ACT.Copy).then_inc(h_hi_made, 1)

                    def before_mla(u):
                        if u == U_LAT + 4:
                            wait_group(U_LAT)
                            rows = G[:, group(U_LAT) % 2, :, 0:LAT]
                            for t in range(TT):
                                nc.scalar.activation(lat_junk[:, t, 0:QL], rows[:, t, 0:QL], ACT.Square,
                                                     accum_out=ss[:, J_LAT, t:t + 1])
                            for t in range(TT):
                                ins = nc.scalar.activation(lat_junk[:, t, QL:], rows[:, t, QL:QL + KVL], ACT.Square,
                                                           accum_out=ss[:, J_LAT, 2 + t:3 + t])
                            ins.then_inc(stats_made, 1)
                            nc.scalar.activation(lat[:, :, :], rows, ACT.Copy).then_inc(lat_copied, 1)
                        if u == U_LAT + 8:
                            act.wait_ge(lat_turned, 1)
                            for k in range(3):
                                g = G_Q + k if k < 2 else G_KV
                                src = A[:, k // 2, (k % 2) * S:(k % 2 + 1) * S]
                                nc.scalar.activation(bT_hi[:, k, :], src, ACT.Copy,
                                                     scale=gl[:, g:g + 1]).then_inc(lat_hi_made, 1)
                        for i, first in enumerate((U_RQ, U_RK)):
                            if u == first + 4:
                                wait_group(first)
                                if i:
                                    act.wait_ge(r_rows_made, 1)
                                nc.scalar.activation(r_src, G[:, group(first) % 2, :, :].rearrange(
                                    "p t (h n) -> p t h n", h=RH), ACT.Copy).then_inc(r_copied, 1)
                        m = u - (U_UKV + 1)
                        if 0 <= m < 4:
                            wait_group(U_UKV + m)
                            kv = G[:, group(U_UKV + m) % 2, :, :].rearrange("p t (h n) -> p t h n", h=4)
                            nc.scalar.activation(k_rows[:, :, 4 * m:4 * m + 4, 0:MN], kv[:, :, :, 0:MN], ACT.Copy)
                            nc.scalar.activation(v_rows[:, :, 4 * m:4 * m + 4, :], kv[:, :, :, MN:],
                                                 ACT.Copy).then_inc(kv_rows_made, 1)
                        m = u - (U_UQ + 1)
                        if 0 <= m < 4:
                            wait_group(U_UQ + m)
                            q = G[:, group(U_UQ + m) % 2, :, 0:4 * MQ].rearrange("p t (h n) -> p t h n", h=4)
                            nc.scalar.activation(q_rows[:, :, 4 * m:4 * m + 4, :], q, ACT.Copy).then_inc(q_copied, 1)
                        for i, at in enumerate((U_RQ + 8, U_RK + 9)):
                            if u == at:
                                act.wait_ge(r_turned, i + 1)
                                nc.scalar.activation(area_r[:, i, :], A[:, 2:4, :].rearrange("p a b -> p (a b)"),
                                                     ACT.Copy).then_inc(r_cols_made, 1)

                    def exps(H):
                        if not 0 <= H < MH + 2 * DH:
                            return
                        act.wait_ge(logits_made, H + 1)
                        if H >= MH:
                            act.wait_ge(probs_turned, MH + (H - MH) // 2)
                        elif H >= 2:
                            act.wait_ge(probs_turned, H - 1)
                        b = H % 2
                        nc.scalar.activation(probs[:, b, 0:P], logits[:, b, 0:P], ACT.Exp, bias=negmax[:, b, 0:1],
                                             scale=-1.0, accum_out=rowsum[:, b, 0:1])
                        nc.scalar.activation(probs[:, b, P:384], logits[:, b, P:384], ACT.Exp, bias=negmax[:, b, 1:2],
                                             scale=-1.0, accum_out=rowsum[:, b, 1:2]).then_inc(exp_made, 1)

                    def probs_cols(H):
                        J = mix_index(H)
                        if J is None or J >= MH + DH:
                            return
                        act.wait_ge(probs_turned, J + 1)
                        if J >= 1:
                            act.wait_ge(mix_made, J)
                        nc.scalar.activation(probsT[:, :], A[:, 2, 0:384], ACT.Copy).then_inc(probsT_made, 1)

                    def mixed(H):
                        J, K = mix_index(H), head_index(H)
                        if J is None:
                            return
                        if J < MH and J % 2:
                            act.wait_ge(mix_made, J + 1)
                            nc.scalar.activation(bT_hi[:, J // 2, :], A[:, 3, 0:S], ACT.Copy).then_inc(pair_hi_made, 1)
                        if K is not None and K < DH:
                            act.wait_ge(mix_made, J + 1)
                            if K >= 1:
                                act.wait_ge(head_turned, K)
                            for t in range(TT):
                                ins = nc.scalar.activation(junk[:, t * P:(t + 1) * P], A[:, 3, t * P:(t + 1) * P], ACT.Square,
                                                           scale=rrow_sum[:, K % 2, 0, t:t + 1],
                                                           accum_out=ss[:, J_HEAD + K, t:t + 1])
                            ins.then_inc(stats_made, 1)
                            for t in range(TT):
                                ins = nc.scalar.activation(orow[:, t * P:(t + 1) * P], A[:, 3, t * P:(t + 1) * P],
                                                           ACT.Copy, scale=rrow_sum[:, K % 2, 0, t:t + 1])
                            ins.then_inc(head_stats, 1)
                        if K is not None and K >= DH:
                            act.wait_ge(mix_made, J + 1)
                            for t in range(TT):
                                ins = nc.scalar.activation(junk[:, t * RDV:(t + 1) * RDV], A[:, 3, t * RDV:(t + 1) * RDV], ACT.Square,
                                                           accum_out=ss[:, J_HEAD + K, t:t + 1])
                            ins.then_inc(stats_made, 1)

                    def head_cols(H):
                        K = head_index(H)
                        if K is None:
                            return
                        act.wait_ge(head_turned, K + 1)
                        if K < DH:
                            nc.scalar.activation(dT_hi[:, K, :], A[:, 0, 0:S], ACT.Copy,
                                                 scale=gl[:, G_SUB:G_SUB + 1]).then_inc(head_hi, 1)
                        else:
                            r = K - DH
                            act.wait_ge(unit_used, U_MLAO + 8)
                            nc.scalar.activation(bT_hi[:, 2 * r:2 * r + 2, :].rearrange("p k s -> p (k s)"), A[:, 0, :],
                                                 ACT.Copy, scale=0.5).then_inc(head_hi, 1)

                    def attention(u):
                        s = u - U_DQ
                        if s < 0:
                            return
                        m = s // 2
                        if s % 2 == 0:
                            exps(m - 1)
                            probs_cols(m - 2)
                        else:
                            if m < MH:
                                act.wait_ge(qk_turned, m + 1)
                                if m >= 1:
                                    act.wait_ge(scores_made, m)
                                nc.scalar.activation(qkT[:, :], A[0:MQ, 0, :], ACT.Copy).then_inc(qk_cols_made, 1)
                            mixed(m - 2)
                            head_cols(m - 3)

                    def gates(u):
                        for first, out in ((U_G2, tanh_g), (U_RG, rg_rows), (U_G1, tanh_g1), (U_G0, tanh_g)):
                            for half in range(2):
                                if u == first + 4 * half + 4:
                                    wait_group(first + 4 * half)
                                    if first == U_G0:
                                        act.wait_ge(gated, 2)
                                    if first == U_RG:
                                        act.wait_ge(mix_made, MH)
                                    nc.scalar.activation(
                                        out[:, :, 512 * half:512 * half + 512],
                                        G[:, group(first + 4 * half) % 2, :, :], ACT.Tanh, scale=0.5
                                    ).then_inc(tanh_made, 1)

                    def merged_cols(half):
                        act.wait_ge(merged_turned, half + 1)
                        nc.scalar.activation(hT_hi[:, 4 * half:4 * half + 4, :].rearrange("p k s -> p (k s)"),
                                             A[:, 2 * half:2 * half + 2, :].rearrange("p a b -> p (a b)"),
                                             ACT.Copy, scale=0.5).then_inc(merged_hi, 1)



                    def hidden(u):
                        for j in range(8):
                            if u == U_UP[j] + 4:
                                wait_group(U_UP[j])
                                if j >= 1:
                                    act.wait_ge(square_made, j)
                                nc.scalar.activation(relu_h, G[:, group(U_UP[j]) % 2, :, :].rearrange("p a b -> p (a b)"),
                                                     ACT.Relu).then_inc(relu_made, 1)
                            if u == U_UP[j] + 5:
                                act.wait_ge(square_made, j + 1)
                                if j >= 2:
                                    act.wait_ge(unit_used, U_DN[j - 2] + 4)
                                nc.scalar.activation(hid_hi[:, j % 2, :, :].rearrange("p k s -> p (k s)"), square_h,
                                                     ACT.Copy).then_inc(hid_hi_made, 1)

                    for t in range(TT):
                        act.wait_ge(x_in[t], 16)
                        for half in range(2):
                            add_squares(PRE_MIX, t, half, x[:, t, 512 * half:512 * half + 512])
                    split(0)
                    normed_hi(PRE_MIX, 0, 0)
                    split(1)
                    normed_hi(PRE_MIX, 0, 1)
                    split(2)
                    normed_hi(PRE_MIX, 1, 0)
                    normed_hi(PRE_MIX, 1, 1)
                    split(3)
                    for u in range(1, U_WOUT + 5):
                        if u in (U_RQ + 4, U_RK + 4) or U_UKV < u <= U_DQ:
                            before_mla(u)
                            split(u + 3)
                        else:
                            split(u + 3)
                            before_mla(u)
                        attention(u)
                        gates(u)
                        if u == U_RETO:
                            act.dma_start(area_e[:, 2048:2048 + 4 * DM],
                                          io["gain_rows"][l].rearrange("(a n) -> a n", a=1).broadcast_to([P, 4 * DM])
                                          ).then_inc(gain_rows_in, 16)
                        if u == U_RETO + 6:
                            merged_cols(0)
                        if u == U_WOUT + 2:
                            merged_cols(1)
                    y = [[G[:, group(U_WOUT + 4 * half) % 2, t, :] for half in range(2)] for t in range(TT)]
                    for half in range(2):
                        y_squares(POST_MIX, 0, half, y[0][half])
                    pre_mlp_squares(0)
                    y_squares(POST_MIX, 1, 0, y[1][0])
                    split(U_UP[0])
                    y_squares(POST_MIX, 1, 1, y[1][1])
                    normed_hi(PRE_MLP, 0, 0)
                    normed_hi(PRE_MLP, 0, 1)
                    pre_mlp_squares(1)
                    normed_hi(PRE_MLP, 1, 0)
                    split(U_UP[0] + 1)
                    normed_hi(PRE_MLP, 1, 1)
                    split(U_UP[0] + 2)
                    for u in range(U_UP[0], NU):
                        if u + 3 < NU:
                            split(u + 3)
                        hidden(u)
                    for t in range(TT):
                        for half in range(2):
                            y_squares(POST_MLP, t, half, A[:, 2 * t + half, :])

                @block.vector
                def _(dve):
                    steps, reads = [0], [0]

                    def settle(ins):
                        steps[0] += 1
                        ins.then_inc(dve_step, 1)
                        dve.wait_ge(dve_step, steps[0])

                    def split(u):
                        _, _, _, kt, n = UNITS[u]
                        dve.wait_ge(hi_made, u + 1)
                        nc.vector.tensor_tensor(w_lo[:, u % SLOTS, 0:kt * n], raw[:, u % SLOTS, 0:kt * n],
                                                f32(w_hi[:, u % SLOTS, 0:kt * n]), ALU.subtract).then_inc(lo_made, 1)

                    def wait_group(first):
                        dve.wait_ge(unit_used, first + GROUPS[first][0])



                    def pre_norm_rows(norm, t, half):
                        if norm == PRE_MIX:
                            dve.wait_ge(x_in[t], 16)
                            dve.wait_ge(first_gain_in, 16)
                        dve.wait_ge(inv_made, inv_by(norm, t))
                        cols = slice(512 * half, 512 * half + 512)
                        nc.vector.scalar_tensor_tensor(xn[:, t, cols], x[:, t, cols], inv[:, norm, t:t + 1],
                                                       gain_rows[:, R_PRE_MLP if norm == PRE_MLP else R_NEXT_PRE_MIX, cols],
                                                       ALU.mult, ALU.mult).then_inc(xn_made, 1)

                    def normed_lo(norm, t, b):
                        dve.wait_ge(h_hi_made, normed_by(norm, t, b))
                        nc.vector.tensor_tensor(hT_lo[:, 4 * b:4 * b + 4, t * P:(t + 1) * P],
                                                A[:, 2 * t + b, :].rearrange("p (k s) -> p k s", k=4),
                                                f32(hT_hi[:, 4 * b:4 * b + 4, t * P:(t + 1) * P]),
                                                ALU.subtract).then_inc(h_lo_made, 1)

                    def gained(norm, t, half, y):
                        dve.wait_ge(sums_made, sums_by(norm, t, half))
                        cols = slice(512 * half, 512 * half + 512)
                        nc.vector.tensor_tensor(xn[:, t, cols], y,
                                                gain_rows[:, R_POST_MLP if norm == POST_MLP else R_POST_MIX, cols],
                                                ALU.mult).then_inc(y_read, 1)
                        reads[0] += 1

                    def post_norm(norm, t):
                        dve.wait_ge(inv_made, inv_by(norm, t))
                        dve.wait_ge(y_read, reads[0])
                        for half in range(2):
                            cols = slice(512 * half, 512 * half + 512)
                            nc.vector.scalar_tensor_tensor(x[:, t, cols], xn[:, t, cols], inv[:, norm, t:t + 1],
                                                           x[:, t, cols], ALU.mult, ALU.add).then_inc(x_made, 1)

                    def rope(out, src, cos, sin, half, tmp):
                        nc.vector.tensor_tensor(out, src, cos, ALU.mult)
                        nc.vector.tensor_tensor(tmp[..., 0:half], src[..., half:], sin[..., 0:half], ALU.mult)
                        return nc.vector.tensor_tensor(tmp[..., half:], src[..., 0:half], sin[..., half:], ALU.mult)

                    def before_mla(u):
                        if u == U_LAT + 6:
                            dve.wait_ge(rstd_made, J_LAT + 1)
                            dve.wait_ge(lat_copied, 1)
                            kp = lat[:, :, QL + KVL:LAT]
                            settle(rope(kpe_tmp[:, :, 0:MR], kp, m_cos, m_sin, MR // 2, kpe_tmp[:, :, MR:2 * MR]))
                            nc.vector.tensor_tensor(kpe_tmp[:, :, 0:MR], kpe_tmp[:, :, 0:MR], kpe_tmp[:, :, MR:2 * MR],
                                                    ALU.add).then_inc(kpe_made, 1)
                            for t in range(TT):
                                nc.vector.tensor_scalar(lat[:, t, 0:QL], lat[:, t, 0:QL], rstd[:, J_LAT, t:t + 1], None,
                                                        ALU.mult)
                                ins = nc.vector.tensor_scalar(lat[:, t, QL:QL + KVL], lat[:, t, QL:QL + KVL],
                                                              rstd[:, J_LAT, 2 + t:3 + t], None, ALU.mult)
                            ins.then_inc(lat_rows_made, 1)
                        if u == U_LAT + 8:
                            for k in range(3):
                                g = G_Q + k if k < 2 else G_KV
                                dve.wait_ge(lat_hi_made, 2 if k < 2 else 3)
                                nc.vector.scalar_tensor_tensor(
                                    bT_lo[:, k, :], A[:, k // 2, (k % 2) * S:(k % 2 + 1) * S], gl[:, g:g + 1],
                                    f32(bT_hi[:, k, :]), ALU.mult, ALU.subtract).then_inc(lat_lo_made, 1)
                        for i, first in enumerate((U_RQ, U_RK)):
                            if u == first + 4:
                                dve.wait_ge(r_copied, i + 1)
                                if i:
                                    dve.wait_ge(r_turned, 1)
                                cos = r_cos.rearrange("p t (h n) -> p t h n", h=1).broadcast_to([P, TT, RH, RDK])
                                sin = r_sin.rearrange("p t (h n) -> p t h n", h=1).broadcast_to([P, TT, RH, RDK])
                                settle(rope(r_rows, r_src, cos, sin, RDK // 2, r_tmp))
                                nc.vector.tensor_tensor(r_rows, r_rows, r_tmp, ALU.add).then_inc(r_rows_made, 1)
                        m = u - (U_UQ + 1)
                        if 0 <= m < 4:
                            dve.wait_ge(q_copied, m + 1)
                            q = q_rows[:, :, 4 * m:4 * m + 4, MN:MQ]
                            cos = m_cos.rearrange("p t (h n) -> p t h n", h=1).broadcast_to([P, TT, 4, MR])
                            sin = m_sin.rearrange("p t (h n) -> p t h n", h=1).broadcast_to([P, TT, 4, MR])
                            a, b = r_rows[:, :, :, 0:MR], r_rows[:, :, :, MR:2 * MR]
                            if m == 0:
                                dve.wait_ge(r_turned, 2)
                            settle(rope(a, q, cos, sin, MR // 2, b))
                            ins = nc.vector.tensor_tensor(q, a, b, ALU.add)
                            ins.then_inc(q_rows_made, 1)
                            dve.wait_ge(q_rows_made, m + 1)

                    def logits_of(H):
                        if not 0 <= H < N_HEADS:
                            return
                        dve.wait_ge(scores_made, H + 1)
                        b = H % 2
                        if H >= MH + 2 * DH:
                            r = H - MH - 2 * DH
                            if r == 0:
                                dve.wait_ge(exp_made, H)
                            if r >= 2:
                                dve.wait_ge(mix_made, MH + DH + r - 1)
                            nc.vector.tensor_tensor(logits[:, b, :], A[:, 1, 0:384], decay[:, r, :],
                                                    ALU.mult).then_inc(logits_made, 1)
                            return
                        if H >= 2:
                            dve.wait_ge(exp_made, H - 1)
                        if H == MH:
                            dve.wait_ge(tables_in, 16 * (P // COPIES + 1))
                        if H < MH:
                            add, scale = mask, float(MQ) ** -0.5
                        else:
                            add, scale = bias[:, (H - MH) // 2, :], float(DD) ** -0.5
                        nc.vector.tensor_tensor_reduce(logits[:, b, 0:P], A[:, 1, 0:P], add[:, P:S], -scale, BIG,
                                                       ALU.add, ALU.min, negmax[:, b, 0:1])
                        nc.vector.tensor_tensor_reduce(logits[:, b, P:384], A[:, 1, P:384], add, -scale, BIG,
                                                       ALU.add, ALU.min, negmax[:, b, 1:2]).then_inc(logits_made, 1)

                    def probs_of(H):
                        J = mix_index(H)
                        if J is None or J >= MH + DH:
                            return
                        dve.wait_ge(exp_made, H + 1)
                        if H < MH:
                            b = H % 2
                            settle(nc.vector.reciprocal(rrow_sum[:, b, 0, :], rowsum[:, b, :]))
                            nc.vector.tensor_scalar(probs[:, b, 0:P], probs[:, b, 0:P], rrow_sum[:, b, 0, 0:1], None,
                                                    ALU.mult)
                            nc.vector.tensor_scalar(probs[:, b, P:384], probs[:, b, P:384], rrow_sum[:, b, 0, 1:2], None,
                                                    ALU.mult).then_inc(probs_made, 1)
                        else:
                            k = J - MH
                            if k >= 2:
                                dve.wait_ge(head_stats, k - 1)
                            settle(nc.vector.reciprocal(rrow_sum[:, k % 2, :, :], rowsum[:, :, :]))
                            settle(nc.vector.scalar_tensor_tensor(negr[:, :], rrow_sum[:, k % 2, 1, :],
                                                                  gl[:, G_LAM:G_LAM + 1], rowsum[:, 0, :],
                                                                  ALU.mult, ALU.mult))
                            nc.vector.scalar_tensor_tensor(probs[:, 0, 0:P], probs[:, 1, 0:P], negr[:, 0:1],
                                                           probs[:, 0, 0:P], ALU.mult, ALU.add)
                            nc.vector.scalar_tensor_tensor(probs[:, 0, P:384], probs[:, 1, P:384], negr[:, 1:2],
                                                           probs[:, 0, P:384], ALU.mult, ALU.add).then_inc(probs_made, 1)

                    def pair_lo(H):
                        J = mix_index(H)
                        if J is not None and J < MH and J % 2:
                            dve.wait_ge(pair_hi_made, J // 2 + 1)
                            nc.vector.tensor_tensor(bT_lo[:, J // 2, :], A[:, 3, 0:S], f32(bT_hi[:, J // 2, :]),
                                                    ALU.subtract).then_inc(pair_lo_made, 1)

                    def head_rows_of(H):
                        K = head_index(H)
                        if K is None:
                            return
                        dve.wait_ge(rstd_made, J_HEAD + K + 1)
                        if K >= 1:
                            dve.wait_ge(head_turned, K)
                        for t in range(TT):
                            inv = rstd[:, J_HEAD + K, t:t + 1]
                            if K < DH:
                                if t == 0:
                                    dve.wait_ge(head_stats, K + 1)
                                ins = nc.vector.tensor_scalar(orow[:, t * P:(t + 1) * P], orow[:, t * P:(t + 1) * P], inv,
                                                              None, ALU.mult)
                            else:
                                r = K - DH
                                ins = nc.vector.scalar_tensor_tensor(
                                    orow[:, t * RDV:(t + 1) * RDV], A[:, 3, t * RDV:(t + 1) * RDV], inv,
                                    rg_rows[:, t, r * RDV:(r + 1) * RDV], ALU.mult, ALU.mult)
                        ins.then_inc(head_rows, 1)

                    def head_cols(H):
                        K = head_index(H)
                        if K is None:
                            return
                        dve.wait_ge(head_hi, K + 1)
                        if K < DH:
                            nc.vector.scalar_tensor_tensor(dT_lo[:, K, :], A[:, 0, 0:S], gl[:, G_SUB:G_SUB + 1],
                                                           f32(dT_hi[:, K, :]), ALU.mult, ALU.subtract).then_inc(head_lo, 1)
                        else:
                            r = K - DH
                            nc.vector.scalar_tensor_tensor(
                                bT_lo[:, 2 * r:2 * r + 2, :].rearrange("p k s -> p (k s)"), A[:, 0, :], 0.5,
                                f32(bT_hi[:, 2 * r:2 * r + 2, :]).rearrange("p k s -> p (k s)"),
                                ALU.mult, ALU.subtract).then_inc(head_lo, 1)

                    def attention_first(u):
                        s = u - U_DQ
                        if s >= 0 and s % 2 == 0:
                            logits_of(s // 2 - 1)
                            head_rows_of(s // 2 - 3)

                    def attention_then(u):
                        s = u - U_DQ
                        if s >= 0 and s % 2 == 0:
                            probs_of(s // 2 - 1)
                        if s >= 0 and s % 2 == 1:
                            pair_lo(s // 2 - 2)
                            head_cols(s // 2 - 3)

                    def evacuate(u):
                        for first, out in ((U_DQ, dqT), (U_DK, dkT)):
                            for half in range(2):
                                if u == first + 4 * half + 4:
                                    wait_group(first + 4 * half)
                                    nc.vector.tensor_copy(
                                        out[:, 4 * half:4 * half + 4, :].rearrange("p k s -> p (k s)"),
                                        G[:, group(first + 4 * half) % 2, :, :].rearrange("p a b -> p (a b)")
                                    ).then_inc(evacuated, 1)
                        for first, out in ((U_DV, dv_rows), (U_RV, rv_rows)):
                            for half in range(2):
                                if u == first + 4 * half + 4:
                                    wait_group(first + 4 * half)
                                    if first == U_RV:
                                        dve.wait_ge(mix_made, MH)
                                    nc.vector.tensor_copy(out[:, :, 512 * half:512 * half + 512],
                                                          G[:, group(first + 4 * half) % 2, :, :]).then_inc(evacuated, 1)
                        for half in range(2):
                            cols = slice(512 * half, 512 * half + 512)
                            if u == U_RG + 4 * half + 4:
                                first = U_RG + 4 * half
                                dve.wait_ge(tanh_made, tanh_index(first) + 1)
                                for t in range(TT):
                                    ins = nc.vector.scalar_tensor_tensor(rg_rows[:, t, cols], rg_rows[:, t, cols], 1.0,
                                                                         G[:, group(first) % 2, t, :], ALU.add, ALU.mult)
                                ins.then_inc(silu_made, 1)
                            for i, (first, gate, gate_first) in enumerate((
                                    (U_MLAO, tanh_g, U_G2), (U_DIFFO, tanh_g1, U_G1), (U_RETO, tanh_g, U_G0))):
                                if u == first + 4 * half + 4:
                                    at = first + 4 * half
                                    wait_group(at)
                                    dve.wait_ge(tanh_made, tanh_index(gate_first + 4 * half) + 1)
                                    out = merged if i == 0 else gate
                                    ins = nc.vector.scalar_tensor_tensor(out[:, :, cols], gate[:, :, cols], 1.0,
                                                                         G[:, group(at) % 2, :, :], ALU.add, ALU.mult)
                                    ins.then_inc(gated, 1)
                                    if i:
                                        dve.wait_ge(gated, 2 * i + half + 1)
                                        nc.vector.tensor_tensor(merged[:, :, cols], merged[:, :, cols],
                                                                gate[:, :, cols], ALU.add).then_inc(merged_made, 1)

                    def merged_cols(half):
                        dve.wait_ge(merged_hi, half + 1)
                        nc.vector.scalar_tensor_tensor(
                            hT_lo[:, 4 * half:4 * half + 4, :].rearrange("p k s -> p (k s)"),
                            A[:, 2 * half:2 * half + 2, :].rearrange("p a b -> p (a b)"), 0.5,
                            f32(hT_hi[:, 4 * half:4 * half + 4, :]).rearrange("p k s -> p (k s)"),
                            ALU.mult, ALU.subtract).then_inc(merged_lo, 1)

                    def hidden(u):
                        for j in range(8):
                            if u == U_UP[j] + 4:
                                dve.wait_ge(relu_made, j + 1)
                                if j >= 1:
                                    dve.wait_ge(hid_lo_made, j)
                                ins = nc.vector.tensor_tensor(
                                    square_h, G[:, group(U_UP[j]) % 2, :, :].rearrange("p a b -> p (a b)"), relu_h,
                                    ALU.mult)
                                ins.then_inc(square_made, 1)
                            if u == U_UP[j] + 5:
                                dve.wait_ge(hid_hi_made, j + 1)
                                nc.vector.tensor_tensor(hid_lo[:, j % 2, :, :].rearrange("p k s -> p (k s)"), square_h,
                                                        f32(hid_hi[:, j % 2, :, :]).rearrange("p k s -> p (k s)"),
                                                        ALU.subtract).then_inc(hid_lo_made, 1)

                    nc.vector.tensor_copy(gl[:, :], gains[:, l, :]).then_inc(gains_set, 1)
                    dve.wait_ge(gains_set, 1)
                    for t in range(TT):
                        for half in range(2):
                            pre_norm_rows(PRE_MIX, t, half)
                    split(0)
                    normed_lo(PRE_MIX, 0, 0)
                    split(1)
                    normed_lo(PRE_MIX, 0, 1)
                    normed_lo(PRE_MIX, 1, 0)
                    normed_lo(PRE_MIX, 1, 1)
                    for u in range(1, U_WOUT + 5):
                        attention_first(u)
                        split(u + 3)
                        before_mla(u)
                        attention_then(u)
                        evacuate(u)
                        if u == U_RETO + 6:
                            merged_cols(0)
                        if u == U_WOUT + 2:
                            merged_cols(1)
                    y = [[G[:, group(U_WOUT + 4 * half) % 2, t, :] for half in range(2)] for t in range(TT)]
                    dve.wait_ge(gain_rows_in, 16)
                    for half in range(2):
                        gained(POST_MIX, 0, half, y[0][half])
                    post_norm(POST_MIX, 0)
                    gained(POST_MIX, 1, 0, y[1][0])
                    for half in range(2):
                        pre_norm_rows(PRE_MLP, 0, half)
                    gained(POST_MIX, 1, 1, y[1][1])
                    post_norm(POST_MIX, 1)
                    normed_lo(PRE_MLP, 0, 0)
                    normed_lo(PRE_MLP, 0, 1)
                    pre_norm_rows(PRE_MLP, 1, 0)
                    split(U_UP[0])
                    normed_lo(PRE_MLP, 1, 0)
                    pre_norm_rows(PRE_MLP, 1, 1)
                    split(U_UP[0] + 1)
                    normed_lo(PRE_MLP, 1, 1)
                    split(U_UP[0] + 2)
                    for u in range(U_UP[0], NU):
                        if u + 3 < NU:
                            split(u + 3)
                        hidden(u)
                    for t in range(TT):
                        for half in range(2):
                            gained(POST_MLP, t, half, A[:, 2 * t + half, :])
                        post_norm(POST_MLP, t)

                @block.tensor
                def _(pe):
                    def three(out, stationary, moving, start, stop, check=False):
                        for i, (a, b) in enumerate(((0, 0), (0, 1), (1, 0))):
                            ins = nc.tensor.matmul(out, stationary[a], moving[b], start=start and i == 0,
                                                   stop=stop and i == 2, skip_group_check=check)
                        return ins

                    def tokens_stationary(u, first_tile, acts, outs, start, stop, tiles=range(TT)):
                        _, _, _, kt, n = UNITS[u]
                        pe.wait_ge(*lo_ready(u))
                        for kk in range(kt):
                            k = first_tile + kk
                            for t in tiles:
                                last = three(outs[t],
                                             (acts[0][:, k, t * P:(t + 1) * P], acts[1][:, k, t * P:(t + 1) * P]),
                                             (w_hi[:, u % SLOTS, kk * n:(kk + 1) * n],
                                              w_lo[:, u % SLOTS, kk * n:(kk + 1) * n]),
                                             start and kk == 0, stop and kk == kt - 1)
                        return last

                    def weights_stationary(u, first_tile, acts, out, start, stop):
                        pe.wait_ge(*lo_ready(u))
                        for c in range(4):
                            for kk in range(2):
                                k = first_tile + kk
                                at = kk * 512 + c * P
                                last = three(out[:, c, :],
                                             (w_hi[:, u % SLOTS, at:at + P], w_lo[:, u % SLOTS, at:at + P]),
                                             (acts[0][:, k, :], acts[1][:, k, :]),
                                             start and kk == 0 and c % 2 == 0, stop and kk == 1, check=True)
                        last.then_inc(unit_used, 1)

                    def take_pair(first):
                        n = group(first)
                        if n >= 2:
                            pe.wait_ge(*left_banks(n - 2))
                        return G[:, n % 2, :, :]

                    acts_h, acts_b, acts_d = (hT_hi, hT_lo), (bT_hi, bT_lo), (dT_hi, dT_lo)

                    def gemm(u):
                        if u < U_UKV or U_DQ <= u:
                            first, i = u - u % 4, u % 4
                        else:
                            first, i = u, 0
                        pair = take_pair(first) if u == first else G[:, group(first) % 2, :, :]
                        n = UNITS[u][4]
                        start, stop = u == first, u == first + GROUPS[first][0] - 1
                        if U_UKV <= u < U_UQ:
                            tokens_stationary(u, 2, acts_b, [pair[:, t, 0:n] for t in range(TT)], True, True
                                              ).then_inc(unit_used, 1)
                        elif U_UQ <= u < U_DQ:
                            tokens_stationary(u, 0, acts_b, [pair[:, t, 0:n] for t in range(TT)], True, True
                                              ).then_inc(unit_used, 1)
                        elif U_DQ <= u < U_DV or u >= U_UP[0]:
                            weights_stationary(u, 2 * i, acts_h,
                                               pair.rearrange("p t n -> p (t n)").rearrange("p (c s) -> p c s", c=4),
                                               start, stop)
                        else:
                            acts = acts_h
                            if U_MLAO <= u < U_RG or U_RETO <= u < U_WOUT:
                                acts = acts_b
                            if U_DIFFO <= u < U_RETO:
                                acts = acts_d
                            tokens_stationary(u, 2 * i, acts, [pair[:, t, 0:n] for t in range(TT)], start, stop
                                              ).then_inc(unit_used, 1)

                    def latents():
                        for t in range(TT):
                            for i in range(4):
                                u = U_LAT + i
                                pe.wait_ge(h_lo_made, normed_by(PRE_MIX, t, i // 2))
                                last = tokens_stationary(u, 2 * i, acts_h, [G[:, 0, tt, 0:LAT] for tt in range(TT)],
                                                         i == 0, i == 3, [t])
                                if t == 1:
                                    last.then_inc(unit_used, 1)

                    def mixers_out():
                        pairs = []
                        for i in range(4):
                            if i % 2 == 0:
                                pairs.append(take_pair(U_WOUT + 2 * i))
                            if i == 0:
                                pe.wait_ge(merged_lo, 1)
                            pair = pairs[i // 2]
                            tokens_stationary(U_WOUT + i, 2 * (i % 2), acts_h, [pair[:, t, :] for t in range(TT)],
                                              i % 2 == 0, False).then_inc(unit_used, 1)
                            if i == 1:
                                turn_merged(1)
                        pe.wait_ge(merged_lo, 2)
                        for t in range(TT):
                            for i in range(4):
                                pair = pairs[i // 2]
                                last = tokens_stationary(U_WOUT + 4 + i, 4 + 2 * (i % 2), acts_h,
                                                         [pair[:, tt, :] for tt in range(TT)], False, i % 2 == 1, [t])
                                if t == 1:
                                    last.then_inc(unit_used, 1)
                                elif i % 2:
                                    last.then_inc(y_tile0, 1)

                    def norm_turn(norm, t, b):
                        pe.wait_ge(xn_made, normed_by(norm, t, b))
                        for k in range(4):
                            last = nc.tensor.transpose(A[:, 2 * t + b, k * P:(k + 1) * P],
                                                       xn[:, t, (4 * b + k) * P:(4 * b + k + 1) * P], ident)
                        last.then_inc(xn_turned, 1)

                    def before_mla(u):
                        if u == U_LAT + 7:
                            pe.wait_ge(lat_rows_made, 1)
                            for k in range(3):
                                for t in range(TT):
                                    last = nc.tensor.transpose(
                                        A[:, k // 2, (k % 2) * S + t * P:(k % 2) * S + (t + 1) * P],
                                        lat[:, t, k * P:(k + 1) * P], ident)
                            last.then_inc(lat_turned, 1)
                        for i, at in enumerate((U_RQ + 7, U_RK + 8)):
                            if u == at:
                                pe.wait_ge(r_rows_made, i + 1)
                                if i:
                                    pe.wait_ge(r_cols_made, 1)
                                for h in range(RH):
                                    for t in range(TT):
                                        last = nc.tensor.transpose(
                                            A[:, 2 + h // 2, (h % 2) * S + t * P:(h % 2) * S + (t + 1) * P],
                                            r_rows[:, t, h, :], ident)
                                last.then_inc(r_turned, 1)

                    def turn_qk(h):
                        if h >= MH:
                            return
                        if h == 0:
                            pe.wait_ge(kpe_spread, TT)
                            pe.wait_ge(kv_rows_made, 4)
                        else:
                            pe.wait_ge(qk_cols_made, h)
                        pe.wait_ge(q_rows_made, h // 4 + 1)
                        for i, rows in enumerate((q_rows, k_rows)):
                            for t in range(TT):
                                last = nc.tensor.transpose(A[0:MQ, 0, i * S + t * P:i * S + (t + 1) * P],
                                                           rows[:, t, h, :], ident)
                        last.then_inc(qk_turned, 1)

                    def scores(H):
                        if not 0 <= H < N_HEADS:
                            return
                        if H >= 1:
                            pe.wait_ge(logits_made, H)
                        out = A[:, 1, :]
                        if H < MH:
                            pe.wait_ge(qk_cols_made, H + 1)
                            nc.tensor.matmul(out[:, 0:P], qkT[:, 0:P], qkT[:, S:S + P], start=True, stop=True)
                            last = nc.tensor.matmul(out[:, P:384], qkT[:, P:S], qkT[:, S:2 * S], start=True, stop=True)
                        elif H < MH + 2 * DH:
                            h, c = (H - MH) // 2, (H - MH) % 2
                            if H == MH:
                                pe.wait_ge(evacuated, 4)
                            q, k = dqT[c * DD:(c + 1) * DD, h, :], dkT[c * DD:(c + 1) * DD, h, :]
                            nc.tensor.matmul(out[:, 0:P], q[:, 0:P], k[:, 0:P], start=True, stop=True)
                            last = nc.tensor.matmul(out[:, P:384], q[:, P:S], k, start=True, stop=True)
                        else:
                            r = H - MH - 2 * DH
                            nc.tensor.matmul(out[:, 0:S], rkT[:, r, 0:P], rqT[:, r, :], start=True, stop=True)
                            last = nc.tensor.matmul(out[:, S:384], rkT[:, r, P:S], rqT[:, r, P:S], start=True, stop=True)
                        last.then_inc(scores_made, 1)

                    def turn_probs(H):
                        J = mix_index(H)
                        if J is None or J >= MH + DH:
                            return
                        pe.wait_ge(probs_made, J + 1)
                        if J >= 1:
                            pe.wait_ge(probsT_made, J)
                        else:
                            pe.wait_ge(r_cols_made, 2)
                        b = J % 2 if J < MH else 0
                        for i in range(3):
                            last = nc.tensor.transpose(A[:, 2, i * P:(i + 1) * P], probs[:, b, i * P:(i + 1) * P], ident)
                        last.then_inc(probs_turned, 1)

                    def mix(H):
                        J = mix_index(H)
                        if J is None:
                            return
                        out = A[:, 3, :]
                        if J < MH + DH:
                            pe.wait_ge(probsT_made, J + 1)
                        if J < MH:
                            if J % 2 == 0 and J >= 2:
                                pe.wait_ge(pair_lo_made, J // 2)
                            row = MV * (J % 2)
                            nc.tensor.matmul(out[row:row + MV, 0:S], v_rows[:, 0, J, :], probsT[:, 0:S], start=True,
                                             stop=False)
                            last = nc.tensor.matmul(out[row:row + MV, P:S], v_rows[:, 1, J, :], probsT[:, S:384],
                                                    start=False, stop=True)
                        elif J < MH + DH:
                            k = J - MH
                            if k == 0:
                                pe.wait_ge(pair_lo_made, MH // 2)
                                pe.wait_ge(evacuated, 6)
                            else:
                                pe.wait_ge(head_stats, k)
                            v0, v1 = dv_rows[:, 0, k * P:(k + 1) * P], dv_rows[:, 1, k * P:(k + 1) * P]
                            nc.tensor.matmul(out[:, 0:P], probsT[:, 0:P], v0, start=True, stop=True)
                            nc.tensor.matmul(out[:, P:S], probsT[:, P:S], v0, start=True, stop=False)
                            last = nc.tensor.matmul(out[:, P:S], probsT[:, S:384], v1, start=False, stop=True)
                        else:
                            r = J - MH - DH
                            pe.wait_ge(logits_made, H + 1)
                            if r == 0:
                                pe.wait_ge(head_stats, DH)
                                pe.wait_ge(evacuated, 8)
                            else:
                                pe.wait_ge(head_rows, DH + r)
                            w = logits[:, H % 2, :]
                            v0, v1 = rv_rows[:, 0, r * RDV:(r + 1) * RDV], rv_rows[:, 1, r * RDV:(r + 1) * RDV]
                            nc.tensor.matmul(out[:, 0:RDV], w[:, 0:P], v0, start=True, stop=True)
                            nc.tensor.matmul(out[:, RDV:2 * RDV], w[:, P:S], v0, start=True, stop=False)
                            last = nc.tensor.matmul(out[:, RDV:2 * RDV], w[:, S:384], v1, start=False, stop=True)
                        last.then_inc(mix_made, 1)

                    def turn_head(H):
                        K = head_index(H)
                        if K is None:
                            return
                        pe.wait_ge(head_rows, K + 1)
                        if K == 0:
                            pe.wait_ge(qk_cols_made, MH)
                        else:
                            pe.wait_ge(head_lo, K)
                        if K < DH:
                            for t in range(TT):
                                last = nc.tensor.transpose(A[:, 0, t * P:(t + 1) * P], orow[:, t * P:(t + 1) * P], ident)
                        else:
                            for f in range(RDV // P):
                                for t in range(TT):
                                    last = nc.tensor.transpose(A[:, 0, f * S + t * P:f * S + (t + 1) * P],
                                                               orow[:, t * RDV + f * P:t * RDV + (f + 1) * P], ident)
                        last.then_inc(head_turned, 1)

                    def attention(u):
                        s = u - U_DQ
                        if s < 0:
                            return
                        m = s // 2
                        if s % 2 == 0:
                            turn_qk(m)
                            mix(m - 2)
                            turn_head(m - 3)
                        else:
                            scores(m)
                            turn_probs(m - 1)

                    def turn_merged(half):
                        pe.wait_ge(merged_made, 2 + half + 1)
                        if half == 0:
                            pe.wait_ge(head_lo, DH + RH)
                        for k in range(4):
                            for t in range(TT):
                                at = (k % 2) * S + t * P
                                last = nc.tensor.transpose(A[:, 2 * half + k // 2, at:at + P],
                                                           merged[:, t, 512 * half + k * P:512 * half + (k + 1) * P],
                                                           ident)
                        last.then_inc(merged_turned, 1)

                    def down(j, u, i, tiles=range(TT)):
                        half, pair = i // 2, i % 2
                        return tokens_stationary(u, 2 * pair, (hid_hi[:, j % 2, :, :], hid_lo[:, j % 2, :, :]),
                                                 [A[:, 2 * t + half, :] for t in range(TT)], j == 0 and pair == 0,
                                                 j == 7 and pair == 1, tiles)

                    pe.wait_ge(consts_in, 16)
                    for t in range(TT):
                        for b in range(2):
                            norm_turn(PRE_MIX, t, b)
                    latents()
                    for u in range(U_LAT, U_WOUT):
                        if u == U_UKV:
                            pe.wait_ge(lat_lo_made, 3)
                        if u == U_MLAO:
                            pe.wait_ge(pair_lo_made, MH // 2)
                        if u == U_DIFFO:
                            pe.wait_ge(head_lo, DH)
                        if u == U_RETO:
                            pe.wait_ge(head_lo, DH + RH)
                        if u >= U_RQ:
                            gemm(u)
                        before_mla(u)
                        attention(u)
                        if u == U_RETO + 5:
                            turn_merged(0)
                    mixers_out()
                    for t in range(TT):
                        for b in range(2 - t):
                            norm_turn(PRE_MLP, t, b)
                    for j in range(9):
                        if j < 8:
                            for i in range(4):
                                if j == 0 and i == 1:
                                    norm_turn(PRE_MLP, 1, 1)
                                if j == 0:
                                    pe.wait_ge(h_lo_made, normed_by(PRE_MLP, 1, i // 2))
                                gemm(U_UP[j] + i)
                        if j >= 1:
                            pe.wait_ge(hid_lo_made, j)
                        if 1 <= j < 8:
                            for i in range(4):
                                down(j - 1, U_DN[j - 1] + i, i).then_inc(unit_used, 1)
                    for t in range(TT):
                        for i in range(4):
                            last = down(7, U_DN[7] + i, i, [t])
                            if t == 1:
                                last.then_inc(unit_used, 1)
                            elif i % 2:
                                last.then_inc(y_tile0, 1)

        with nc.Fori(0, L) as l:
            layer(l)
            nc.multi_engine_barrier([ENG.PE, ENG.Activation, ENG.DVE, ENG.Pool, ENG.SP],
                                    sems_to_clear=range(first_sem[0].num, last_sem.num + 1))

        out_stored = sem("out_stored")
        with nc.Block() as block:
            @block.sync
            def _(sp):
                sp.dma_start(io["out"][0].rearrange("(t p) d -> p t d", p=P), x[:, :, :]).then_inc(out_stored, 16)
                sp.wait_ge(out_stored, 16)


def shape_constants():
    f = np.float32
    packed, decays = np.zeros((P, K_END), f), np.zeros((P, RH, 384), f)
    p, k = np.arange(P)[:, None], np.arange(P)[None, :]
    packed[:, K_ID:K_ID + P] = np.eye(P, dtype=f)
    packed[:, K_MASK + P:K_MASK + S] = np.where(p >= k, 0.0, NEG)
    log_g = np.log1p(-np.exp2(-5.0 - np.arange(RH, dtype=np.float64)))
    for h in range(RH):
        rel = np.arange(S)[None, :] - p
        wide = np.where(rel >= 0, np.exp(np.maximum(rel, 0) * log_g[h]), 0.0) * RDK ** -0.5
        decays[:, h, :] = np.concatenate([wide, wide[:, 0:P]], axis=1)

    def rotations(at_cos, at_sin, inv_freq, width):
        pos = np.arange(S, dtype=f)
        angle = (pos[:, None] * inv_freq.astype(f)[None, :]).astype(np.float64)
        cos, sin = np.cos(angle), np.sin(angle)
        for t in range(TT):
            rows = slice(t * P, (t + 1) * P)
            packed[:, at_cos + t * width:at_cos + (t + 1) * width] = np.concatenate([cos[rows], cos[rows]], axis=1)
            packed[:, at_sin + t * width:at_sin + (t + 1) * width] = np.concatenate([-sin[rows], sin[rows]], axis=1)

    rotations(K_RC, K_RS, 1.0 / (10000.0 ** np.linspace(0.0, 1.0, RDK // 2)), RDK)
    rotations(K_MC, K_MS, 1.0 / (10000.0 ** (np.arange(0, MR, 2) / MR)), MR)


    dist = S - 1 - np.arange(LINE)
    exact = BUCKETS // 2
    far = exact + (np.log(np.maximum(dist, 1).astype(f) / f(exact)) / f(np.log(MAX_DIST / exact))
                   * f(BUCKETS - exact)).astype(np.int32)
    bucket = np.where(dist < exact, np.maximum(dist, 0), np.minimum(far, BUCKETS - 1))
    onehot = np.zeros((BUCKETS + 1, LINE), f)
    onehot[bucket, np.arange(LINE)] = dist >= 0
    onehot[BUCKETS] = dist < 0
    return {"consts": packed, "onehot": onehot, "decay": decays}


def lay_out(inputs):
    vec = {name: np.asarray(inputs[name]) for name in _SMALL}
    init = [[lambda_init(l), 1.0 - lambda_init(l)] for l in range(L)]
    cols = [vec[name].reshape(L, -1, P) for name in ("mla_q_norm_g", "mla_kv_norm_g", "diff_subln_g")]
    cols.append(np.zeros((L, 1, P), np.float32))
    cols.append(np.broadcast_to(np.array(init, np.float32)[:, :, None], (L, 2, P)))
    gains = np.ascontiguousarray(np.concatenate(cols, axis=1).transpose(2, 0, 1))
    lambdas = np.ascontiguousarray(np.stack([vec[f"lambda_{n}"] for n in ("q1", "k1", "q2", "k2")], axis=1
                                            ).reshape(4 * L, DD).T)
    next_pre_mix = np.concatenate([vec["pre_mix_g"][1:], vec["pre_mix_g"][:1]])
    gain_rows = np.ascontiguousarray(np.stack([vec["post_mix_g"], vec["post_mlp_g"], vec["pre_mlp_g"], next_pre_mix],
                                              axis=1).reshape(L, 4 * DM))
    return {"gains": gains, "lambdas": lambdas, "gain_rows": gain_rows}


_INS = ["x", "rel_bias", "w_in", "w_ret_o", "w_diff_o", "w_mla_uq", "w_mla_ukv", "w_mla_o", "w_out", "w_up", "w_down"]
_SMALL = ["pre_mix_g", "post_mix_g", "pre_mlp_g", "post_mlp_g", "mla_q_norm_g", "mla_kv_norm_g", "diff_subln_g",
          "lambda_q1", "lambda_k1", "lambda_q2", "lambda_k2"]


def kernel(**inputs):
    import concourse.bacc as bacc
    from concourse.bass_utils import run_bass_kernel_spmd

    nc = bacc.Bacc("TRN2", target_bir_lowering=False, num_devices=1)


    arrays, io = {}, {}
    for name, a in [(n, np.ascontiguousarray(inputs[n])) for n in _INS] + list(shape_constants().items()) + list(
            lay_out(inputs).items()):
        arrays[f"in_{name}"] = a
        io[name] = nc.dram_tensor(f"in_{name}", a.shape, mybir.dt.from_np(a.dtype), kind="ExternalInput").ap()
    io["line"] = nc.dram_tensor("line", (COPIES, DH, LINE), F32, kind="Internal").ap()
    io["out"] = nc.dram_tensor("out", (1, S, DM), F32, kind="ExternalOutput").ap()
    build(nc, io)
    r = run_bass_kernel_spmd(nc, [arrays], core_ids=[0])
    return r.results[0]["out"]
```

```python
import math
from contextlib import ExitStack

import numpy as np

import concourse.bass as bass
from concourse import mybir

F32 = mybir.dt.float32
F32R = mybir.dt.float32r
ALU = mybir.AluOpType
ACT = mybir.ActivationFunctionType
ENG = mybir.EngineType

P = 128
L, S, DM = 2, 256, 1024
TT = S // P
KD = DM // P
EPS = 1e-6
RH, RDK, RDV = 4, 128, 256
DH, DD = 8, 64
MH, MN, MR, MV = 16, 64, 32, 64
MQ = MN + MR
QL, KVL = 256, 128
LAT = QL + KVL + MR
NEG = -1e30
BIG = 3e38
BUCKETS, MAX_DIST = 32, 128
LINE = 384
COPIES = 32

C_RQ, C_RK, C_RV, C_RG = 0, 512, 1024, 2048
C_DQ, C_DK, C_DV, C_LAT = 3072, 4096, 5120, 6144
C_G0, C_G1, C_G2 = 6560, 7584, 8608

K_ID = 0
K_MASK = K_ID + P
K_RC = K_MASK + S
K_RS = K_RC + TT * RDK
K_MC = K_RS + TT * RDK
K_MS = K_MC + TT * MR
K_END = K_MS + TT * MR

G_Q, G_KV, G_SUB, G_LAM, G_INIT, G_LESS, G_N = 0, 2, 3, 4, 5, 6, 7


def lambda_init(l):
    return 0.8 - 0.6 * math.exp(-0.3 * l)


def weight_units():
    units = []

    def rows(name, col, n):
        units.extend((name, 2 * P * i, col, 2, n) for i in range(4))

    rows("w_in", C_LAT, LAT)
    rows("w_in", C_RQ, 512)
    rows("w_in", C_RK, 512)
    units.extend(("w_mla_ukv", 0, 512 * m, 1, 512) for m in range(4))
    units.extend(("w_mla_uq", 0, 512 * m, 2, 512) for m in range(2))
    units.extend(("w_mla_uq", P * k, MH * MN, 1, MH * MR) for k in range(2))
    for name, col in (("w_in", C_DQ), ("w_in", C_DK), ("w_in", C_DV), ("w_in", C_G2), ("w_in", C_RV),
                      ("w_mla_o", 0), ("w_in", C_RG), ("w_in", C_G1), ("w_in", C_G0), ("w_diff_o", 0),
                      ("w_ret_o", 0)):
        rows(name, col, 512)
        rows(name, col + 512, 512)
    for rows_half in range(2):
        for cols_half in range(2):
            units.extend(("w_out", 2 * P * (2 * rows_half + i), 512 * cols_half, 2, 512) for i in range(2))

    def up(j):
        rows("w_up", 512 * j, 512)

    def down(j):
        units.extend(("w_down", 512 * j + 2 * P * (i % 2), 512 * (i // 2), 2, 512) for i in range(4))

    up(0)
    for j in range(1, 8):
        up(j)
        down(j - 1)
    down(7)
    return units


UNITS = weight_units()
NU = len(UNITS)
SLOTS = 4
U_LAT, U_RQ, U_RK, U_UK, U_UV, U_UQ, U_UQR = 0, 4, 8, 12, 14, 16, 18
U_DQ, U_DK, U_DV, U_G2, U_RV, U_MLAO, U_RG, U_G1, U_G0, U_DIFFO, U_RETO, U_WOUT = range(20, 116, 8)
U_UP = [116] + [120 + 8 * (j - 1) for j in range(1, 8)]
U_DN = [124 + 8 * j for j in range(7)] + [176]
POOL_UNITS = (2, U_UQ, U_UP[0] + 1)
ATTENTION = U_DQ + 2
assert NU == 180

GROUPS = {}


def _groups():
    n = 0
    for first, units in [(U_LAT, 4), (U_RQ, 4), (U_RK, 4)] + [(u, 1) for u in range(U_UK, U_UQR)] + [(U_UQR, 2)] + \
            [(u, 4) for u in range(U_DQ, U_UP[0], 4)] + [(u, 4) for u in U_UP]:
        GROUPS[first] = (units, n)
        n += 1


_groups()


def group(first):
    return GROUPS[first][1]


J_LAT = 0
J_HEAD = 1
N_JOBS = 13

PRE_MIX, POST_MIX, PRE_MLP, POST_MLP = range(4)
SUMS = [(PRE_MIX, 0, 0), (PRE_MIX, 0, 1), (PRE_MIX, 1, 0), (PRE_MIX, 1, 1), (POST_MIX, 0, 0), (POST_MIX, 0, 1),
        (PRE_MLP, 0, 0), (PRE_MLP, 0, 1), (POST_MIX, 1, 0), (POST_MIX, 1, 1), (PRE_MLP, 1, 0), (PRE_MLP, 1, 1),
        (POST_MLP, 0, 0), (POST_MLP, 0, 1), (POST_MLP, 1, 0), (POST_MLP, 1, 1)]
ROOT_DM = 32.0
assert ROOT_DM ** 2 == DM
R_POST_MIX, R_POST_MLP, R_PRE_MLP, R_NEXT_PRE_MIX = range(4)


def sums_by(norm, t, half):
    return SUMS.index((norm, t, half)) + 1


def inv_by(norm, t):
    return [s[:2] for s in SUMS if s[2]].index((norm, t)) + 1


def normed_by(norm, t, b):
    return 4 * (norm == PRE_MLP) + 2 * t + b + 1


def x_halves_by(norm, t, half):
    return 4 * (norm == POST_MLP) + 2 * t + half + 1


N_HEADS = MH + 2 * DH + RH


def mix_index(H):
    if H < 0 or H >= N_HEADS:
        return None
    if H < MH:
        return H
    if H < MH + 2 * DH:
        return MH + (H - MH) // 2 if H % 2 else None
    return MH + DH + H - MH - 2 * DH


def head_index(H):
    j = mix_index(H)
    return None if j is None or j < MH else j - MH


def build(nc, io):
    with ExitStack() as ctx:
        def sb(name, shape, dt=F32):
            return ctx.enter_context(nc.sbuf_tensor(name, shape, dt))

        def sem(name):
            return ctx.enter_context(nc.semaphore(name))

        raw = sb("raw", [P, SLOTS, 1024])
        w_hi = sb("w_hi", [P, SLOTS, 1024], F32R)
        w_lo = sb("w_lo", [P, SLOTS, 1024], F32R)
        x = sb("x", [P, TT, DM])
        const = sb("const", [P, K_END])
        bias = sb("bias", [P, DH, S])
        decay = sb("decay", [P, RH, 384])
        hT_hi = sb("hT_hi", [P, KD, S], F32R)
        hT_lo = sb("hT_lo", [P, KD, S], F32R)
        bT_hi = sb("bT_hi", [P, KD, S], F32R)
        bT_lo = sb("bT_lo", [P, KD, S], F32R)
        dT_hi = sb("dT_hi", [P, KD, S], F32R)
        dT_lo = sb("dT_lo", [P, KD, S], F32R)
        area_d = sb("area_d", [P, 8192])
        area_e = sb("area_e", [P, 6144])
        area_g = sb("area_g", [P, 2048])
        area_r = sb("area_r", [P, 2, 1024])
        qkT = sb("qkT", [MQ, 2 * S])
        logits = sb("logits", [P, 2, 384])
        probs = sb("probs", [P, 2, 384])
        probsT = sb("probsT", [P, 384])
        orow = sb("orow", [P, 512])
        junk = sb("junk", [P, 512], mybir.dt.bfloat16)
        gains = sb("gains", [P, L, G_N])
        gl = sb("gl", [P, G_N])
        negmax = sb("negmax", [P, 2, 2])
        rowsum = sb("rowsum", [P, 2, 2])
        rrow_sum = sb("rrow_sum", [P, 2, 2, 2])
        negr = sb("negr", [P, 2])
        ss = sb("ss", [P, N_JOBS, 4])
        rstd = sb("rstd", [P, N_JOBS, 4])
        sums = sb("sums", [P, 4, TT, 4])
        inv = sb("inv", [P, 4, TT])
        neghalf = sb("neghalf", [P, 4])
        lam = sb("lam", [P, 8])

        def view(area, first, shape):
            n = int(np.prod(shape))
            flat = area[:, first:first + n]
            names = "abcd"[:len(shape)]
            return flat.rearrange(f"p ({' '.join(names)}) -> p {' '.join(names)}", **dict(zip(names, shape)))

        qkT_own = view(area_d, 0, (MH // 2, 2, S))
        q_ropeT = view(area_d, 4096, (MH // 4, S))
        v_rows = view(area_d, 6144, (TT, MH, MV))
        rv_rows = view(area_d, 0, (TT, DM))
        rg_rows = view(area_d, 2048, (TT, DM))
        merged = view(area_d, 4096, (TT, DM))
        tanh_g1 = view(area_d, 6144, (TT, DM))
        dqT = view(area_e, 0, (DH, S))
        dkT = view(area_e, 2048, (DH, S))
        dv_rows = view(area_e, 4096, (TT, DM))
        lat = view(area_e, 0, (TT, LAT))
        r_rows = view(area_e, 1024, (TT, RH, RDK))
        r_tmp = view(area_e, 2048, (TT, RH, RDK))
        kpe_tmp = view(area_e, 3072, (TT, 2 * MR))
        r_src = view(area_e, 4096, (TT, RH, RDK))
        q_rope_rows = view(area_e, 1024, (TT, MH, MR))
        q_rope_tmp = view(area_e, 2048, (TT, MH, MR))
        q_rope_src = view(area_e, 4096, (TT, MH, MR))
        gain_rows = view(area_e, 2048, (4, DM))
        tanh_g = view(area_g, 0, (TT, DM))
        xn = view(area_g, 0, (TT, DM))
        rqT = area_r[:, 0, :].rearrange("p (h s) -> p h s", h=RH)
        rkT = area_r[:, 1, :].rearrange("p (h s) -> p h s", h=RH)
        relu_h = area_r[:, 0, :]
        square_h = area_r[:, 1, :]
        norm_junk = area_r[:, :, :]
        lat_junk = view(area_g, 0, (TT, QL + KVL))
        hid_hi = dT_hi[:, :, :].rearrange("p (b k) s -> p b k s", b=2)
        hid_lo = dT_lo[:, :, :].rearrange("p (b k) s -> p b k s", b=2)

        ident = const[:, K_ID:K_ID + P]
        mask = const[:, K_MASK:K_MASK + S]

        r_cos = const[:, K_RC:K_RC + TT * RDK].rearrange("p (t n) -> p t n", t=TT)
        r_sin = const[:, K_RS:K_RS + TT * RDK].rearrange("p (t n) -> p t n", t=TT)
        m_cos = const[:, K_MC:K_MC + TT * MR].rearrange("p (t n) -> p t n", t=TT)
        m_sin = const[:, K_MS:K_MS + TT * MR].rearrange("p (t n) -> p t n", t=TT)


        G = ctx.enter_context(nc.psum_tensor("G", [P, 2, TT, 512], F32))
        A = ctx.enter_context(nc.psum_tensor("A", [P, 4, 512], F32))

        def f32(ap):
            return ap.bitcast(F32)

        rows_in = sem("rows_in")
        x_in = [sem(f"x_in{t}") for t in range(TT)]
        consts_in = sem("consts_in")
        small_in = sem("small_in")
        pool_set = sem("pool_set")
        lines_made = sem("lines_made")
        line_ready = sem("line_ready")
        line_out = sem("line_out")
        lam_step = sem("lam_step")
        lambdas_in = sem("lambdas_in")
        first_gain_in = sem("first_gain_in")
        lam_dots = sem("lam_dots")
        lam_exp = sem("lam_exp")

        lam_vec = area_d[0:DD, 0:4 * L].rearrange("p (l i) -> p l i", l=L)
        lam_prod = area_d[0:DD, 64:64 + 2 * L]
        ones = area_d[0:DD, 128:128 + P]
        rel_in = area_d[0:BUCKETS + 1, 5000:5000 + DH]
        onehot = area_d[0:BUCKETS + 1, 5120:5120 + LINE]
        line_sb = area_d[0:DH, 6000:6000 + LINE]

        with nc.Block() as block:
            @block.sync
            def _(sp):
                sp.dma_start(onehot, io["onehot"]).then_inc(rows_in, 16)
                for t in range(TT):
                    sp.dma_start(x[:, t, :], io["x"][0, t * P:(t + 1) * P, :]).then_inc(x_in[t], 16)

                sp.dma_start(gain_rows[:, R_NEXT_PRE_MIX, :],
                             io["gain_rows"][L - 1:L, R_NEXT_PRE_MIX * DM:].broadcast_to([P, DM])
                             ).then_inc(first_gain_in, 16)
                sp.dma_start(const[:, :], io["consts"]).then_inc(consts_in, 16)
                sp.wait_ge(line_ready, 1)
                sp.dma_start(io["line"].rearrange("r h n -> h r n"),
                             line_sb.rearrange("h (r n) -> h r n", r=1).broadcast_to([DH, COPIES, LINE])
                             ).then_inc(line_out, 16)


            @block.gpsimd
            def _(pool):
                pool.dma_start(gains[:, :, :], io["gains"]).then_inc(small_in, 16)
                nc.gpsimd.memset(neghalf[:, :], -0.5).then_inc(pool_set, 1)
                pool.wait_ge(pool_set, 1)
                nc.gpsimd.memset(area_d[BUCKETS:BUCKETS + 1, 5000:5000 + DH], NEG).then_inc(pool_set, 1)
                pool.wait_ge(pool_set, 2)
                nc.gpsimd.memset(ones, 1.0).then_inc(pool_set, 1)

            @block.scalar
            def _(act):
                act.dma_start(area_d[0:BUCKETS, 5000:5000 + DH], io["rel_bias"]).then_inc(rows_in, 16)
                act.dma_start(area_d[0:DD, 0:4 * L], io["lambdas"]).then_inc(lambdas_in, 16)
                act.wait_ge(pool_set, 1)
                nc.scalar.activation(lam[:, 4:8], neghalf[:, :], ACT.Exp).then_inc(lam_exp, 1)
                act.wait_ge(lines_made, 1)
                nc.scalar.activation(line_sb, A[0:DH, 0, 0:LINE], ACT.Copy, scale=8.0).then_inc(line_ready, 1)
                act.wait_ge(lam_dots, 1)
                nc.scalar.activation(lam[:, 0:2 * L], A[:, 1, 0:2 * L], ACT.Exp).then_inc(lam_exp, 1)

            @block.tensor
            def _(pe):
                pe.wait_ge(rows_in, 32)
                pe.wait_ge(pool_set, 2)
                nc.tensor.matmul(A[0:DH, 0, 0:LINE], rel_in, onehot, start=True, stop=True).then_inc(lines_made, 1)
                pe.wait_ge(lam_step, L)
                pe.wait_ge(pool_set, 3)
                nc.tensor.matmul(A[:, 1, 0:2 * L], ones, lam_prod, start=True, stop=True).then_inc(lam_dots, 1)

            @block.vector
            def _(dve):
                dve.wait_ge(lambdas_in, 16)
                for l in range(L):
                    nc.vector.tensor_tensor(lam_prod[:, 2 * l:2 * l + 2], lam_vec[:, l, 0:4:2], lam_vec[:, l, 1:4:2],
                                            ALU.mult).then_inc(lam_step, 1)
                dve.wait_ge(small_in, 16)
                dve.wait_ge(lam_exp, 2)
                for l in range(L):
                    nc.vector.scalar_tensor_tensor(gains[:, l, G_LAM:G_LAM + 1], lam[:, 2 * l + 1:2 * l + 2],
                                                   lam[:, 2 * l:2 * l + 1], gains[:, l, G_INIT:G_INIT + 1],
                                                   ALU.subtract, ALU.subtract).then_inc(lam_step, 1)
                    nc.vector.tensor_tensor(gains[:, l, G_SUB:G_SUB + 1], gains[:, l, G_SUB:G_SUB + 1],
                                            gains[:, l, G_LESS:G_LESS + 1], ALU.mult).then_inc(lam_step, 1)

        first_sem = raw_in = [sem(f"raw_in{i}") for i in range(SLOTS)]
        hi_made = sem("hi_made")
        lo_made = sem("lo_made")
        pool_lo_made = sem("pool_lo_made")
        unit_used = sem("unit_used")
        gains_set = sem("gains_set")
        sums_made = sem("sums_made")
        inv_made = sem("inv_made")
        tables_in = sem("tables_in")
        y_tile0 = sem("y_tile0")
        y_read = sem("y_read")
        stats_made = sem("stats_made")
        rstd_made = sem("rstd_made")
        pool_step = sem("pool_step")
        dve_step = sem("dve_step")
        xn_made = sem("xn_made")
        xn_turned = sem("xn_turned")
        h_hi_made = sem("h_hi_made")
        h_lo_made = sem("h_lo_made")
        x_made = sem("x_made")
        lat_copied = sem("lat_copied")
        silu_made = sem("silu_made")
        gated = sem("gated")
        lat_rows_made = sem("lat_rows_made")
        lat_turned = sem("lat_turned")
        lat_hi_made = sem("lat_hi_made")
        lat_lo_made = sem("lat_lo_made")
        kpe_made = sem("kpe_made")

        r_rows_made = sem("r_rows_made")
        r_copied = sem("r_copied")
        r_turned = sem("r_turned")
        r_cols_made = sem("r_cols_made")
        mla_copied = sem("mla_copied")
        q_rope_made = sem("q_rope_made")
        q_rope_turned = sem("q_rope_turned")
        q_rope_cols = sem("q_rope_cols")
        k_rope_cols = sem("k_rope_cols")



        qk_cols_made = sem("qk_cols_made")
        scores_made = sem("scores_made")
        logits_made = sem("logits_made")
        exp_made = sem("exp_made")
        probs_made = sem("probs_made")
        probs_turned = sem("probs_turned")
        probsT_made = sem("probsT_made")
        mix_made = sem("mix_made")
        pair_hi_made = sem("pair_hi_made")
        pair_lo_made = sem("pair_lo_made")
        head_stats = sem("head_stats")
        head_rows = sem("head_rows")
        head_turned = sem("head_turned")
        head_hi = sem("head_hi")
        head_lo = sem("head_lo")
        tanh_made = sem("tanh_made")
        evacuated = sem("evacuated")
        merged_made = sem("merged_made")
        merged_turned = sem("merged_turned")
        merged_hi = sem("merged_hi")
        merged_lo = sem("merged_lo")
        gain_rows_in = sem("gain_rows_in")
        relu_made = sem("relu_made")
        square_made = sem("square_made")
        hid_turned = sem("hid_turned")
        hid_hi_made = sem("hid_hi_made")
        hid_lo_made = last_sem = sem("hid_lo_made")

        def tanh_index(first):
            order = [U_G2, U_G2 + 4, U_RG, U_RG + 4, U_G1, U_G1 + 4, U_G0, U_G0 + 4]
            return order.index(first)

        def left_banks(n):
            first = next(f for f, (_, g) in GROUPS.items() if g == n)
            half = first % 8 // 4 ^ (U_DQ % 8 // 4)
            if first == U_LAT:
                return lat_copied, 1
            if first in (U_RQ, U_RK):
                return r_copied, 1 + (first == U_RK)
            if U_UK <= first < U_DQ:
                return mla_copied, first - U_UK + 1
            for i, base in enumerate((U_DQ, U_DK, U_DV, U_RV)):
                if base <= first < base + 8:
                    return evacuated, 2 * i + half + 1
            if U_RG <= first < U_RG + 8:
                return silu_made, half + 1
            for base in (U_G2, U_G1, U_G0):
                if base <= first < base + 8:
                    return tanh_made, tanh_index(first) + 1
            for i, base in enumerate((U_MLAO, U_DIFFO, U_RETO)):
                if base <= first < base + 8:
                    return gated, 2 * i + half + 1
            if U_WOUT <= first < U_WOUT + 8:
                return y_read, 2 * (TT - 1) + half + 1
            return square_made, U_UP.index(first) + 1

        def lo_ready(u):
            by_pool = sum(p <= u for p in POOL_UNITS)
            return (pool_lo_made, by_pool) if u in POOL_UNITS else (lo_made, u + 1 - by_pool)

        def layer(l):
            with nc.Block() as block:
                @block.sync
                def _(sp):
                    for u, (name, row, col, kt, n) in enumerate(UNITS):
                        if u >= SLOTS:
                            sp.wait_ge(*lo_ready(u - SLOTS))
                        for first in range(0, P, COPIES):
                            if u == U_DQ + 2 + first // COPIES * 4:
                                sp.wait_ge(line_out, 16)
                                shifted = bass.AP(io["line"].tensor, P - 1 - first,
                                                  [[DH * LINE - 1, COPIES], [LINE, DH], [1, S]])
                                sp.dma_start(bias[first:first + COPIES, :, :], shifted).then_inc(tables_in, 16)
                        if u == U_G2:
                            sp.dma_start(decay[:, :, :], io["decay"]).then_inc(tables_in, 16)
                        sp.dma_start(raw[:, u % SLOTS, 0:kt * n].rearrange("p (k n) -> p k n", k=kt),
                                     io[name][l, row:row + kt * P, col:col + n].rearrange("(k p) n -> p k n", p=P)
                                     ).then_inc(raw_in[u % SLOTS], 16)

                @block.gpsimd
                def _(pool):
                    steps = [0]

                    def settle(ins):
                        steps[0] += 1
                        ins.then_inc(pool_step, 1)
                        pool.wait_ge(pool_step, steps[0])

                    def inverse_rms(j, cols, parts):
                        pool.wait_ge(stats_made, j + 1)
                        for at, n, count in parts:
                            settle(nc.gpsimd.tensor_scalar(rstd[:, j, at:at + n], ss[:, j, at:at + n], 1.0 / count, EPS,
                                                           ALU.mult, ALU.add))
                        nc.gpsimd.tensor_tensor(rstd[:, j, 0:cols], rstd[:, j, 0:cols], neghalf[:, 0:cols],
                                                ALU.pow).then_inc(rstd_made, 1)




                    def inverse_roots(jobs):
                        for norm, t, half in jobs:
                            pool.wait_ge(sums_made, sums_by(norm, t, half))
                            if half == 0:
                                settle(nc.gpsimd.tensor_scalar(sums[:, norm, t, 2:3], sums[:, norm, t, 0:1], EPS,
                                                               None, ALU.add))
                            else:
                                settle(nc.gpsimd.tensor_tensor(sums[:, norm, t, 3:4], sums[:, norm, t, 1:2],
                                                               sums[:, norm, t, 2:3], ALU.add))
                                nc.gpsimd.tensor_tensor(inv[:, norm, t:t + 1], sums[:, norm, t, 3:4],
                                                        neghalf[:, 0:1], ALU.pow).then_inc(inv_made, 1)

                    def split(u):
                        _, _, _, kt, n = UNITS[u]
                        pool.wait_ge(hi_made, u + 1)
                        nc.gpsimd.tensor_tensor(w_lo[:, u % SLOTS, 0:kt * n], raw[:, u % SLOTS, 0:kt * n],
                                                f32(w_hi[:, u % SLOTS, 0:kt * n]), ALU.subtract).then_inc(pool_lo_made, 1)
                        pool.wait_ge(pool_lo_made, sum(p <= u for p in POOL_UNITS))

                    inverse_roots(SUMS[0:4])
                    split(2)
                    inverse_rms(J_LAT, 4, [(0, 2, QL), (2, 2, KVL)])
                    split(U_UQ)

                    for k in range(DH):
                        inverse_rms(J_HEAD + k, 2, [(0, 2, 2 * DD)])
                    for k in range(RH):
                        inverse_rms(J_HEAD + DH + k, 2, [(0, 2, RDV)])
                    inverse_roots(SUMS[4:8])
                    split(U_UP[0] + 1)
                    inverse_roots(SUMS[8:])


                @block.scalar
                def _(act):
                    def split(u):
                        _, _, _, kt, n = UNITS[u]
                        act.wait_ge(raw_in[u % SLOTS], 16 * (u // SLOTS + 1))
                        if u >= SLOTS:
                            act.wait_ge(unit_used, u - SLOTS + 1)
                        nc.scalar.activation(w_hi[:, u % SLOTS, 0:kt * n], raw[:, u % SLOTS, 0:kt * n],
                                             ACT.Copy).then_inc(hi_made, 1)

                    def wait_group(first):
                        act.wait_ge(unit_used, first + GROUPS[first][0])

                    def add_squares(norm, t, half, src):
                        nc.scalar.activation(norm_junk[:, t, 512 * half:512 * half + 512], src, ACT.Square,
                                             scale=1.0 / ROOT_DM, accum_out=sums[:, norm, t, half:half + 1]
                                             ).then_inc(sums_made, 1)

                    def y_squares(norm, t, half, bank):
                        if t == 0:
                            act.wait_ge(y_tile0, 2 * (norm == POST_MLP) + half + 1)
                        else:
                            first = U_DN[7] if norm == POST_MLP else U_WOUT + 4
                            act.wait_ge(unit_used, first + 2 * half + 2)
                        add_squares(norm, t, half, bank)

                    def pre_mlp_squares(t):
                        for half in range(2):
                            act.wait_ge(x_made, x_halves_by(POST_MIX, t, half))
                            add_squares(PRE_MLP, t, half, x[:, t, 512 * half:512 * half + 512])

                    def normed_hi(norm, t, b):
                        act.wait_ge(xn_turned, normed_by(norm, t, b))
                        nc.scalar.activation(hT_hi[:, 4 * b:4 * b + 4, t * P:(t + 1) * P],
                                             A[:, 2 * t + b, :].rearrange("p (k s) -> p k s", k=4),
                                             ACT.Copy).then_inc(h_hi_made, 1)

                    def before_mla(u):
                        if u == U_LAT + 4:
                            wait_group(U_LAT)
                            rows = G[:, group(U_LAT) % 2, :, 0:LAT]
                            for t in range(TT):
                                nc.scalar.activation(lat_junk[:, t, 0:QL], rows[:, t, 0:QL], ACT.Square,
                                                     accum_out=ss[:, J_LAT, t:t + 1])
                            for t in range(TT):
                                ins = nc.scalar.activation(lat_junk[:, t, QL:], rows[:, t, QL:QL + KVL], ACT.Square,
                                                           accum_out=ss[:, J_LAT, 2 + t:3 + t])
                            ins.then_inc(stats_made, 1)
                            nc.scalar.activation(lat[:, :, :], rows, ACT.Copy).then_inc(lat_copied, 1)
                        if u == U_LAT + 8:
                            act.wait_ge(lat_turned, 1)
                            nc.scalar.activation(qkT[MN:MQ, S:2 * S], A[0:MR, 1, S:2 * S],
                                                 ACT.Copy).then_inc(k_rope_cols, 1)
                            for k in range(3):
                                g = G_Q + k if k < 2 else G_KV
                                src = A[:, k // 2, (k % 2) * S:(k % 2 + 1) * S]
                                nc.scalar.activation(bT_hi[:, k, :], src, ACT.Copy,
                                                     scale=gl[:, g:g + 1]).then_inc(lat_hi_made, 1)
                        for i, first in enumerate((U_RQ, U_RK)):
                            if u == first + 4:
                                wait_group(first)
                                if i:
                                    act.wait_ge(r_rows_made, 1)
                                nc.scalar.activation(r_src, G[:, group(first) % 2, :, :].rearrange(
                                    "p t (h n) -> p t h n", h=RH), ACT.Copy).then_inc(r_copied, 1)
                        for m in range(2):
                            if u == U_UK + m + 1 or u == U_UQ + m + 1:
                                wait_group(u - 1)
                                i = int(u < U_UQ)
                                nc.scalar.activation(
                                    qkT_own[:, 4 * m:4 * m + 4, i, :],
                                    G[:, group(u - 1) % 2, :, :].rearrange("p t n -> p (t n)").rearrange(
                                        "p (c s) -> p c s", c=4), ACT.Copy).then_inc(mla_copied, 1)
                            if u == U_UV + m + 1:
                                wait_group(u - 1)
                                nc.scalar.activation(
                                    v_rows[:, :, 8 * m:8 * m + 8, :],
                                    G[:, group(u - 1) % 2, :, :].rearrange("p t (h n) -> p t h n", h=8),
                                    ACT.Copy).then_inc(mla_copied, 1)
                        if u == U_UQR + 2:
                            wait_group(U_UQR)
                            act.wait_ge(r_rows_made, 2)
                            nc.scalar.activation(q_rope_src, G[:, group(U_UQR) % 2, :, :].rearrange(
                                "p t (h n) -> p t h n", h=MH), ACT.Copy).then_inc(mla_copied, 1)
                        if u == U_DQ + 2:
                            act.wait_ge(q_rope_turned, 1)
                            nc.scalar.activation(q_ropeT, A[:, 0:2, :].rearrange("p a (g s) -> p (a g) s", g=2),
                                                 ACT.Copy).then_inc(q_rope_cols, 1)
                        for i, at in enumerate((U_RQ + 8, U_RK + 9)):
                            if u == at:
                                act.wait_ge(r_turned, i + 1)
                                nc.scalar.activation(area_r[:, i, :], A[:, 2:4, :].rearrange("p a b -> p (a b)"),
                                                     ACT.Copy).then_inc(r_cols_made, 1)

                    def exps(H):
                        if not 0 <= H < MH + 2 * DH:
                            return
                        act.wait_ge(logits_made, H + 1)
                        if H >= MH:
                            act.wait_ge(probs_turned, MH + (H - MH) // 2)
                        elif H >= 2:
                            act.wait_ge(probs_turned, H - 1)
                        b = H % 2
                        nc.scalar.activation(probs[:, b, 0:P], logits[:, b, 0:P], ACT.Exp, bias=negmax[:, b, 0:1],
                                             scale=-1.0, accum_out=rowsum[:, b, 0:1])
                        nc.scalar.activation(probs[:, b, P:384], logits[:, b, P:384], ACT.Exp, bias=negmax[:, b, 1:2],
                                             scale=-1.0, accum_out=rowsum[:, b, 1:2]).then_inc(exp_made, 1)

                    def probs_cols(H):
                        J = mix_index(H)
                        if J is None or J >= MH + DH:
                            return
                        act.wait_ge(probs_turned, J + 1)
                        if J >= 1:
                            act.wait_ge(mix_made, J)
                        nc.scalar.activation(probsT[:, :], A[:, 2, 0:384], ACT.Copy).then_inc(probsT_made, 1)

                    def mixed(H):
                        J, K = mix_index(H), head_index(H)
                        if J is None:
                            return
                        if J < MH and J % 2:
                            act.wait_ge(mix_made, J + 1)
                            nc.scalar.activation(bT_hi[:, J // 2, :], A[:, 3, 0:S], ACT.Copy).then_inc(pair_hi_made, 1)
                        if K is not None and K < DH:
                            act.wait_ge(mix_made, J + 1)
                            if K >= 1:
                                act.wait_ge(head_turned, K)
                            for t in range(TT):
                                cols = slice(t * P, (t + 1) * P)
                                ins = nc.scalar.activation(junk[:, cols], A[:, 3, cols], ACT.Square,
                                                           scale=rrow_sum[:, K % 2, 0, t:t + 1],
                                                           accum_out=ss[:, J_HEAD + K, t:t + 1])
                            ins.then_inc(stats_made, 1)
                            for t in range(TT):
                                ins = nc.scalar.activation(orow[:, t * P:(t + 1) * P], A[:, 3, t * P:(t + 1) * P],
                                                           ACT.Copy, scale=rrow_sum[:, K % 2, 0, t:t + 1])
                            ins.then_inc(head_stats, 1)
                        if K is not None and K >= DH:
                            act.wait_ge(mix_made, J + 1)
                            for t in range(TT):
                                cols = slice(t * RDV, (t + 1) * RDV)
                                ins = nc.scalar.activation(junk[:, cols], A[:, 3, cols], ACT.Square,
                                                           accum_out=ss[:, J_HEAD + K, t:t + 1])
                            ins.then_inc(stats_made, 1)

                    def head_cols(H):
                        K = head_index(H)
                        if K is None:
                            return
                        act.wait_ge(head_turned, K + 1)
                        if K < DH:
                            nc.scalar.activation(dT_hi[:, K, :], A[:, 0, 0:S], ACT.Copy,
                                                 scale=gl[:, G_SUB:G_SUB + 1]).then_inc(head_hi, 1)
                        else:
                            r = K - DH
                            act.wait_ge(unit_used, U_MLAO + 8)
                            nc.scalar.activation(bT_hi[:, 2 * r:2 * r + 2, :].rearrange("p k s -> p (k s)"), A[:, 0, :],
                                                 ACT.Copy, scale=0.5).then_inc(head_hi, 1)

                    def qk_cols(h):
                        if h >= MH:
                            return
                        if h == 0:
                            act.wait_ge(mla_copied, 7)
                            act.wait_ge(q_rope_cols, 1)
                            act.wait_ge(k_rope_cols, 1)
                        else:
                            act.wait_ge(scores_made, h)
                        own, rope = MN * (h % 2), MR * (h % 4)
                        nc.scalar.activation(qkT[0:MN, :], qkT_own[own:own + MN, h // 2, :, :].rearrange(
                            "p i s -> p (i s)"), ACT.Copy)
                        nc.scalar.activation(qkT[MN:MQ, 0:S], q_ropeT[rope:rope + MR, h // 4, :],
                                             ACT.Copy).then_inc(qk_cols_made, 1)

                    def attention(u):
                        s = u - ATTENTION
                        if s < 0:
                            return
                        m = s // 2
                        if s % 2 == 0:
                            qk_cols(m)
                            exps(m - 1)
                            probs_cols(m - 2)
                        else:
                            mixed(m - 2)
                            head_cols(m - 3)

                    def gates(u):
                        for first, out in ((U_G2, tanh_g), (U_RG, rg_rows), (U_G1, tanh_g1), (U_G0, tanh_g)):
                            for half in range(2):
                                if u == first + 4 * half + 4:
                                    wait_group(first + 4 * half)
                                    if first == U_G0:
                                        act.wait_ge(gated, 2)
                                    if first == U_RG:
                                        act.wait_ge(mix_made, MH)
                                    nc.scalar.activation(
                                        out[:, :, 512 * half:512 * half + 512],
                                        G[:, group(first + 4 * half) % 2, :, :], ACT.Tanh, scale=0.5
                                    ).then_inc(tanh_made, 1)

                    def merged_cols(half):
                        act.wait_ge(merged_turned, half + 1)
                        nc.scalar.activation(hT_hi[:, 4 * half:4 * half + 4, :].rearrange("p k s -> p (k s)"),
                                             A[:, 2 * half:2 * half + 2, :].rearrange("p a b -> p (a b)"),
                                             ACT.Copy, scale=0.5).then_inc(merged_hi, 1)



                    def hidden(u):
                        for j in range(8):
                            if u == U_UP[j] + 4:
                                wait_group(U_UP[j])
                                if j >= 1:
                                    act.wait_ge(square_made, j)
                                nc.scalar.activation(relu_h, G[:, group(U_UP[j]) % 2, :, :].rearrange("p a b -> p (a b)"),
                                                     ACT.Relu).then_inc(relu_made, 1)
                            if j == 0 and u == U_UP[1] + 2:
                                act.wait_ge(hid_turned, 1)
                                nc.scalar.activation(hid_hi[:, 0, :, :].rearrange("p k s -> p (k s)"),
                                                     A[:, 0:2, :].rearrange("p a b -> p (a b)"),
                                                     ACT.Copy).then_inc(hid_hi_made, 1)
                            if j >= 1 and u == U_UP[j] + 5:
                                act.wait_ge(square_made, j + 1)
                                if j >= 2:
                                    act.wait_ge(unit_used, U_DN[j - 2] + 4)
                                nc.scalar.activation(hid_hi[:, j % 2, :, :].rearrange("p k s -> p (k s)"), square_h,
                                                     ACT.Copy).then_inc(hid_hi_made, 1)

                    for t in range(TT):
                        act.wait_ge(x_in[t], 16)
                        for half in range(2):
                            add_squares(PRE_MIX, t, half, x[:, t, 512 * half:512 * half + 512])
                    split(0)
                    normed_hi(PRE_MIX, 0, 0)
                    split(1)
                    normed_hi(PRE_MIX, 0, 1)
                    split(2)
                    split(3)
                    normed_hi(PRE_MIX, 1, 0)
                    normed_hi(PRE_MIX, 1, 1)
                    for u in range(1, U_WOUT + 5):
                        if u in (U_RQ + 4, U_RK + 4) or U_UK < u <= U_DQ:
                            before_mla(u)
                            split(u + 3)
                        else:
                            split(u + 3)
                            before_mla(u)
                        attention(u)
                        gates(u)
                        if u == U_RETO:
                            act.dma_start(area_e[:, 2048:2048 + 4 * DM],
                                          io["gain_rows"][l].rearrange("(a n) -> a n", a=1).broadcast_to([P, 4 * DM])
                                          ).then_inc(gain_rows_in, 16)
                        if u == U_RETO + 6:
                            merged_cols(0)
                        if u == U_WOUT + 2:
                            merged_cols(1)
                    y = [[G[:, group(U_WOUT + 4 * half) % 2, t, :] for half in range(2)] for t in range(TT)]
                    for half in range(2):
                        y_squares(POST_MIX, 0, half, y[0][half])
                    split(U_UP[0])
                    pre_mlp_squares(0)
                    split(U_UP[0] + 1)
                    y_squares(POST_MIX, 1, 0, y[1][0])
                    y_squares(POST_MIX, 1, 1, y[1][1])
                    normed_hi(PRE_MLP, 0, 0)
                    split(U_UP[0] + 2)
                    normed_hi(PRE_MLP, 0, 1)
                    split(U_UP[0] + 3)
                    pre_mlp_squares(1)
                    normed_hi(PRE_MLP, 1, 0)
                    normed_hi(PRE_MLP, 1, 1)
                    for u in range(U_UP[0] + 1, NU):
                        if u + 3 < NU:
                            split(u + 3)
                        hidden(u)
                    for t in range(TT):
                        for half in range(2):
                            y_squares(POST_MLP, t, half, A[:, 2 * t + half, :])

                @block.vector
                def _(dve):
                    steps, reads = [0], [0]

                    def settle(ins):
                        steps[0] += 1
                        ins.then_inc(dve_step, 1)
                        dve.wait_ge(dve_step, steps[0])

                    def split(u):
                        if u in POOL_UNITS:
                            return
                        _, _, _, kt, n = UNITS[u]
                        dve.wait_ge(hi_made, u + 1)
                        nc.vector.tensor_tensor(w_lo[:, u % SLOTS, 0:kt * n], raw[:, u % SLOTS, 0:kt * n],
                                                f32(w_hi[:, u % SLOTS, 0:kt * n]), ALU.subtract).then_inc(lo_made, 1)

                    def wait_group(first):
                        dve.wait_ge(unit_used, first + GROUPS[first][0])



                    def pre_norm_rows(norm, t, half):
                        if norm == PRE_MIX:
                            dve.wait_ge(x_in[t], 16)
                            dve.wait_ge(first_gain_in, 16)
                        dve.wait_ge(inv_made, inv_by(norm, t))
                        cols = slice(512 * half, 512 * half + 512)
                        nc.vector.scalar_tensor_tensor(xn[:, t, cols], x[:, t, cols], inv[:, norm, t:t + 1],
                                                       gain_rows[:, R_PRE_MLP if norm == PRE_MLP else R_NEXT_PRE_MIX, cols],
                                                       ALU.mult, ALU.mult).then_inc(xn_made, 1)

                    def normed_lo(norm, t, b):
                        dve.wait_ge(h_hi_made, normed_by(norm, t, b))
                        nc.vector.tensor_tensor(hT_lo[:, 4 * b:4 * b + 4, t * P:(t + 1) * P],
                                                A[:, 2 * t + b, :].rearrange("p (k s) -> p k s", k=4),
                                                f32(hT_hi[:, 4 * b:4 * b + 4, t * P:(t + 1) * P]),
                                                ALU.subtract).then_inc(h_lo_made, 1)

                    def gained(norm, t, half, y):
                        dve.wait_ge(sums_made, sums_by(norm, t, half))
                        cols = slice(512 * half, 512 * half + 512)
                        nc.vector.tensor_tensor(xn[:, t, cols], y,
                                                gain_rows[:, R_POST_MLP if norm == POST_MLP else R_POST_MIX, cols],
                                                ALU.mult).then_inc(y_read, 1)
                        reads[0] += 1

                    def post_norm(norm, t):
                        dve.wait_ge(inv_made, inv_by(norm, t))
                        dve.wait_ge(y_read, reads[0])
                        for half in range(2):
                            cols = slice(512 * half, 512 * half + 512)
                            nc.vector.scalar_tensor_tensor(x[:, t, cols], xn[:, t, cols], inv[:, norm, t:t + 1],
                                                           x[:, t, cols], ALU.mult, ALU.add).then_inc(x_made, 1)

                    def rope(out, src, cos, sin, half, tmp):
                        nc.vector.tensor_tensor(out, src, cos, ALU.mult)
                        nc.vector.tensor_tensor(tmp[..., 0:half], src[..., half:], sin[..., 0:half], ALU.mult)
                        return nc.vector.tensor_tensor(tmp[..., half:], src[..., 0:half], sin[..., half:], ALU.mult)

                    def before_mla(u):
                        if u == U_LAT + 6:
                            dve.wait_ge(rstd_made, J_LAT + 1)
                            dve.wait_ge(lat_copied, 1)
                            kp = lat[:, :, QL + KVL:LAT]
                            settle(rope(kpe_tmp[:, :, 0:MR], kp, m_cos, m_sin, MR // 2, kpe_tmp[:, :, MR:2 * MR]))
                            nc.vector.tensor_tensor(kpe_tmp[:, :, 0:MR], kpe_tmp[:, :, 0:MR], kpe_tmp[:, :, MR:2 * MR],
                                                    ALU.add).then_inc(kpe_made, 1)
                            for t in range(TT):
                                nc.vector.tensor_scalar(lat[:, t, 0:QL], lat[:, t, 0:QL], rstd[:, J_LAT, t:t + 1], None,
                                                        ALU.mult)
                                ins = nc.vector.tensor_scalar(lat[:, t, QL:QL + KVL], lat[:, t, QL:QL + KVL],
                                                              rstd[:, J_LAT, 2 + t:3 + t], None, ALU.mult)
                            ins.then_inc(lat_rows_made, 1)
                        if u == U_LAT + 8:
                            for k in range(3):
                                g = G_Q + k if k < 2 else G_KV
                                dve.wait_ge(lat_hi_made, 2 if k < 2 else 3)
                                nc.vector.scalar_tensor_tensor(
                                    bT_lo[:, k, :], A[:, k // 2, (k % 2) * S:(k % 2 + 1) * S], gl[:, g:g + 1],
                                    f32(bT_hi[:, k, :]), ALU.mult, ALU.subtract).then_inc(lat_lo_made, 1)
                        for i, first in enumerate((U_RQ, U_RK)):
                            if u == first + 4:
                                dve.wait_ge(r_copied, i + 1)
                                if i:
                                    dve.wait_ge(r_turned, 1)
                                cos = r_cos.rearrange("p t (h n) -> p t h n", h=1).broadcast_to([P, TT, RH, RDK])
                                sin = r_sin.rearrange("p t (h n) -> p t h n", h=1).broadcast_to([P, TT, RH, RDK])
                                settle(rope(r_rows, r_src, cos, sin, RDK // 2, r_tmp))
                                nc.vector.tensor_tensor(r_rows, r_rows, r_tmp, ALU.add).then_inc(r_rows_made, 1)
                        if u == U_UQR + 2:
                            dve.wait_ge(mla_copied, 7)
                            dve.wait_ge(r_turned, 2)
                            cos = m_cos.rearrange("p t (h n) -> p t h n", h=1).broadcast_to([P, TT, MH, MR])
                            sin = m_sin.rearrange("p t (h n) -> p t h n", h=1).broadcast_to([P, TT, MH, MR])
                            settle(rope(q_rope_rows, q_rope_src, cos, sin, MR // 2, q_rope_tmp))
                            nc.vector.tensor_tensor(q_rope_rows, q_rope_rows, q_rope_tmp,
                                                    ALU.add).then_inc(q_rope_made, 1)


                    def logits_of(H):
                        if not 0 <= H < N_HEADS:
                            return
                        dve.wait_ge(scores_made, H + 1)
                        b = H % 2
                        if H >= MH + 2 * DH:
                            r = H - MH - 2 * DH
                            if r == 0:
                                dve.wait_ge(exp_made, H)
                            if r >= 2:
                                dve.wait_ge(mix_made, MH + DH + r - 1)
                            nc.vector.tensor_tensor(logits[:, b, :], A[:, 1, 0:384], decay[:, r, :],
                                                    ALU.mult).then_inc(logits_made, 1)
                            return
                        if H >= 2:
                            dve.wait_ge(exp_made, H - 1)
                        if H == MH:
                            dve.wait_ge(tables_in, 16 * (P // COPIES + 1))
                        if H < MH:
                            add, scale = mask, float(MQ) ** -0.5
                        else:
                            add, scale = bias[:, (H - MH) // 2, :], float(DD) ** -0.5
                        nc.vector.tensor_tensor_reduce(logits[:, b, 0:P], A[:, 1, 0:P], add[:, P:S], -scale, BIG,
                                                       ALU.add, ALU.min, negmax[:, b, 0:1])
                        nc.vector.tensor_tensor_reduce(logits[:, b, P:384], A[:, 1, P:384], add, -scale, BIG,
                                                       ALU.add, ALU.min, negmax[:, b, 1:2]).then_inc(logits_made, 1)

                    def probs_of(H):
                        J = mix_index(H)
                        if J is None or J >= MH + DH:
                            return
                        dve.wait_ge(exp_made, H + 1)
                        if H < MH:
                            b = H % 2
                            settle(nc.vector.reciprocal(rrow_sum[:, b, 0, :], rowsum[:, b, :]))
                            nc.vector.tensor_scalar(probs[:, b, 0:P], probs[:, b, 0:P], rrow_sum[:, b, 0, 0:1], None,
                                                    ALU.mult)
                            nc.vector.tensor_scalar(probs[:, b, P:384], probs[:, b, P:384], rrow_sum[:, b, 0, 1:2], None,
                                                    ALU.mult).then_inc(probs_made, 1)
                        else:
                            k = J - MH
                            if k >= 2:
                                dve.wait_ge(head_stats, k - 1)
                            settle(nc.vector.reciprocal(rrow_sum[:, k % 2, :, :], rowsum[:, :, :]))
                            settle(nc.vector.scalar_tensor_tensor(negr[:, :], rrow_sum[:, k % 2, 1, :],
                                                                  gl[:, G_LAM:G_LAM + 1], rowsum[:, 0, :],
                                                                  ALU.mult, ALU.mult))
                            nc.vector.scalar_tensor_tensor(probs[:, 0, 0:P], probs[:, 1, 0:P], negr[:, 0:1],
                                                           probs[:, 0, 0:P], ALU.mult, ALU.add)
                            nc.vector.scalar_tensor_tensor(probs[:, 0, P:384], probs[:, 1, P:384], negr[:, 1:2],
                                                           probs[:, 0, P:384], ALU.mult, ALU.add).then_inc(probs_made, 1)

                    def pair_lo(H):
                        J = mix_index(H)
                        if J is not None and J < MH and J % 2:
                            dve.wait_ge(pair_hi_made, J // 2 + 1)
                            nc.vector.tensor_tensor(bT_lo[:, J // 2, :], A[:, 3, 0:S], f32(bT_hi[:, J // 2, :]),
                                                    ALU.subtract).then_inc(pair_lo_made, 1)

                    def head_rows_of(H):
                        K = head_index(H)
                        if K is None:
                            return
                        dve.wait_ge(rstd_made, J_HEAD + K + 1)
                        if K >= 1:
                            dve.wait_ge(head_turned, K)
                        for t in range(TT):
                            inv = rstd[:, J_HEAD + K, t:t + 1]
                            if K < DH:
                                if t == 0:
                                    dve.wait_ge(head_stats, K + 1)
                                ins = nc.vector.tensor_scalar(orow[:, t * P:(t + 1) * P], orow[:, t * P:(t + 1) * P], inv,
                                                              None, ALU.mult)
                            else:
                                r = K - DH
                                ins = nc.vector.scalar_tensor_tensor(
                                    orow[:, t * RDV:(t + 1) * RDV], A[:, 3, t * RDV:(t + 1) * RDV], inv,
                                    rg_rows[:, t, r * RDV:(r + 1) * RDV], ALU.mult, ALU.mult)
                        ins.then_inc(head_rows, 1)

                    def head_cols(H):
                        K = head_index(H)
                        if K is None:
                            return
                        dve.wait_ge(head_hi, K + 1)
                        if K < DH:
                            nc.vector.scalar_tensor_tensor(dT_lo[:, K, :], A[:, 0, 0:S], gl[:, G_SUB:G_SUB + 1],
                                                           f32(dT_hi[:, K, :]), ALU.mult, ALU.subtract).then_inc(head_lo, 1)
                        else:
                            r = K - DH
                            nc.vector.scalar_tensor_tensor(
                                bT_lo[:, 2 * r:2 * r + 2, :].rearrange("p k s -> p (k s)"), A[:, 0, :], 0.5,
                                f32(bT_hi[:, 2 * r:2 * r + 2, :]).rearrange("p k s -> p (k s)"),
                                ALU.mult, ALU.subtract).then_inc(head_lo, 1)

                    def attention_first(u):
                        s = u - ATTENTION
                        if s >= 0 and s % 2 == 0:
                            logits_of(s // 2 - 1)
                            head_rows_of(s // 2 - 3)

                    def attention_then(u):
                        s = u - ATTENTION
                        if s >= 0 and s % 2 == 0:
                            probs_of(s // 2 - 1)
                        if s >= 0 and s % 2 == 1:
                            pair_lo(s // 2 - 2)
                            head_cols(s // 2 - 3)

                    def evacuate(u):
                        for first, out in ((U_DQ, dqT), (U_DK, dkT)):
                            for half in range(2):
                                if u == first + 4 * half + 4:
                                    wait_group(first + 4 * half)
                                    nc.vector.tensor_copy(
                                        out[:, 4 * half:4 * half + 4, :].rearrange("p k s -> p (k s)"),
                                        G[:, group(first + 4 * half) % 2, :, :].rearrange("p a b -> p (a b)")
                                    ).then_inc(evacuated, 1)
                        for first, out in ((U_DV, dv_rows), (U_RV, rv_rows)):
                            for half in range(2):
                                if u == first + 4 * half + 4:
                                    wait_group(first + 4 * half)
                                    if first == U_RV:
                                        dve.wait_ge(qk_cols_made, MH)
                                    if first == U_DQ:
                                        dve.wait_ge(q_rope_turned, 1)
                                    nc.vector.tensor_copy(out[:, :, 512 * half:512 * half + 512],
                                                          G[:, group(first + 4 * half) % 2, :, :]).then_inc(evacuated, 1)
                        for half in range(2):
                            cols = slice(512 * half, 512 * half + 512)
                            if u == U_RG + 4 * half + 4:
                                first = U_RG + 4 * half
                                dve.wait_ge(tanh_made, tanh_index(first) + 1)
                                for t in range(TT):
                                    ins = nc.vector.scalar_tensor_tensor(rg_rows[:, t, cols], rg_rows[:, t, cols], 1.0,
                                                                         G[:, group(first) % 2, t, :], ALU.add, ALU.mult)
                                ins.then_inc(silu_made, 1)
                            for i, (first, gate, gate_first) in enumerate((
                                    (U_MLAO, tanh_g, U_G2), (U_DIFFO, tanh_g1, U_G1), (U_RETO, tanh_g, U_G0))):
                                if u == first + 4 * half + 4:
                                    at = first + 4 * half
                                    wait_group(at)
                                    dve.wait_ge(tanh_made, tanh_index(gate_first + 4 * half) + 1)
                                    out = merged if i == 0 else gate
                                    ins = nc.vector.scalar_tensor_tensor(out[:, :, cols], gate[:, :, cols], 1.0,
                                                                         G[:, group(at) % 2, :, :], ALU.add, ALU.mult)
                                    ins.then_inc(gated, 1)
                                    if i:
                                        dve.wait_ge(gated, 2 * i + half + 1)
                                        nc.vector.tensor_tensor(merged[:, :, cols], merged[:, :, cols],
                                                                gate[:, :, cols], ALU.add).then_inc(merged_made, 1)

                    def merged_cols(half):
                        dve.wait_ge(merged_hi, half + 1)
                        nc.vector.scalar_tensor_tensor(
                            hT_lo[:, 4 * half:4 * half + 4, :].rearrange("p k s -> p (k s)"),
                            A[:, 2 * half:2 * half + 2, :].rearrange("p a b -> p (a b)"), 0.5,
                            f32(hT_hi[:, 4 * half:4 * half + 4, :]).rearrange("p k s -> p (k s)"),
                            ALU.mult, ALU.subtract).then_inc(merged_lo, 1)

                    def hidden(u):
                        for j in range(8):
                            if u == U_UP[j] + 4:
                                dve.wait_ge(relu_made, j + 1)
                                if j >= 1:
                                    dve.wait_ge(hid_lo_made, j)
                                ins = nc.vector.tensor_tensor(
                                    square_h, G[:, group(U_UP[j]) % 2, :, :].rearrange("p a b -> p (a b)"), relu_h,
                                    ALU.mult)
                                ins.then_inc(square_made, 1)
                            if j == 0 and u == U_UP[1] + 2:
                                dve.wait_ge(hid_hi_made, 1)
                                nc.vector.tensor_tensor(hid_lo[:, 0, :, :].rearrange("p k s -> p (k s)"),
                                                        A[:, 0:2, :].rearrange("p a b -> p (a b)"),
                                                        f32(hid_hi[:, 0, :, :]).rearrange("p k s -> p (k s)"),
                                                        ALU.subtract).then_inc(hid_lo_made, 1)
                            if j >= 1 and u == U_UP[j] + 5:
                                dve.wait_ge(hid_hi_made, j + 1)
                                nc.vector.tensor_tensor(hid_lo[:, j % 2, :, :].rearrange("p k s -> p (k s)"), square_h,
                                                        f32(hid_hi[:, j % 2, :, :]).rearrange("p k s -> p (k s)"),
                                                        ALU.subtract).then_inc(hid_lo_made, 1)

                    nc.vector.tensor_copy(gl[:, :], gains[:, l, :]).then_inc(gains_set, 1)
                    dve.wait_ge(gains_set, 1)
                    for t in range(TT):
                        for half in range(2):
                            pre_norm_rows(PRE_MIX, t, half)
                    split(0)
                    normed_lo(PRE_MIX, 0, 0)
                    split(1)
                    normed_lo(PRE_MIX, 0, 1)
                    split(3)
                    normed_lo(PRE_MIX, 1, 0)
                    normed_lo(PRE_MIX, 1, 1)
                    for u in range(1, U_WOUT + 5):
                        attention_first(u)
                        split(u + 3)
                        before_mla(u)
                        attention_then(u)
                        evacuate(u)
                        if u == U_RETO + 6:
                            merged_cols(0)
                        if u == U_WOUT + 2:
                            merged_cols(1)
                    y = [[G[:, group(U_WOUT + 4 * half) % 2, t, :] for half in range(2)] for t in range(TT)]
                    dve.wait_ge(gain_rows_in, 16)
                    for half in range(2):
                        gained(POST_MIX, 0, half, y[0][half])
                    post_norm(POST_MIX, 0)
                    split(U_UP[0])
                    for half in range(2):
                        pre_norm_rows(PRE_MLP, 0, half)
                    for half in range(2):
                        gained(POST_MIX, 1, half, y[1][half])
                    normed_lo(PRE_MLP, 0, 0)
                    split(U_UP[0] + 2)
                    normed_lo(PRE_MLP, 0, 1)
                    post_norm(POST_MIX, 1)
                    split(U_UP[0] + 3)
                    for half in range(2):
                        pre_norm_rows(PRE_MLP, 1, half)
                    normed_lo(PRE_MLP, 1, 0)
                    normed_lo(PRE_MLP, 1, 1)
                    for u in range(U_UP[0] + 1, NU):
                        if u + 3 < NU:
                            split(u + 3)
                        hidden(u)
                    for t in range(TT):
                        for half in range(2):
                            gained(POST_MLP, t, half, A[:, 2 * t + half, :])
                        post_norm(POST_MLP, t)

                @block.tensor
                def _(pe):
                    def three(out, stationary, moving, start, stop, check=False):
                        for i, (a, b) in enumerate(((0, 0), (0, 1), (1, 0))):
                            ins = nc.tensor.matmul(out, stationary[a], moving[b], start=start and i == 0,
                                                   stop=stop and i == 2, skip_group_check=check)
                        return ins

                    def tokens_stationary(u, first_tile, acts, outs, start, stop, tiles=range(TT)):
                        _, _, _, kt, n = UNITS[u]
                        pe.wait_ge(*lo_ready(u))
                        for kk in range(kt):
                            k = first_tile + kk
                            for t in tiles:
                                last = three(outs[t],
                                             (acts[0][:, k, t * P:(t + 1) * P], acts[1][:, k, t * P:(t + 1) * P]),
                                             (w_hi[:, u % SLOTS, kk * n:(kk + 1) * n],
                                              w_lo[:, u % SLOTS, kk * n:(kk + 1) * n]),
                                             start and kk == 0, stop and kk == kt - 1)
                        return last

                    def weights_stationary(u, first_tile, acts, out, start, stop):
                        kt = UNITS[u][3]
                        pe.wait_ge(*lo_ready(u))
                        for c in range(4):
                            for kk in range(kt):
                                k = first_tile + kk
                                at = kk * 512 + c * P
                                last = three(out[:, c, :],
                                             (w_hi[:, u % SLOTS, at:at + P], w_lo[:, u % SLOTS, at:at + P]),
                                             (acts[0][:, k, :], acts[1][:, k, :]),
                                             start and kk == 0 and c % 2 == 0, stop and kk == kt - 1, check=True)
                        last.then_inc(unit_used, 1)

                    def take_pair(first):
                        n = group(first)
                        if n >= 2:
                            pe.wait_ge(*left_banks(n - 2))
                        return G[:, n % 2, :, :]

                    acts_h, acts_b, acts_d = (hT_hi, hT_lo), (bT_hi, bT_lo), (dT_hi, dT_lo)

                    def gemm(u):
                        first = u if U_UK <= u < U_UQR else u - u % 4 if u < U_UK or U_DQ <= u else U_UQR
                        i = u - first
                        pair = take_pair(u) if i == 0 else G[:, group(first) % 2, :, :]
                        cols = pair.rearrange("p t n -> p (t n)").rearrange("p (c s) -> p c s", c=4)
                        n = UNITS[u][4]
                        start, stop = i == 0, i == GROUPS[first][0] - 1
                        if U_UK <= u < U_UV:
                            weights_stationary(u, 2, acts_b, cols, True, True)
                        elif U_UQ <= u < U_UQR:
                            weights_stationary(u, 0, acts_b, cols, True, True)
                        elif U_UV <= u < U_DQ:
                            tokens_stationary(u, 2 if u < U_UQ else i, acts_b, [pair[:, t, 0:n] for t in range(TT)],
                                              start, stop).then_inc(unit_used, 1)
                        elif U_DQ <= u < U_DV or u >= U_UP[0]:
                            weights_stationary(u, 2 * i, acts_h, cols, start, stop)
                        else:
                            acts = acts_h
                            if U_MLAO <= u < U_RG or U_RETO <= u < U_WOUT:
                                acts = acts_b
                            if U_DIFFO <= u < U_RETO:
                                acts = acts_d
                            tokens_stationary(u, 2 * i, acts, [pair[:, t, 0:n] for t in range(TT)], start, stop
                                              ).then_inc(unit_used, 1)

                    def latents():
                        for t in range(TT):
                            for i in range(4):
                                u = U_LAT + i
                                pe.wait_ge(h_lo_made, normed_by(PRE_MIX, t, i // 2))
                                last = tokens_stationary(u, 2 * i, acts_h, [G[:, 0, tt, 0:LAT] for tt in range(TT)],
                                                         i == 0, i == 3, [t])
                                if t == 1:
                                    last.then_inc(unit_used, 1)

                    def mixers_out():
                        pairs = []
                        for i in range(4):
                            if i % 2 == 0:
                                pairs.append(take_pair(U_WOUT + 2 * i))
                            if i == 0:
                                pe.wait_ge(merged_lo, 1)
                            pair = pairs[i // 2]
                            tokens_stationary(U_WOUT + i, 2 * (i % 2), acts_h, [pair[:, t, :] for t in range(TT)],
                                              i % 2 == 0, False).then_inc(unit_used, 1)
                            if i == 1:
                                turn_merged(1)
                        pe.wait_ge(merged_lo, 2)
                        for t in range(TT):
                            for i in range(4):
                                pair = pairs[i // 2]
                                last = tokens_stationary(U_WOUT + 4 + i, 4 + 2 * (i % 2), acts_h,
                                                         [pair[:, tt, :] for tt in range(TT)], False, i % 2 == 1, [t])
                                if t == 1:
                                    last.then_inc(unit_used, 1)
                                elif i % 2:
                                    last.then_inc(y_tile0, 1)

                    def norm_turn(norm, t, b):
                        pe.wait_ge(xn_made, normed_by(norm, t, b))
                        for k in range(4):
                            last = nc.tensor.transpose(A[:, 2 * t + b, k * P:(k + 1) * P],
                                                       xn[:, t, (4 * b + k) * P:(4 * b + k + 1) * P], ident)
                        last.then_inc(xn_turned, 1)

                    def before_mla(u):
                        if u == U_LAT + 7:
                            pe.wait_ge(lat_rows_made, 1)
                            for k in range(3):
                                for t in range(TT):
                                    last = nc.tensor.transpose(
                                        A[:, k // 2, (k % 2) * S + t * P:(k % 2) * S + (t + 1) * P],
                                        lat[:, t, k * P:(k + 1) * P], ident)
                            for t in range(TT):
                                last = nc.tensor.transpose(A[0:MR, 1, S + t * P:S + (t + 1) * P], kpe_tmp[:, t, 0:MR],
                                                           ident)
                            last.then_inc(lat_turned, 1)
                        for i, at in enumerate((U_RQ + 7, U_RK + 8)):
                            if u == at:
                                pe.wait_ge(r_rows_made, i + 1)
                                if i:
                                    pe.wait_ge(r_cols_made, 1)
                                for h in range(RH):
                                    for t in range(TT):
                                        last = nc.tensor.transpose(
                                            A[:, 2 + h // 2, (h % 2) * S + t * P:(h % 2) * S + (t + 1) * P],
                                            r_rows[:, t, h, :], ident)
                                last.then_inc(r_turned, 1)

                    def turn_q_rope():
                        pe.wait_ge(q_rope_made, 1)
                        rows = q_rope_rows.rearrange("p t h n -> p t (h n)")
                        for g in range(MH // 4):
                            for t in range(TT):
                                last = nc.tensor.transpose(A[:, g // 2, (g % 2) * S + t * P:(g % 2) * S + (t + 1) * P],
                                                           rows[:, t, g * P:(g + 1) * P], ident)
                        last.then_inc(q_rope_turned, 1)


                    def scores(H):
                        if not 0 <= H < N_HEADS:
                            return
                        if H >= 1:
                            pe.wait_ge(logits_made, H)
                        out = A[:, 1, :]
                        if H < MH:
                            pe.wait_ge(qk_cols_made, H + 1)
                            nc.tensor.matmul(out[:, 0:P], qkT[:, 0:P], qkT[:, S:S + P], start=True, stop=True)
                            last = nc.tensor.matmul(out[:, P:384], qkT[:, P:S], qkT[:, S:2 * S], start=True, stop=True)
                        elif H < MH + 2 * DH:
                            h, c = (H - MH) // 2, (H - MH) % 2
                            if H == MH:
                                pe.wait_ge(evacuated, 4)
                            q, k = dqT[c * DD:(c + 1) * DD, h, :], dkT[c * DD:(c + 1) * DD, h, :]
                            nc.tensor.matmul(out[:, 0:P], q[:, 0:P], k[:, 0:P], start=True, stop=True)
                            last = nc.tensor.matmul(out[:, P:384], q[:, P:S], k, start=True, stop=True)
                        else:
                            r = H - MH - 2 * DH
                            nc.tensor.matmul(out[:, 0:S], rkT[:, r, 0:P], rqT[:, r, :], start=True, stop=True)
                            last = nc.tensor.matmul(out[:, S:384], rkT[:, r, P:S], rqT[:, r, P:S], start=True, stop=True)
                        last.then_inc(scores_made, 1)

                    def turn_probs(H):
                        J = mix_index(H)
                        if J is None or J >= MH + DH:
                            return
                        pe.wait_ge(probs_made, J + 1)
                        if J >= 1:
                            pe.wait_ge(probsT_made, J)
                        else:
                            pe.wait_ge(r_cols_made, 2)
                        b = J % 2 if J < MH else 0
                        for i in range(3):
                            last = nc.tensor.transpose(A[:, 2, i * P:(i + 1) * P], probs[:, b, i * P:(i + 1) * P], ident)
                        last.then_inc(probs_turned, 1)

                    def mix(H):
                        J = mix_index(H)
                        if J is None:
                            return
                        out = A[:, 3, :]
                        if J < MH + DH:
                            pe.wait_ge(probsT_made, J + 1)
                        if J < MH:
                            if J % 2 == 0 and J >= 2:
                                pe.wait_ge(pair_lo_made, J // 2)
                            row = MV * (J % 2)
                            nc.tensor.matmul(out[row:row + MV, 0:S], v_rows[:, 0, J, :], probsT[:, 0:S], start=True,
                                             stop=False)
                            last = nc.tensor.matmul(out[row:row + MV, P:S], v_rows[:, 1, J, :], probsT[:, S:384],
                                                    start=False, stop=True)
                        elif J < MH + DH:
                            k = J - MH
                            if k == 0:
                                pe.wait_ge(pair_lo_made, MH // 2)
                                pe.wait_ge(evacuated, 6)
                            else:
                                pe.wait_ge(head_stats, k)
                            v0, v1 = dv_rows[:, 0, k * P:(k + 1) * P], dv_rows[:, 1, k * P:(k + 1) * P]
                            nc.tensor.matmul(out[:, 0:P], probsT[:, 0:P], v0, start=True, stop=True)
                            nc.tensor.matmul(out[:, P:S], probsT[:, P:S], v0, start=True, stop=False)
                            last = nc.tensor.matmul(out[:, P:S], probsT[:, S:384], v1, start=False, stop=True)
                        else:
                            r = J - MH - DH
                            pe.wait_ge(logits_made, H + 1)
                            if r == 0:
                                pe.wait_ge(head_stats, DH)
                                pe.wait_ge(evacuated, 8)
                            else:
                                pe.wait_ge(head_rows, DH + r)
                            w = logits[:, H % 2, :]
                            v0, v1 = rv_rows[:, 0, r * RDV:(r + 1) * RDV], rv_rows[:, 1, r * RDV:(r + 1) * RDV]
                            nc.tensor.matmul(out[:, 0:RDV], w[:, 0:P], v0, start=True, stop=True)
                            nc.tensor.matmul(out[:, RDV:2 * RDV], w[:, P:S], v0, start=True, stop=False)
                            last = nc.tensor.matmul(out[:, RDV:2 * RDV], w[:, S:384], v1, start=False, stop=True)
                        last.then_inc(mix_made, 1)

                    def turn_head(H):
                        K = head_index(H)
                        if K is None:
                            return
                        pe.wait_ge(head_rows, K + 1)
                        if K >= 1:
                            pe.wait_ge(head_lo, K)
                        if K < DH:
                            for t in range(TT):
                                last = nc.tensor.transpose(A[:, 0, t * P:(t + 1) * P], orow[:, t * P:(t + 1) * P], ident)
                        else:
                            for f in range(RDV // P):
                                for t in range(TT):
                                    last = nc.tensor.transpose(A[:, 0, f * S + t * P:f * S + (t + 1) * P],
                                                               orow[:, t * RDV + f * P:t * RDV + (f + 1) * P], ident)
                        last.then_inc(head_turned, 1)

                    def attention(u):
                        s = u - ATTENTION
                        if u == U_DQ + 2:
                            turn_q_rope()
                        if s < 0:
                            return
                        m = s // 2
                        if s % 2 == 0:
                            mix(m - 2)
                            turn_head(m - 3)
                        else:
                            scores(m)
                            turn_probs(m - 1)

                    def turn_merged(half):
                        pe.wait_ge(merged_made, 2 + half + 1)
                        if half == 0:
                            pe.wait_ge(head_lo, DH + RH)
                        for k in range(4):
                            for t in range(TT):
                                at = (k % 2) * S + t * P
                                last = nc.tensor.transpose(A[:, 2 * half + k // 2, at:at + P],
                                                           merged[:, t, 512 * half + k * P:512 * half + (k + 1) * P],
                                                           ident)
                        last.then_inc(merged_turned, 1)

                    def hidden_turn():
                        pe.wait_ge(square_made, 1)
                        for c in range(4):
                            for t in range(TT):
                                last = nc.tensor.transpose(A[:, c // 2, (c % 2) * S + t * P:(c % 2) * S + (t + 1) * P],
                                                           square_h[:, t * 512 + c * P:t * 512 + (c + 1) * P], ident)
                        last.then_inc(hid_turned, 1)

                    def down(j, u, i, tiles=range(TT)):
                        half, pair = i // 2, i % 2
                        return tokens_stationary(u, 2 * pair, (hid_hi[:, j % 2, :, :], hid_lo[:, j % 2, :, :]),
                                                 [A[:, 2 * t + half, :] for t in range(TT)], j == 0 and pair == 0,
                                                 j == 7 and pair == 1, tiles)

                    pe.wait_ge(consts_in, 16)
                    for t in range(TT):
                        for b in range(2):
                            norm_turn(PRE_MIX, t, b)
                    latents()
                    for u in range(U_LAT, U_WOUT):
                        if u == U_UK:
                            pe.wait_ge(lat_lo_made, 3)
                        if u == U_MLAO:
                            pe.wait_ge(pair_lo_made, MH // 2)
                        if u == U_DIFFO:
                            pe.wait_ge(head_lo, DH)
                        if u == U_RETO:
                            pe.wait_ge(head_lo, DH + RH)
                        if u >= U_RQ:
                            gemm(u)
                        before_mla(u)
                        attention(u)
                        if u == U_RETO + 5:
                            turn_merged(0)
                    mixers_out()
                    for t in range(TT):
                        for b in range(2):
                            norm_turn(PRE_MLP, t, b)
                        pair = take_pair(U_UP[0])
                        for i in range(4):
                            pe.wait_ge(h_lo_made, normed_by(PRE_MLP, t, i // 2))
                            last = tokens_stationary(U_UP[0] + i, 2 * i, acts_h, [pair[:, tt, :] for tt in range(TT)],
                                                     i == 0, i == 3, [t])
                            if t == 1:
                                last.then_inc(unit_used, 1)
                    for j in range(1, 8):
                        for i in range(4):
                            gemm(U_UP[j] + i)
                            if j == 1 and i == 1:
                                hidden_turn()
                        pe.wait_ge(hid_lo_made, j)
                        for i in range(4):
                            down(j - 1, U_DN[j - 1] + i, i).then_inc(unit_used, 1)
                    pe.wait_ge(hid_lo_made, 8)
                    for t in range(TT):
                        for i in range(4):
                            last = down(7, U_DN[7] + i, i, [t])
                            if t == 1:
                                last.then_inc(unit_used, 1)
                            elif i % 2:
                                last.then_inc(y_tile0, 1)

        with nc.Fori(0, L) as l:
            layer(l)
            nc.multi_engine_barrier([ENG.PE, ENG.Activation, ENG.DVE, ENG.Pool, ENG.SP],
                                    sems_to_clear=range(first_sem[0].num, last_sem.num + 1))

        out_stored = sem("out_stored")
        with nc.Block() as block:
            @block.sync
            def _(sp):
                sp.dma_start(io["out"][0].rearrange("(t p) d -> p t d", p=P), x[:, :, :]).then_inc(out_stored, 16)
                sp.wait_ge(out_stored, 16)


def shape_constants():
    f = np.float32
    packed, decays = np.zeros((P, K_END), f), np.zeros((P, RH, 384), f)
    p, k = np.arange(P)[:, None], np.arange(P)[None, :]
    packed[:, K_ID:K_ID + P] = np.eye(P, dtype=f)
    packed[:, K_MASK + P:K_MASK + S] = np.where(p >= k, 0.0, NEG)
    log_g = np.log1p(-np.exp2(-5.0 - np.arange(RH, dtype=np.float64)))
    for h in range(RH):
        rel = np.arange(S)[None, :] - p
        wide = np.where(rel >= 0, np.exp(np.maximum(rel, 0) * log_g[h]), 0.0) * RDK ** -0.5
        decays[:, h, :] = np.concatenate([wide, wide[:, 0:P]], axis=1)

    def rotations(at_cos, at_sin, inv_freq, width):
        pos = np.arange(S, dtype=f)
        angle = (pos[:, None] * inv_freq.astype(f)[None, :]).astype(np.float64)
        cos, sin = np.cos(angle), np.sin(angle)
        for t in range(TT):
            rows = slice(t * P, (t + 1) * P)
            packed[:, at_cos + t * width:at_cos + (t + 1) * width] = np.concatenate([cos[rows], cos[rows]], axis=1)
            packed[:, at_sin + t * width:at_sin + (t + 1) * width] = np.concatenate([-sin[rows], sin[rows]], axis=1)

    rotations(K_RC, K_RS, 1.0 / (10000.0 ** np.linspace(0.0, 1.0, RDK // 2)), RDK)
    rotations(K_MC, K_MS, 1.0 / (10000.0 ** (np.arange(0, MR, 2) / MR)), MR)


    dist = S - 1 - np.arange(LINE)
    exact = BUCKETS // 2
    far = exact + (np.log(np.maximum(dist, 1).astype(f) / f(exact)) / f(np.log(MAX_DIST / exact))
                   * f(BUCKETS - exact)).astype(np.int32)
    bucket = np.where(dist < exact, np.maximum(dist, 0), np.minimum(far, BUCKETS - 1))
    onehot = np.zeros((BUCKETS + 1, LINE), f)
    onehot[bucket, np.arange(LINE)] = dist >= 0
    onehot[BUCKETS] = dist < 0
    return {"consts": packed, "onehot": onehot, "decay": decays}


def lay_out(inputs):
    vec = {name: np.asarray(inputs[name]) for name in _SMALL}
    init = [[lambda_init(l), 1.0 - lambda_init(l)] for l in range(L)]
    cols = [vec[name].reshape(L, -1, P) for name in ("mla_q_norm_g", "mla_kv_norm_g", "diff_subln_g")]
    cols.append(np.zeros((L, 1, P), np.float32))
    cols.append(np.broadcast_to(np.array(init, np.float32)[:, :, None], (L, 2, P)))
    gains = np.ascontiguousarray(np.concatenate(cols, axis=1).transpose(2, 0, 1))
    lambdas = np.ascontiguousarray(np.stack([vec[f"lambda_{n}"] for n in ("q1", "k1", "q2", "k2")], axis=1
                                            ).reshape(4 * L, DD).T)
    next_pre_mix = np.concatenate([vec["pre_mix_g"][1:], vec["pre_mix_g"][:1]])
    gain_rows = np.ascontiguousarray(np.stack([vec["post_mix_g"], vec["post_mlp_g"], vec["pre_mlp_g"], next_pre_mix],
                                              axis=1).reshape(L, 4 * DM))
    return {"gains": gains, "lambdas": lambdas, "gain_rows": gain_rows}


def heads_apart(inputs):
    ukv = np.asarray(inputs["w_mla_ukv"]).reshape(L, KVL, MH, 2, MN).transpose(0, 1, 3, 2, 4).reshape(L, KVL, -1)
    uq = np.asarray(inputs["w_mla_uq"]).reshape(L, QL, MH, MQ)
    uq = np.concatenate([uq[..., :MN].reshape(L, QL, -1), uq[..., MN:].reshape(L, QL, -1)], axis=2)
    return {"w_mla_ukv": np.ascontiguousarray(ukv), "w_mla_uq": uq}


_INS = ["x", "rel_bias", "w_in", "w_ret_o", "w_diff_o", "w_mla_o", "w_out", "w_up", "w_down"]
_SMALL = ["pre_mix_g", "post_mix_g", "pre_mlp_g", "post_mlp_g", "mla_q_norm_g", "mla_kv_norm_g", "diff_subln_g",
          "lambda_q1", "lambda_k1", "lambda_q2", "lambda_k2"]


def kernel(**inputs):
    import concourse.bacc as bacc
    from concourse.bass_utils import run_bass_kernel_spmd

    nc = bacc.Bacc("TRN2", target_bir_lowering=False, num_devices=1)


    arrays, io = {}, {}
    for name, a in [(n, np.ascontiguousarray(inputs[n])) for n in _INS] + list(shape_constants().items()) + list(
            lay_out(inputs).items()) + list(heads_apart(inputs).items()):
        arrays[f"in_{name}"] = a
        io[name] = nc.dram_tensor(f"in_{name}", a.shape, mybir.dt.from_np(a.dtype), kind="ExternalInput").ap()
    io["line"] = nc.dram_tensor("line", (COPIES, DH, LINE), F32, kind="Internal").ap()
    io["out"] = nc.dram_tensor("out", (1, S, DM), F32, kind="ExternalOutput").ap()
    build(nc, io)
    r = run_bass_kernel_spmd(nc, [arrays], core_ids=[0])
    return r.results[0]["out"]
```
